# Optimizing a Trainium2 kernel written in Bass

```python
import jax
import jax.numpy as jnp
from jax import lax
import numpy as np

D_MODEL = 1024
BATCH = 1
SEQ = 1024
DEPTH = 2

GRID_W = 64
CTX_LEN = 256
N_MIXERS = 2
N_ATTN_LAYERS = (DEPTH + N_MIXERS - 1) // N_MIXERS
N_RWKV_LAYERS = DEPTH // N_MIXERS
N_MOD = 6
NORM_EPS = 1e-6

N_HEADS = 16
N_KV_HEADS = 4
HEAD_DIM = D_MODEL // N_HEADS
Q_DIM = N_HEADS * HEAD_DIM
KV_DIM = N_KV_HEADS * HEAD_DIM
ROPE_THETA = 10000.0
Q_BLOCK = 128

RWKV_HEAD = 64
RWKV_HEADS = D_MODEL // RWKV_HEAD
DECAY_LORA = 64
AAA_LORA = 64
GATE_LORA = 160
GN_EPS = 64e-5
N_DIRS = 2

D_FF = 2816
CONV_W = 3

kernel_name = 'hybrid_attn_rwkv7_convffn_dit'

def rms_norm(x):
    xf = x.astype(jnp.float32)
    return (xf * lax.rsqrt(jnp.mean(xf * xf, axis=-1, keepdims=True) + NORM_EPS)).astype(x.dtype)

def modulate(x, shift, scale):
    return rms_norm(x) * (1.0 + scale) + shift

def centred_shift(x):
    xp = jnp.pad(x, ((0, 0), (1, 1), (0, 0)))
    return 0.5 * (xp[:, :-2] + xp[:, 2:])

def centred_dwconv(x, w, b):
    t = x.shape[1]
    p = CONV_W // 2
    xp = jnp.pad(x, ((0, 0), (p, p), (0, 0)))
    return sum(w[j] * xp[:, j:j + t] for j in range(CONV_W)) + b

def axial_rope_tables(n_tokens):
    rows = n_tokens // GRID_W
    row = jnp.repeat(jnp.arange(rows, dtype=jnp.float32), GRID_W)
    col = jnp.tile(jnp.arange(GRID_W, dtype=jnp.float32), rows)
    n_freq = HEAD_DIM // 4
    inv_freq = ROPE_THETA ** (-jnp.arange(n_freq, dtype=jnp.float32) / n_freq)
    ang = jnp.concatenate([row[:, None] * inv_freq, col[:, None] * inv_freq], axis=-1)
    return jnp.cos(ang), jnp.sin(ang)

def apply_rope(x, cos, sin):
    xp = x.reshape(*x.shape[:-1], HEAD_DIM // 2, 2)
    x0, x1 = xp[..., 0], xp[..., 1]
    c = cos[None, :, None, :].astype(x.dtype)
    s = sin[None, :, None, :].astype(x.dtype)
    return jnp.stack([x0 * c - x1 * s, x0 * s + x1 * c], axis=-1).reshape(x.shape)

def gqa_attend(q, k, v):
    s = jnp.einsum('bqhgd,bkhd->bhgqk', q, k).astype(jnp.float32) * (HEAD_DIM ** -0.5)
    p = jax.nn.softmax(s, axis=-1).astype(v.dtype)
    return jnp.einsum('bhgqk,bkhd->bqhgd', p, v)

def attention_mixer(h_lat, h_ctx, w_qkv, q_gain, k_gain, w_o, cos, sin, need_ctx_out):
    n_group = N_HEADS // N_KV_HEADS

    def project(h):
        b, t, _ = h.shape
        q, k, v = jnp.split(h @ w_qkv, [Q_DIM, Q_DIM + KV_DIM], axis=-1)
        q = rms_norm(q.reshape(b, t, N_HEADS, HEAD_DIM)) * q_gain
        k = rms_norm(k.reshape(b, t, N_KV_HEADS, HEAD_DIM)) * k_gain
        return q, k, v.reshape(b, t, N_KV_HEADS, HEAD_DIM)

    q_l, k_l, v_l = project(h_lat)
    q_c, k_c, v_c = project(h_ctx)
    q_l = apply_rope(q_l, cos, sin)
    k_l = apply_rope(k_l, cos, sin)
    k_all = jnp.concatenate([k_c, k_l], axis=1)
    v_all = jnp.concatenate([v_c, v_l], axis=1)

    b, s, _ = h_lat.shape
    n_blk = s // Q_BLOCK
    q_blk = jnp.moveaxis(q_l.reshape(b, n_blk, Q_BLOCK, N_KV_HEADS, n_group, HEAD_DIM), 1, 0)
    o_l = lax.map(lambda qb: gqa_attend(qb, k_all, v_all), q_blk)
    o_l = jnp.moveaxis(o_l, 0, 1).reshape(b, s, Q_DIM) @ w_o

    o_c = None
    if need_ctx_out:
        c_len = h_ctx.shape[1]
        o_c = gqa_attend(q_c.reshape(b, c_len, N_KV_HEADS, n_group, HEAD_DIM), k_c, v_c)
        o_c = o_c.reshape(b, c_len, Q_DIM) @ w_o
    return o_l, o_c

def rwkv_heads(t):
    return t.reshape(t.shape[0], t.shape[1], RWKV_HEADS, RWKV_HEAD)

def l2_normalize(x):
    xf = x.astype(jnp.float32)
    return (xf / jnp.maximum(jnp.sqrt(jnp.sum(xf * xf, axis=-1, keepdims=True)), 1e-12)).astype(x.dtype)

def wkv7_scan(state0, decay, k, v, a, b, r, reverse):
    emit = r is not None
    seq = (decay, k, v, a, b) + ((r,) if emit else ())
    xs = tuple(jnp.moveaxis(t, 1, 0) for t in seq)

    def step(S, inp):
        d_t, k_t, v_t, a_t, b_t = inp[:5]
        sa = jnp.einsum('bhvk,bhk->bhv', S, a_t)
        S = S * d_t[:, :, None, :] + sa[..., None] * b_t[:, :, None, :] + v_t[..., None] * k_t[:, :, None, :]
        y = jnp.einsum('bhvk,bhk->bhv', S, inp[5]) if emit else None
        return S, y

    S, ys = lax.scan(step, state0, xs, reverse=reverse)
    return S, (jnp.moveaxis(ys, 0, 1) if emit else None)

def rwkv7_mixer(h_lat, h_ctx, mu, w_r, w_k, w_v, w_o, decay_w0, decay_w1, decay_w2,
                aaa_a0, aaa_a1, aaa_a2, gate_g1, gate_g2, k_k, k_a, r_k, gn_w, gn_b, need_ctx_out):
    def scan_inputs(h):
        xx = centred_shift(h) - h
        xw, xk, xv, xa = (h + xx * mu[i] for i in (1, 2, 3, 4))
        k = xk @ w_k
        v = rwkv_heads(xv @ w_v)
        kk = l2_normalize(rwkv_heads(k * k_k))
        dirs = []
        for d in range(N_DIRS):
            w_log = -jax.nn.softplus(-(decay_w0[d] + jnp.tanh(xw @ decay_w1[d]) @ decay_w2[d])) - 0.5
            a = jax.nn.sigmoid(aaa_a0[d] + (xa @ aaa_a1[d]) @ aaa_a2[d])
            decay = rwkv_heads(jnp.exp(-jnp.exp(w_log)))
            k_d = rwkv_heads(k * (1.0 + (a - 1.0) * k_a))
            dirs.append((decay, k_d, -kk, kk * rwkv_heads(a)))
        return xx, v, dirs

    def receptance(h, xx):
        return rwkv_heads((h + xx * mu[0]) @ w_r)

    def readout(h, xx, r, v, dirs, y):
        b, t, _ = h.shape
        mean = jnp.mean(y, axis=-1, keepdims=True)
        var = jnp.mean(jnp.square(y - mean), axis=-1, keepdims=True)
        y_n = ((y - mean) * lax.rsqrt(var + GN_EPS)).reshape(b, t, D_MODEL).astype(h.dtype) * gn_w + gn_b
        bonus = sum(jnp.sum(r * k_d * r_k, axis=-1, keepdims=True) for (_, k_d, _, _) in dirs) * v
        g = jax.nn.sigmoid((h + xx * mu[5]) @ gate_g1) @ gate_g2
        return ((y_n + bonus.reshape(b, t, D_MODEL)) * g) @ w_o

    b = h_lat.shape[0]
    xx_c, v_c, dirs_c = scan_inputs(h_ctx)
    xx_l, v_l, dirs_l = scan_inputs(h_lat)
    r_c = receptance(h_ctx, xx_c) if need_ctx_out else None
    r_l = receptance(h_lat, xx_l)
    state0 = jnp.zeros((b, RWKV_HEADS, RWKV_HEAD, RWKV_HEAD), jnp.float32)
    ys_l, ys_c = [], []
    for d in range(N_DIRS):
        reverse = d == 1
        dec_c, kd_c, a_c, b_c = dirs_c[d]
        s_ctx, y_c = wkv7_scan(state0, dec_c, kd_c, v_c, a_c, b_c, r_c, reverse)
        dec_l, kd_l, a_l, b_l = dirs_l[d]
        _, y_l = wkv7_scan(s_ctx, dec_l, kd_l, v_l, a_l, b_l, r_l, reverse)
        ys_l.append(y_l)
        ys_c.append(y_c)
    o_l = readout(h_lat, xx_l, r_l, v_l, dirs_l, sum(ys_l))
    o_c = readout(h_ctx, xx_c, r_c, v_c, dirs_c, sum(ys_c)) if need_ctx_out else None
    return o_l, o_c

def conv_ffn(h, w_up, conv_w, conv_b, w_down):
    u = centred_dwconv(h @ w_up, conv_w, conv_b)
    gate, val = jnp.split(u, 2, axis=-1)
    return (jax.nn.silu(gate) * val) @ w_down

def setup_inputs(seed: int = 0) -> dict:
    key = jax.random.key(seed)
    ks = iter(jax.random.split(key, 40))
    D = D_MODEL

    def nrm(shape, scale):
        return jax.random.normal(next(ks), shape, jnp.float32) * scale

    def gain(shape):
        return 1.0 + nrm(shape, 0.05)

    return {
        'x': nrm((BATCH, SEQ, D), 1.0),
        'c': nrm((BATCH, D), 1.0),
        'ctx': nrm((BATCH, CTX_LEN, D), 1.0),
        'c_ctx': nrm((D,), 1.0),
        'ada_w': nrm((DEPTH, D, N_MOD * D), 0.5 * D ** -0.5),
        'ada_b': nrm((DEPTH, N_MOD * D), 0.02),
        'attn_w_qkv': nrm((N_ATTN_LAYERS, D, Q_DIM + 2 * KV_DIM), D ** -0.5),
        'attn_q_gain': gain((N_ATTN_LAYERS, HEAD_DIM)),
        'attn_k_gain': gain((N_ATTN_LAYERS, HEAD_DIM)),
        'attn_w_o': nrm((N_ATTN_LAYERS, Q_DIM, D), Q_DIM ** -0.5),
        'rwkv_mu': jax.random.uniform(next(ks), (N_RWKV_LAYERS, 6, D), jnp.float32),
        'rwkv_w_r': nrm((N_RWKV_LAYERS, D, D), D ** -0.5),
        'rwkv_w_k': nrm((N_RWKV_LAYERS, D, D), D ** -0.5),
        'rwkv_w_v': nrm((N_RWKV_LAYERS, D, D), D ** -0.5),
        'rwkv_w_o': nrm((N_RWKV_LAYERS, D, D), D ** -0.5),
        'rwkv_decay_w0': jax.random.uniform(next(ks), (N_RWKV_LAYERS, N_DIRS, D), jnp.float32, minval=-7.0, maxval=-2.0),
        'rwkv_decay_w1': nrm((N_RWKV_LAYERS, N_DIRS, D, DECAY_LORA), D ** -0.5),
        'rwkv_decay_w2': nrm((N_RWKV_LAYERS, N_DIRS, DECAY_LORA, D), 0.1 * DECAY_LORA ** -0.5),
        'rwkv_aaa_a0': nrm((N_RWKV_LAYERS, N_DIRS, D), 0.1),
        'rwkv_aaa_a1': nrm((N_RWKV_LAYERS, N_DIRS, D, AAA_LORA), D ** -0.5),
        'rwkv_aaa_a2': nrm((N_RWKV_LAYERS, N_DIRS, AAA_LORA, D), 0.1 * AAA_LORA ** -0.5),
        'rwkv_gate_g1': nrm((N_RWKV_LAYERS, D, GATE_LORA), D ** -0.5),
        'rwkv_gate_g2': nrm((N_RWKV_LAYERS, GATE_LORA, D), GATE_LORA ** -0.5),
        'rwkv_k_k': 0.85 + nrm((N_RWKV_LAYERS, D), 0.05),
        'rwkv_k_a': gain((N_RWKV_LAYERS, D)),
        'rwkv_r_k': nrm((N_RWKV_LAYERS, RWKV_HEADS, RWKV_HEAD), 0.1),
        'rwkv_gn_w': gain((N_RWKV_LAYERS, D)),
        'rwkv_gn_b': nrm((N_RWKV_LAYERS, D), 0.02),
        'ffn_w_up': nrm((DEPTH, D, 2 * D_FF), D ** -0.5),
        'ffn_conv_w': nrm((DEPTH, CONV_W, 2 * D_FF), CONV_W ** -0.5),
        'ffn_conv_b': nrm((DEPTH, 2 * D_FF), 0.02),
        'ffn_w_down': nrm((DEPTH, D_FF, D), D_FF ** -0.5),
        'final_gain': gain((D,)),
    }

def reference(x, c, ctx, c_ctx, ada_w, ada_b, attn_w_qkv, attn_q_gain, attn_k_gain, attn_w_o,
              rwkv_mu, rwkv_w_r, rwkv_w_k, rwkv_w_v, rwkv_w_o, rwkv_decay_w0, rwkv_decay_w1, rwkv_decay_w2,
              rwkv_aaa_a0, rwkv_aaa_a1, rwkv_aaa_a2, rwkv_gate_g1, rwkv_gate_g2, rwkv_k_k, rwkv_k_a, rwkv_r_k,
              rwkv_gn_w, rwkv_gn_b, ffn_w_up, ffn_conv_w, ffn_conv_b, ffn_w_down, final_gain):
    cos, sin = axial_rope_tables(x.shape[1])
    x_lat, x_ctx = x, ctx
    for i in range(DEPTH):
        ctx_out = i < DEPTH - 1
        j = i // N_MIXERS
        mod_l = (jax.nn.silu(c) @ ada_w[i] + ada_b[i])[:, None, :]
        mod_c = (jax.nn.silu(c_ctx) @ ada_w[i] + ada_b[i])[None, None, :]
        sh1_l, sc1_l, g1_l, sh2_l, sc2_l, g2_l = jnp.split(mod_l, N_MOD, axis=-1)
        sh1_c, sc1_c, g1_c, sh2_c, sc2_c, g2_c = jnp.split(mod_c, N_MOD, axis=-1)
        h_l = modulate(x_lat, sh1_l, sc1_l)
        h_c = modulate(x_ctx, sh1_c, sc1_c)
        if i % N_MIXERS == 0:
            y_l, y_c = attention_mixer(h_l, h_c, attn_w_qkv[j], attn_q_gain[j], attn_k_gain[j], attn_w_o[j],
                                       cos, sin, ctx_out)
        else:
            y_l, y_c = rwkv7_mixer(h_l, h_c, rwkv_mu[j], rwkv_w_r[j], rwkv_w_k[j], rwkv_w_v[j], rwkv_w_o[j],
                                   rwkv_decay_w0[j], rwkv_decay_w1[j], rwkv_decay_w2[j],
                                   rwkv_aaa_a0[j], rwkv_aaa_a1[j], rwkv_aaa_a2[j],
                                   rwkv_gate_g1[j], rwkv_gate_g2[j], rwkv_k_k[j], rwkv_k_a[j], rwkv_r_k[j],
                                   rwkv_gn_w[j], rwkv_gn_b[j], ctx_out)
        x_lat = x_lat + g1_l * y_l
        x_lat = x_lat + g2_l * conv_ffn(modulate(x_lat, sh2_l, sc2_l),
                                        ffn_w_up[i], ffn_conv_w[i], ffn_conv_b[i], ffn_w_down[i])
        if ctx_out:
            x_ctx = x_ctx + g1_c * y_c
            x_ctx = x_ctx + g2_c * conv_ffn(modulate(x_ctx, sh2_c, sc2_c),
                                            ffn_w_up[i], ffn_conv_w[i], ffn_conv_b[i], ffn_w_down[i])
    return rms_norm(x_lat) * final_gain


_drawn_inputs = setup_inputs


def setup_inputs(seed=0):
    import zlib

    import numpy as np

    out = dict(_drawn_inputs(seed))
    spreads = {}
    factors = {'attn_q_gain': 8.0,
     'attn_k_gain': 8.0,
     'rwkv_decay_w1': 8.0,
     'rwkv_decay_w2': 8.0,
     'rwkv_aaa_a0': 8.0,
     'rwkv_aaa_a1': 8.0,
     'rwkv_aaa_a2': 8.0,
     'rwkv_gn_w': 7.161,
     'rwkv_gn_b': 31.785,
     'ffn_conv_b': 6.805}
    for name, (base, spread) in spreads.items():
        noise = np.random.default_rng([zlib.crc32(name.encode()), seed]).standard_normal(out[name].shape)
        drawn = base * np.exp(spread * noise) if base else spread * noise
        out[name] = jnp.asarray(drawn.astype(out[name].dtype))
    for name, factor in factors.items():
        out[name] = (out[name] * factor).astype(out[name].dtype)
    return out
```

```python
from contextlib import ExitStack

import concourse.bass as bass
from concourse import mybir
import numpy as np

F32 = mybir.dt.float32
ALU = mybir.AluOpType
ACT = mybir.ActivationFunctionType
AX_X = mybir.AxisListType.X
ds = bass.ds

P = 128
D = 1024
KD = D // P
TC, TL = 256, 1024
T = TC + TL
H, HKV, DH = 16, 4, 64
FF = 2816
FJ = FF // P
FH = FJ // 2
CH = 64
NU = 8
GT = 4 * CH
NGR = T // GT
NPAIR = H // 2
LEVELS = [2, 4, 8, 16, 32]
EPS, GN_EPS = 1e-6, 64e-5
DECAY = float(np.exp(-0.5))
NLEV = 10

SLICES = [(0, TC, 1), (TC, 512, 0), (TC + 512, 512, 0)]
LAT = SLICES[1:]
PADW = T + 4


def padded(t0):
    return t0 + 1 if t0 < TC else t0 + 2


VEC = {}
_at = 0
for _name, _n in (("ada_b", 96), ("qk_gain", 10), ("mu", 48), ("w0", 16), ("a0", 16), ("k_k", 8), ("k_a", 8),
                  ("r_k", 8), ("gn_w", 8), ("gn_b", 8), ("final_gain", 8), ("conv", 2 * FJ * 2 * 4)):
    VEC[_name] = _at
    _at += _n
NVEC = _at
CST = {"mean1024": 0, "mean64": 128, "sum64": 256, "swap": 384, "ident": 512, "masks": 640}
NCST = 640 + NLEV * 2 * CH


class Dense:

    def __init__(self, n, k, slices, before):
        self.n, self.k, self.slices, self.j = n, k, slices, len(slices)
        self.slots = min(n, 2)
        self.loops = n // self.slots
        self.w0 = [0, 0] if before is None else list(before.w1)
        self.p0 = [0, 0] if before is None else list(before.p1)
        self.w1 = [w + (self.loops if s < self.slots else 0) for s, w in enumerate(self.w0)]
        self.p1 = [p + (self.loops * self.j if s < self.slots else 0) for s, p in enumerate(self.p0)]


def program(nc, stop, a_xT, a_cT, a_vec, a_cst, a_rope, a_adaw, a_wqk, a_wv, a_wo, a_wup, a_wdn,
            a_lora1, a_g1, a_rk, a_rv, a_rr, a_ro, a_lora2, a_g2, out):
    order = {}
    last = None

    def dense(name, n, k, slices):
        nonlocal last
        last = order[name] = Dense(n, k, slices, last)

    dense("qk", 10, 8, SLICES)
    dense("wo", 8, 8, SLICES)
    for half in range(2):
        dense(f"up0{half}", 2 * FH, 8, SLICES)
        dense(f"dn0{half}", 8, FH, SLICES)
    dense("lw", 1, 8, SLICES)
    dense("la", 1, 8, SLICES)
    dense("g", 2, 8, LAT)
    dense("v", 8, 8, SLICES)
    dense("r", 8, 8, LAT)
    dense("k", 8, 8, SLICES)
    dense("ro", 8, 8, LAT)
    for half in range(2):
        dense(f"up1{half}", 2 * FH, 8, LAT)
        dense(f"dn1{half}", 8, FH, LAT)
    src = {"qk": a_wqk, "wo": a_wo, "lw": a_lora1[0:1], "la": a_lora1[1:2], "k": a_rk, "v": a_rv, "r": a_rr,
           "g": a_g1, "ro": a_ro}
    for lay in range(2):
        for half in range(2):
            src[f"up{lay}{half}"] = a_wup[lay, half]
            src[f"dn{lay}{half}"] = a_wdn[lay, half]

    k_dram = nc.dram_tensor("k_scratch", (KD, P, T), F32, kind="Internal").ap()
    n_dram = nc.dram_tensor("kk_scratch", (KD, P, T), F32, kind="Internal").ap()
    v_dram = nc.dram_tensor("v_scratch", (KD, P, T), F32, kind="Internal").ap()
    r_dram = nc.dram_tensor("r_scratch", (KD, P, T), F32, kind="Internal").ap()

    with ExitStack() as ctx:
        SB = ctx.enter_context(nc.sbuf_tensor("SB", [P, 52900], F32))
        PS = ctx.enter_context(nc.psum_tensor("PS", [P, 4096], F32))
        top = [0]

        def take(n):
            top[0] += n
            assert top[0] <= 52900, top[0]
            return SB[:, top[0] - n:top[0]]

        def sem(name):
            return ctx.enter_context(nc.semaphore(name))

        def bank(b, n=1):
            return PS[:, b * 512:(b + n) * 512]

        XL = take(KD * TL)
        MOD = take(192)
        SCL = take(64)
        VECS = take(NVEC)
        CSTS = take(NCST)
        SILU = take(16)
        DER = take(48)
        WS = [take(FH * P) for _ in range(2)]
        KA = take(2)
        NEG = take(16)
        XC = take(KD * TC)
        base = top[0]

        def xs(f, sl):
            t0, w, stream = sl
            if stream:
                return XC[:, ds(f * TC, w)]
            return XL[:, ds(f * TL + (t0 - TC), w)]

        def cst(name, rows=P, n=P):
            return CSTS[0:rows, CST[name]:CST[name] + n]

        def mask(lev):
            o = CST["masks"] + lev * 2 * CH
            return CSTS[:, o:o + 2 * CH]

        def vec(name, i=0, n=1):
            return VECS[:, ds(VEC[name] + i, n)]

        def mod(layer, comp, f, stream):
            return MOD[:, ds(((layer * 6 + comp) * 8 + f) * 2 + stream, 1)]

        def scl(layer, norm, f, stream):
            return SCL[:, ds(((layer * 2 + norm) * 8 + f) * 2 + stream, 1)]

        s_const = sem("const_loaded")
        s_adaw = [sem(f"ada_w_loaded{i}") for i in range(2)]
        s_adap = sem("ada_product")
        s_silu = sem("silu_c")
        s_bar = sem("stage_over")
        s_passed = sem("wait_passed")
        s_w = [sem(f"weights_loaded{i}") for i in range(2)]
        s_ps = [sem(f"tile_summed{i}") for i in range(2)]
        s_read = {name: [sem(f"tile_read_{name}_{i}") for i in range(2)] for name in order}
        s_sq = sem("squares_ready")
        s_ms = sem("mean_square_ready")
        s_root = sem("root_ready")
        s_scaled = sem("scaled_ready")
        s_hsq = sem("head_squares_ready")
        s_hms = sem("head_sums_ready")
        s_hroot = sem("head_roots_ready")
        s_rd = sem("rms_done_reading")
        s_load = sem("stage_input_loaded")
        s_v = sem("v_tile_summed")
        s_vr = sem("v_tile_read")
        s_qn = sem("qk_normed")
        s_rot = sem("qk_swapped")
        s_cosd = sem("cos_part_ready")
        s_qkd = sem("qk_roped")
        s_qs = sem("q_block_copied")
        s_qsr = sem("q_block_used")
        s_sc = sem("scores_ready")
        s_mx = sem("max_ready")
        s_pr = sem("probs_ready")
        s_pt = sem("probs_turned")
        s_pta = sem("probs_even_copied")
        s_ptd = sem("probs_odd_copied")
        s_pv = sem("values_summed")
        s_os = sem("head_out_scaled")
        s_ot = sem("head_out_turned")
        s_otc = sem("head_out_copied")
        s_cv = [sem(f"conv_done{i}") for i in range(2)]
        s_sg = sem("gate_silu_ready")
        s_gd = sem("gated_ready")
        s_mix = sem("mix_ready")
        s_sp = sem("spill_ready")
        s_kst = sem("k_stored")
        s_spd = [sem(f"spill_stored{i}") for i in range(2)]
        s_kin = sem("group_inputs_loaded")
        s_rin = sem("group_r_loaded")
        s_lz = sem("lora_summed")
        s_th = sem("tanh_ready")
        s_cum = sem("decay_sums_ready")
        s_xp = sem("decay_powers_ready")
        s_kd = sem("k_and_b_ready")
        s_hat = sem("hats_ready")
        s_bd = sem("hats_spread")
        s_bdr = sem("r_hat_spread")
        s_vt = sem("v_turned")
        s_vc = sem("v_stacked")
        s_s1 = sem("products_ready")
        s_m1 = sem("products_masked")
        s_tr = sem("hat_turned")
        s_trc = sem("hat_turned_copied")
        s_gt = sem("inverse_turned")
        s_gtc = sem("inverse_turned_spread")
        s_z = sem("join_inner_ready")
        s_zc = sem("join_inner_masked")
        s_gz = sem("join_outer_ready")
        s_g = sem("inverse_grown")
        s_gb = sem("inverse_spread")
        s_W = sem("w_summed")
        s_Wc = sem("w_copied")
        s_U = sem("u_summed")
        s_Uc = sem("u_copied")
        s_D = sem("state_delta_ready")
        s_St = sem("state_updated")
        s_y = sem("y_ready")
        s_yc = sem("y_added")
        s_out = sem("out_stored")
        s_r3 = sem("readout_loaded")
        s_r3c = sem("readout_copied")
        s_r3p = sem("readout_product")
        s_r3a = sem("readout_act")
        s_r3v = sem("readout_vector")
        s_r3r = sem("readout_inputs_used")
        block = ctx.enter_context(nc.Block())

        STAGES = ["start", "ada", "norm_a0", "qk", "heads", "attention", "wo", "norm_f0", "ffn0", "norm_a1", "shift",
                  "mix1", "lw", "mix4", "la", "mix5", "g", "mix3", "v", "mix0", "r", "mix2", "k", "kk", "scan_init",
                  "scan", "read", "ro", "norm_f1", "ffn1", "norm_end"]

        def over(name):
            return 4 * (STAGES.index(name) + 1)

        def stage_over(eng, name):
            eng.drain().then_inc(s_bar, 1)
            eng.wait_ge(s_bar, over(name))

        def apart(eng):
            eng.sem_inc(s_passed, 1)

        def dense_loads(sp, name, store=None):
            d = order[name]
            w = src[name]

            def load(i, s):
                sp.dma_start(WS[s][:, 0:d.k * P], w[d.slots * i + s] if isinstance(i, int) else
                             w[ds(d.slots * i + s, 1)].rearrange("o p q -> (o p) q")).then_inc(s_w[s], 16)

            for s in range(d.slots):
                if d.w0[s] > 0:
                    sp.wait_ge(s_ps[s], d.p0[s])
                load(0, s)
            if d.loops > 1:
                with sp.Fori(1, d.loops) as i:
                    for s in range(d.slots):
                        sp.wait_ge(s_ps[s], i * d.j + d.p0[s])
                        load(i, s)
                        if store:
                            store(i - 1, s)
                for s in range(d.slots if store else 0):
                    store(d.loops - 1, s)

        def dense_products(pe, name, rhs):
            d = order[name]

            def body(i):
                for s in range(d.slots):
                    pe.wait_ge(s_w[s], (i + d.w0[s] + 1) * 16)
                    for j, sl in enumerate(d.slices):
                        pe.wait_ge(s_read[name][s], i * d.j + (j + 1))
                        o = PS[:, (3 * s + j) * 512:(3 * s + j) * 512 + sl[1]]
                        for k in range(d.k):
                            mm = pe.matmul(o, WS[s][:, k * P:(k + 1) * P], rhs(k, sl), start=k == 0, stop=k == d.k - 1)
                        mm.then_inc(s_ps[s], 1)

            if d.loops > 1:
                with pe.Fori(0, d.loops) as i:
                    body(i)
            else:
                body(0)

        def dense_evac(eng, name, read, before=None, after=None, only=(0, 1)):
            d = order[name]
            for s in [x for x in only if x < d.slots]:
                eng.sem_inc(s_read[name][s], d.j)

            def body(i):
                for s in [x for x in only if x < d.slots]:
                    if before:
                        before(i, s)
                    for j, sl in enumerate(d.slices):
                        eng.wait_ge(s_ps[s], i * d.j + (d.p0[s] + j + 1))
                        o = PS[:, (3 * s + j) * 512:(3 * s + j) * 512 + sl[1]]
                        read(i * d.slots + s, s, j, sl, o).then_inc(s_read[name][s], 1)
                    if after:
                        after(i, s)

            if d.loops > 1:
                with eng.Fori(0, d.loops) as i:
                    body(i)
            else:
                body(0)

        norms = {}
        nn = 0
        for key, sls in (("a0", SLICES), ("f0", SLICES), ("a1", SLICES), ("f1", LAT), ("end", LAT)):
            norms[key] = (nn, sls)
            nn += len(sls)

        def norm_act(act, key, layer, which, hs):
            n0, sls = norms[key]
            sq, rr = norm_tmp[key]
            for q, sl in enumerate(sls):
                n = n0 + q
                for f in range(KD):
                    m = n * KD + f
                    if m >= 2:
                        act.wait_ge(s_rd, m - 1)
                    act.activation(sq[f % 2][:, 0:sl[1]], xs(f, sl), ACT.Square).then_inc(s_sq, 1)
                act.wait_ge(s_ms, n + 1)
                if q:
                    act.wait_ge(s_scaled, (n - 1) * KD + KD)
                act.activation(rr[:, 0:sl[1]], PS[:, 6 * 512:6 * 512 + sl[1]], ACT.Sqrt, bias=NEG[:, 1:2]
                               ).then_inc(s_root, 1)
                if hs is not None:
                    for f in range(KD):
                        act.wait_ge(s_scaled, n * KD + f + 1)
                        act.activation(hs(f, sl), hs(f, sl), ACT.Identity, bias=mod(layer, 3 * which, f, sl[2]),
                                       scale=scl(layer, which, f, sl[2]))

        def norm_pe(pe, key):
            n0, sls = norms[key]
            sq, _ = norm_tmp[key]
            for q, sl in enumerate(sls):
                n = n0 + q
                if q:
                    pe.wait_ge(s_root, n)
                for f in range(KD):
                    pe.wait_ge(s_sq, n * KD + f + 1)
                    mm = pe.matmul(PS[:, 6 * 512:6 * 512 + sl[1]], cst("mean1024"), sq[f % 2][:, 0:sl[1]],
                                   start=f == 0, stop=f == KD - 1)
                    mm.then_inc(s_rd, 1)
                pe.drain().then_inc(s_ms, 1)

        def norm_dve(dve, key, hs):
            n0, sls = norms[key]
            _, rr = norm_tmp[key]
            for q, sl in enumerate(sls):
                n = n0 + q
                dve.wait_ge(s_root, n + 1)
                r = rr[:, 0:sl[1]]
                dve.reciprocal(r, r)
                dve.drain()
                for f in range(KD):
                    if hs is None:
                        dve.scalar_tensor_tensor(xs(f, sl), xs(f, sl), vec("final_gain", f), r, ALU.mult, ALU.mult
                                                 ).then_inc(s_scaled, 1)
                    else:
                        dve.tensor_tensor(hs(f, sl), xs(f, sl), r, ALU.mult).then_inc(s_scaled, 1)

        top[0] = base
        AH = take(KD * T)
        QK = take(10 * T)
        VT = take(10 * HKV * DH)
        KDUP = take(HKV * T)
        ROPE = take(2 * T)
        at_tmp = top[0]
        WV = take(KD * HKV * DH)
        sq_at = top[0]
        top[0] = at_tmp
        SQQ = take(T)
        T1 = take(T)
        top[0] = base + KD * T + 10 * T + 10 * HKV * DH + HKV * T
        PB = [take(T) for _ in range(2)]
        PTB = take(T)
        QS = [[take(P) for _ in range(2)] for _ in range(2)]
        OS = [take(P) for _ in range(2)]
        MXN = take(4)
        RSUM = take(4)
        RINV = take(4)
        att_top = top[0]
        SQ_att = [None, None]
        SQa = [KDUP[:, 0:512], KDUP[:, 512:1024]]
        RRa = KDUP[:, 1024:1536]
        top[0] = base
        FHB = take(KD * T)
        G = take(FH * T)
        UB = [take(PADW) for _ in range(2)]
        CB = [take(PADW) for _ in range(2)]
        SQf = [take(512) for _ in range(2)]
        RRf = take(512)
        HW = SB[:, base - KD * TC:base - KD * TC + T]
        top[0] = base
        HP = take(KD * PADW)
        XX = take(KD * PADW)
        MX1 = take(KD * PADW)
        HA = take(T)
        HG = take(2 * TL)
        STG = [take(T) for _ in range(2)]
        SQr = [STG[0][:, 0:512], STG[0][:, 512:1024]]
        RRr = STG[1][:, 0:512]
        KF = HP[:, 0:KD * T]
        NF = XX[:, 0:KD * T]
        top[0] = base
        YS = take(KD * TL)
        KIN = take(4 * 2 * GT)
        W2 = take(4 * P)
        TZ = take(2 * GT)
        TA = take(2 * GT)
        F1 = take(GT)
        IN = take(2 * GT)
        EX = take(2 * GT)
        XN = take(2 * GT)
        TK = take(2 * GT)
        TB = take(2 * GT)
        BH = take(2 * GT)
        AR = take(2 * 2 * GT)
        BDB, BDK, BDA, BDR = (take(4 * GT) for _ in range(4))
        BT = take(8 * GT)
        NB, AAK, ARB, ARK = (take(4 * GT) for _ in range(4))
        GS = take(2 * GT)
        ZS = take(2 * GT)
        TBD = take(4 * GT)
        GBD = take(4 * GT)
        VST = take(2 * GT)
        MS = [take(P) for _ in range(2)]
        MP = take(P)
        WSB = take(P)
        USB = take(P)
        CM = STG[0][:, 0:GT]
        assert top[0] <= base + 3 * KD * PADW, top[0] - base - 3 * KD * PADW
        top[0] = base + KD * TL
        RIN = take(3 * TL)
        RW2 = take(2 * P)
        RG2 = take(2 * P)
        YC = take(TL)
        YT = take(TL)
        SQY = take(TL)
        RTY = take(TL)
        RTA = take(2 * TL)
        RBY = take(TL)
        BVY = take(TL)

        norm_tmp = {"a0": (SQa, RRa), "f0": (SQf, RRf), "a1": (SQr, RRr), "f1": (SQf, RRf), "end": (SQf, RRf)}

        def a_rhs(k, sl):
            return AH[:, k * T + sl[0]:k * T + sl[0] + sl[1]]

        def f_rhs(k, sl):
            return FHB[:, k * T + sl[0]:k * T + sl[0] + sl[1]]

        def g_rhs(k, sl):
            return G[:, k * T + sl[0]:k * T + sl[0] + sl[1]]

        def m_rhs(k, sl):
            return MX1[:, k * PADW + padded(sl[0]):k * PADW + padded(sl[0]) + sl[1]]

        def ah_h(f, sl):
            return AH[:, f * T + sl[0]:f * T + sl[0] + sl[1]]

        def fh_h(f, sl):
            return FHB[:, f * T + sl[0]:f * T + sl[0] + sl[1]]

        def hp_h(f, sl):
            return HP[:, f * PADW + padded(sl[0]):f * PADW + padded(sl[0]) + sl[1]]

        lat = dict(nk=10, q0=TC, per=4, it0=0, its=NPAIR * 4, even=2, odd=1, g0=0, e0=0, o0=0)
        con = dict(nk=2, q0=0, per=1, it0=NPAIR * 4, its=NPAIR, even=1, odd=0, g0=NPAIR * 16 * 3, e0=NPAIR * 16 * 2,
                   o0=NPAIR * 16)

        def att_pieces(a):
            return [(c, min(512, a["nk"] * P - c)) for c in range(0, a["nk"] * P, 512)]

        def att_groups(a):
            return [list(range(g, min(g + 4, a["nk"]))) for g in range(0, a["nk"], 4)]

        def att_cols(a, i, tt):
            if a["per"] == 1:
                return i, a["q0"] + tt * P
            return i // a["per"], (i % a["per"]) * (2 * P) + (a["q0"] + tt * P)

        def att_ahead(a, i, u, n):
            return (i, u + n) if u + n < 4 else (i + 1, u + n - 4)

        def att_steps(eng, a, body):
            with eng.Fori(0, a["its"] - 1) as i:
                for u in range(4):
                    body(i, u, False)
            for u in range(4):
                body(a["its"] - 1, u, True)

        def att_pe(pe, a):
            pieces, groups = att_pieces(a), att_groups(a)
            ng = len(groups)

            def scores(i, u, piece):
                tt, hh = u // 2, u % 2
                hp, _ = att_cols(a, i, tt)
                if piece == 0:
                    pe.wait_ge(s_qs, (i + a["it0"]) * 2 + tt + 1)
                    pe.wait_ge(s_pr, (i + a["it0"]) * 4 + u + 1)
                c, w = pieces[piece]
                mm = pe.matmul(PS[:, 1536 * (u % 2) + c:1536 * (u % 2) + c + w], QS[tt][hh],
                               KDUP[:, ds((hp // 2) * T + c, w)], start=True, stop=True)
                if piece == len(pieces) - 1:
                    mm.then_inc(s_sc, 1)

            def unit(i, u, last):
                tt, hh = u // 2, u % 2
                n = (i + a["it0"]) * 4 + u
                b = (i + a["it0"]) * 2 + tt
                hp, _ = att_cols(a, i, tt)
                nxt = None if last and u >= 2 else att_ahead(a, i, u, 2)
                left = list(range(len(pieces))) if nxt else []
                pe.wait_ge(s_pr, n + 3)
                for g, tiles in enumerate(groups):
                    if g == 1:
                        pe.wait_ge(s_pta, (i * 4 + u) * a["even"] + a["e0"] + 1)
                    if g == 2:
                        pe.wait_ge(s_ptd, (i * 4 + u) * a["odd"] + a["o0"] + 1)
                    for x, kt in enumerate(tiles):
                        o = 6 * 512 + x * P
                        mm = pe.transpose(PS[:, o:o + P], PB[u % 2][:, kt * P:(kt + 1) * P], cst("ident"))
                    mm.then_inc(s_pt, 1)
                    if left:
                        scores(*nxt, left.pop(0))
                while left:
                    scores(*nxt, left.pop(0))
                pe.wait_ge(s_os, n + 2)
                pe.wait_ge(s_otc, b + 2)
                pe.wait_ge(s_pta, (i * 4 + u) * a["even"] + a["e0"] + a["even"])
                if a["odd"]:
                    pe.wait_ge(s_ptd, (i * 4 + u) * a["odd"] + a["o0"] + a["odd"])
                o = 7 * 512
                for kt in range(a["nk"]):
                    mm = pe.matmul(PS[:, o:o + DH], PTB[:, kt * P:(kt + 1) * P],
                                   VT[:, ds((hp // 2) * DH + kt * HKV * DH, DH)], start=kt == 0, stop=kt == a["nk"] - 1)
                mm.then_inc(s_pv, 1)
                if hh == 1:
                    pe.wait_ge(s_os, n + 3)
                    o = 7 * 512 + 256
                    pe.transpose(PS[:, o:o + P], OS[tt], cst("ident")).then_inc(s_ot, 1)

            for u in range(2):
                for p in range(len(pieces)):
                    scores(0, u, p)
            att_steps(pe, a, unit)

        def att_pool(pool, a):
            with pool.Fori(0, a["its"]) as i:
                for tt in range(2):
                    hp, t0 = att_cols(a, i, tt)
                    pool.wait_ge(s_sc, (i + a["it0"]) * 4 + 2 * tt + 2)
                    for hh in range(2):
                        i_ = pool.tensor_copy(QS[tt][hh][64 * hh:64 * hh + 64, :],
                                              QK[64 * hh:64 * hh + 64, ds(hp * T + t0, P)])
                    i_.then_inc(s_qs, 1)

        def att_dve(dve, a):
            groups = att_groups(a)

            def row_max(i, u):
                dve.wait_ge(s_sc, (i + a["it0"]) * 4 + u + 5)
                dve.tensor_reduce(MXN[:, u:u + 1], PS[:, 1536 * (u % 2):1536 * (u % 2) + a["nk"] * P], AX_X, ALU.max,
                                  negate=True).then_inc(s_mx, 1)

            def unit(i, u, last):
                tt, hh = u // 2, u % 2
                n = (i + a["it0"]) * 4 + u
                if not (last and u == 3):
                    row_max(*att_ahead(a, i, u, 1))
                for g in range(1, len(groups), 2):
                    w = len(groups[g]) * P
                    dve.wait_ge(s_pt, (i * 4 + u) * len(groups) + a["g0"] + g + 1)
                    dve.wait_ge(s_pv, n + 2)
                    dve.tensor_copy(PTB[:, groups[g][0] * P:groups[g][0] * P + w],
                                    PS[:, 6 * 512:6 * 512 + w]).then_inc(s_ptd, 1)
                dve.wait_ge(s_pr, n + 3)
                dve.reciprocal(RINV[:, u:u + 1], RSUM[:, u:u + 1])
                dve.drain()
                dve.wait_ge(s_pv, n + 3)
                if hh == 0:
                    dve.wait_ge(s_ot, (i + a["it0"]) * 2 + tt + 1)
                o = 7 * 512
                dve.tensor_scalar(OS[tt][:, hh * DH:(hh + 1) * DH], PS[:, o:o + DH], RINV[:, u:u + 1], None, ALU.mult
                                  ).then_inc(s_os, 1)

            row_max(0, 0)
            att_steps(dve, a, unit)

        def att_act(act, a):
            groups = att_groups(a)

            def probs(i, u):
                act.wait_ge(s_mx, (i + a["it0"]) * 4 + u + 1)
                act.wait_ge(s_pv, (i + a["it0"]) * 4 + u + 1)
                act.activation(PB[u % 2][:, 0:a["nk"] * P], PS[:, 1536 * (u % 2):1536 * (u % 2) + a["nk"] * P],
                               ACT.Exp, bias=MXN[:, u:u + 1], accum_out=RSUM[:, u:u + 1]).then_inc(s_pr, 1)

            def unit(i, u, last):
                tt, hh = u // 2, u % 2
                n = (i + a["it0"]) * 4 + u
                if not (last and u == 3):
                    probs(*att_ahead(a, i, u, 1))
                for g in range(0, len(groups), 2):
                    w = len(groups[g]) * P
                    act.wait_ge(s_pt, (i * 4 + u) * len(groups) + a["g0"] + g + 1)
                    act.wait_ge(s_pv, n + 2)
                    act.activation(PTB[:, groups[g][0] * P:groups[g][0] * P + w], PS[:, 6 * 512:6 * 512 + w],
                                   ACT.Copy).then_inc(s_pta, 1)
                if hh == 1:
                    hp, t0 = att_cols(a, i, tt)
                    act.wait_ge(s_ot, (i + a["it0"]) * 2 + tt + 3)
                    o = 7 * 512 + 256
                    act.activation(AH[:, ds(hp * T + t0, P)], PS[:, o:o + P], ACT.Copy).then_inc(s_otc, 1)

            probs(0, 0)
            att_steps(act, a, unit)

        PIECES = [(0, 512), (512, 512), (1024, 256)]

        def qk_pe(pe):
            with pe.Fori(0, 10) as n:
                pe.wait_ge(s_hsq, n + 1)
                pe.wait_ge(s_hroot, n + 1)
                for c, w in PIECES:
                    mm = pe.matmul(PS[:, c:c + w], cst("mean64"), SQQ[:, c:c + w], start=True, stop=True)
                mm.then_inc(s_hms, 1)
                pe.wait_ge(s_qn, n + 1)
                pe.wait_ge(s_qkd, n + 1)
                for c, w in PIECES:
                    mm = pe.matmul(PS[:, 1536 + c:1536 + c + w], cst("swap"), QK[:, ds(n * T + c, w)], start=True,
                                   stop=True)
                mm.then_inc(s_rot, 1)

        def qk_act(act):
            with act.Fori(0, 10) as n:
                act.wait_ge(s_hms, n + 1)
                act.activation(SQQ, QK[:, ds(n * T, T)], ACT.Square).then_inc(s_hsq, 1)
                act.wait_ge(s_hms, n + 2)
                act.wait_ge(s_qkd, n + 1)
                act.activation(T1, PS[:, 0:T], ACT.Sqrt, bias=NEG[:, 1:2]).then_inc(s_hroot, 1)

        def qk_dve(dve):
            with dve.Fori(0, 10) as n:
                q = QK[:, ds(n * T, T)]
                dve.wait_ge(s_hroot, n + 2)
                dve.reciprocal(T1, T1)
                dve.drain()
                dve.scalar_tensor_tensor(q, q, vec("qk_gain", n), T1, ALU.mult, ALU.mult).then_inc(s_qn, 1)
                dve.drain()
                dve.tensor_tensor(T1, q, ROPE[:, 0:T], ALU.mult)
                dve.drain()
                dve.wait_ge(s_rot, n + 1)
                dve.tensor_tensor(q, PS[:, 1536:1536 + T], ROPE[:, T:2 * T], ALU.mult)
                dve.drain()
                dve.tensor_tensor(q, q, T1, ALU.add).then_inc(s_qkd, 1)

        def up_evac_act(act, lay, half, slices, q0):
            name = f"up{lay}{half}"
            lo = padded(slices[0][0])
            w = padded(T) - lo

            def before(i, s):
                act.wait_ge(s_cv[s], i + q0 + 1)

            def read(n, s, j, sl, ps):
                return act.activation(UB[s][:, padded(sl[0]):padded(sl[0]) + sl[1]], ps, ACT.Copy)

            def after(i, s):
                if s == 1:
                    act.wait_ge(s_cv[0], i + q0 + 2)
                    act.activation(CB[0][:, lo:lo + w], CB[0][:, lo:lo + w], ACT.Silu).then_inc(s_sg, 1)

            dense_evac(act, name, read, before, after)

        def up_evac_dve(dve, lay, half, slices, q0):
            name = f"up{lay}{half}"
            d = order[name]
            lo = padded(slices[0][0])
            w = padded(T) - lo
            with dve.Fori(0, d.loops) as i:
                for s in range(2):
                    dve.wait_ge(s_read[name][s], i * d.j + 2 * d.j)
                    cv = VEC["conv"] + ((lay * FJ + half * FH) * 2 + s) * 4
                    cw = [VECS[:, ds(i * 8 + cv + x, 1)] for x in range(4)]
                    u, c = UB[s], CB[s][:, lo:lo + w]
                    dve.tensor_scalar(c, u[:, lo:lo + w], cw[1], cw[3], ALU.mult, ALU.add)
                    dve.drain()
                    dve.scalar_tensor_tensor(c, u[:, lo - 1:lo - 1 + w], cw[0], c, ALU.mult, ALU.add)
                    dve.drain()
                    dve.scalar_tensor_tensor(c, u[:, lo + 1:lo + 1 + w], cw[2], c, ALU.mult, ALU.add
                                             ).then_inc(s_cv[s], 1)
                dve.drain()
                dve.wait_ge(s_sg, i + q0 + 1)
                for t0, n in ([(0, TC)] if slices[0][0] == 0 else []) + [(TC, TL)]:
                    dve.tensor_tensor(G[:, ds(i * T + t0, n)], CB[0][:, padded(t0):padded(t0) + n],
                                      CB[1][:, padded(t0):padded(t0) + n], ALU.mult)
                dve.drain()

        def add_to_stream(dve, name, lay, comp):
            def read(n, s, j, sl, ps):
                x = xs(n, sl)
                return dve.scalar_tensor_tensor(x, ps, mod(lay, comp, n, sl[2]), x, ALU.mult, ALU.add)

            dense_evac(dve, name, read)

        def mix(dve, m):
            for f in range(KD):
                dve.scalar_tensor_tensor(MX1[:, f * PADW + 1:f * PADW + T + 2], XX[:, f * PADW + 1:f * PADW + T + 2],
                                         vec("mu", m * KD + f), HP[:, f * PADW + 1:f * PADW + T + 2], ALU.mult, ALU.add)

        def shift_pool(pool):
            for f in range(KD):
                o = f * PADW
                pool.tensor_tensor(XX[:, o + 1:o + T + 2], HP[:, o:o + T + 1], HP[:, o + 2:o + T + 3], ALU.add
                                   ).then_inc(s_mix, 1)

        def shift_dve(dve):
            for f in range(KD):
                o = f * PADW
                dve.wait_ge(s_mix, f + 1)
                dve.scalar_tensor_tensor(XX[:, o + 1:o + T + 2], XX[:, o + 1:o + T + 2], 0.5, HP[:, o + 1:o + T + 2],
                                         ALU.mult, ALU.subtract)

        def spill_act(act, name, sp0):
            def before(i, s):
                act.wait_ge(s_spd[s], (i + sp0 + 1) * 16)

            def read(n, s, j, sl, ps):
                return act.activation(STG[s][:, sl[0]:sl[0] + sl[1]], ps, ACT.Copy)

            dense_evac(act, name, read, before)

        def spill_store(sp, name, dram):
            d = order[name]
            t0 = d.slices[0][0]

            def store(i, s):
                sp.wait_ge(s_read[name][s], i * d.j + 2 * d.j)
                o = dram[i * 2 + s] if isinstance(i, int) else dram[ds(i * 2 + s, 1)].rearrange("o p t -> (o p) t")
                sp.dma_start(o[:, t0:T], STG[s][:, t0:T]).then_inc(s_spd[s], 16)

            return store

        KQ, KR = STG

        def kk_pe(pe):
            with pe.Fori(0, KD) as n:
                pe.wait_ge(s_hsq, n + 11)
                pe.wait_ge(s_hroot, n + 11)
                for c, w in PIECES:
                    mm = pe.matmul(PS[:, c:c + w], cst("sum64"), KQ[:, c:c + w], start=True, stop=True)
                mm.then_inc(s_hms, 1)

        def kk_act(act):
            with act.Fori(0, KD) as n:
                act.wait_ge(s_hms, n + 11)
                act.activation(KQ, KF[:, ds(n * T, T)], ACT.Square, scale=vec("k_k", n)).then_inc(s_hsq, 1)
                act.wait_ge(s_hms, n + 12)
                act.wait_ge(s_qn, n + 10)
                act.activation(KR, PS[:, 0:T], ACT.Sqrt).then_inc(s_hroot, 1)

        def kk_dve(dve):
            with dve.Fori(0, KD) as n:
                dve.wait_ge(s_hroot, n + 12)
                dve.tensor_scalar(KR, KR, 1e-12, None, ALU.max)
                dve.drain()
                dve.reciprocal(KR, KR)
                dve.drain()
                dve.scalar_tensor_tensor(NF[:, ds(n * T, T)], KF[:, ds(n * T, T)], vec("k_k", n), KR, ALU.mult, ALU.mult
                                         ).then_inc(s_qn, 1)

        def half(buf, h, n=NU):
            return buf[64 * h:64 * h + 64, :].rearrange("p (u g t) -> p u g t", u=n, g=2)[:, :, h, :]

        def half4(buf, h):
            return buf[64 * h:64 * h + 64, :].rearrange("p (d c g t) -> p d c g t", d=2, c=4, g=2)[:, :, :, h, :]

        def units(ap):
            return ap.rearrange("p (u t) -> p u t", t=CH)

        def mask_half(lev, h):
            return mask(lev)[64 * h:64 * h + 64].rearrange("p (d t) -> p d t", d=2).unsqueeze(2).broadcast_to([64, 2, 4, CH])

        def mask_all(lev):
            return mask(lev).rearrange("p (d t) -> p d t", d=2).unsqueeze(2).broadcast_to([P, 2, 4, CH])

        def dct(ap):
            return ap.rearrange("p (d c t) -> p d c t", d=2, c=4)

        STRICT, STRICT_T, INCL_T, EYE = 6, 7, 8, 9
        NL = len(LEVELS)

        def group_starts(g):
            return [g * GT, (5 - g) % 5 * GT]

        def groups(eng, body):
            with eng.Fori(0, NPAIR) as p:
                body(p, 0, True)
                with eng.Fori(1, NGR) as g:
                    body(p, g, False)

        def scan_unit(d, s):
            return s if d == 0 else 7 - s

        def scan_loads(sp):
            def body(p, g, ctx_):
                it = p * NGR + g
                itl = p * (NGR - 1) + g - 1
                sp.wait_ge(s_hat, it + 1)
                sp.wait_ge(s_kd, it + 1)
                sp.wait_ge(s_vt, it + 1)
                g0 = group_starts(g)
                for x, dram in enumerate((k_dram, n_dram, v_dram)):
                    for d in range(2):
                        o = x * 2 * GT + d * GT
                        sp.dma_start(KIN[:, o:o + GT], dram[ds(p, 1), :, ds(g0[d], GT)].rearrange("o p t -> (o p) t")
                                     ).then_inc(s_kin, 16)
                sp.dma_start(W2, a_lora2[ds(p, 1)].rearrange("o p q -> (o p) q")).then_inc(s_kin, 16)
                if not ctx_:
                    for d in range(2):
                        o = 3 * 2 * GT + d * GT
                        sp.dma_start(KIN[:, o:o + GT], r_dram[ds(p, 1), :, ds(g0[d], GT)].rearrange("o p t -> (o p) t")
                                     ).then_inc(s_rin, 16)

            groups(sp, body)

        def scan_pe(pe):
            def body(p, g, ctx_):
                it = p * NGR + g
                g0 = group_starts(g)
                pe.wait_ge(s_kin, it * 112 + 112)
                for x, hid in enumerate((HW, HA)):
                    for d in range(2):
                        o = (6 + x) * 512 + d * GT
                        mm = pe.matmul(PS[:, o:o + GT], W2[:, (2 * x + d) * P:(2 * x + d + 1) * P],
                                       hid[:, ds(g0[d], GT)], start=True, stop=True)
                mm.then_inc(s_lz, 1)
                pe.wait_ge(s_th, it + 1)
                apart(pe)
                for u in range(NU):
                    o = 2 * 2 * GT + u * CH
                    mm = pe.transpose(PS[0:64, 6 * 512 + u * P:6 * 512 + (u + 1) * P], KIN[:, o:o + CH], cst("ident"))
                mm.then_inc(s_vt, 1)
                pe.wait_ge(s_bd, it + 1)
                pe.wait_ge(s_vc, it + 1)
                for u in range(NU):
                    mm = pe.matmul(PS[:, 6 * 512 + u * CH:6 * 512 + (u + 1) * CH], BDA[:, u * P:(u + 1) * P],
                                   BH[:, u * CH:(u + 1) * CH], start=True, stop=True)
                mm.then_inc(s_s1, 1)
                for x, bd in ((2, BDB), (4, BDK)):
                    for u in range(NU):
                        mm = pe.matmul(PS[:, x * 512 + u * P:x * 512 + (u + 1) * P], bd[:, u * P:(u + 1) * P],
                                       AR[:, u * P:(u + 1) * P], start=True, stop=True)
                    mm.then_inc(s_s1, 1)
                pe.wait_ge(s_m1, it + 1)
                for lv in range(NL):
                    pe.wait_ge(s_g, it * (NL + 1) + lv + 1)
                    apart(pe)
                    for u in range(NU):
                        mm = pe.transpose(PS[0:64, 2 * 512 + u * P:2 * 512 + (u + 1) * P], GS[:, u * CH:(u + 1) * CH],
                                          cst("ident"))
                    mm.then_inc(s_gt, 1)
                    for u in range(NU):
                        mm = pe.matmul(PS[:, 4 * 512 + u * CH:4 * 512 + (u + 1) * CH], NB[:, u * P:(u + 1) * P],
                                       GS[:, u * CH:(u + 1) * CH], start=True, stop=True)
                    mm.then_inc(s_z, 1)
                    if lv < 4:
                        if lv:
                            pe.wait_ge(s_trc, it * 4 + lv)
                        bd = BDB if lv < 2 else BDK
                        for x in range(4):
                            u = (lv % 2) * 4 + x
                            mm = pe.transpose(PS[:, 7 * 512 + x * P:7 * 512 + (x + 1) * P], bd[:, u * P:(u + 1) * P],
                                              cst("ident"))
                        mm.then_inc(s_tr, 1)
                    pe.wait_ge(s_zc, it * NL + lv + 1)
                    pe.wait_ge(s_gtc, it * NL + lv + 1)
                    for u in range(NU):
                        mm = pe.matmul(PS[:, 5 * 512 + u * CH:5 * 512 + (u + 1) * CH], TBD[:, u * P:(u + 1) * P],
                                       ZS[:, u * CH:(u + 1) * CH], start=True, stop=True)
                    mm.then_inc(s_gz, 1)
                if not ctx_:
                    pe.wait_ge(s_bdr, it + 1)
                    pe.wait_ge(s_yc, p * (NGR - 1) + g)
                pe.wait_ge(s_trc, it * 4 + 4)
                for s in range(4):
                    m = MS[s % 2]
                    pe.wait_ge(s_St, it * 4 + s + 1)
                    for d in range(2):
                        u = scan_unit(d, s)
                        o = PS[:, d * CH:(d + 1) * CH]
                        pe.matmul(o, BDA[:, u * P:(u + 1) * P], m[:, d * CH:(d + 1) * CH], start=True, stop=False)
                        mm = pe.matmul(o, AAK[:, u * P:(u + 1) * P], VST[:, u * CH:(u + 1) * CH], start=False, stop=True)
                    mm.then_inc(s_W, 1)
                    if s == 0:
                        pe.wait_ge(s_gb, it + 1)
                    pe.wait_ge(s_Wc, it * 4 + s + 1)
                    for d in range(2):
                        u = scan_unit(d, s)
                        mm = pe.matmul(PS[:, P + d * CH:P + (d + 1) * CH], GBD[:, u * P:(u + 1) * P],
                                       WSB[:, d * CH:(d + 1) * CH], start=True, stop=True)
                    mm.then_inc(s_U, 1)
                    pe.wait_ge(s_Uc, it * 4 + s + 1)
                    for d in range(2):
                        u = scan_unit(d, s)
                        o = PS[:, 2 * P + d * CH:2 * P + (d + 1) * CH]
                        pe.matmul(o, BT[:, u * P:(u + 1) * P], USB[:, d * CH:(d + 1) * CH], start=True, stop=False)
                        mm = pe.matmul(o, BT[:, (NU + u) * P:(NU + u + 1) * P], VST[:, u * CH:(u + 1) * CH],
                                       start=False, stop=True)
                    mm.then_inc(s_D, 1)
                    if ctx_:
                        continue
                    for d in range(2):
                        u = scan_unit(d, s)
                        o = PS[:, 512 + u * CH:512 + (u + 1) * CH]
                        pe.matmul(o, BDR[:, u * P:(u + 1) * P], m[:, d * CH:(d + 1) * CH], start=True, stop=False)
                        pe.matmul(o, ARB[:, u * P:(u + 1) * P], USB[:, d * CH:(d + 1) * CH], start=False, stop=False)
                        mm = pe.matmul(o, ARK[:, u * P:(u + 1) * P], VST[:, u * CH:(u + 1) * CH], start=False, stop=True)
                    mm.then_inc(s_y, 1)

            groups(pe, body)

        def scan_act(act):
            def body(p, g, ctx_):
                it = p * NGR + g
                act.wait_ge(s_lz, it + 1)
                apart(act)
                for d in range(2):
                    act.activation(TZ[:, d * GT:(d + 1) * GT], PS[:, 6 * 512 + d * GT:6 * 512 + (d + 1) * GT], ACT.Tanh,
                                   bias=DER[:, ds(p + d * 8, 1)], scale=0.5)
                for d in range(2):
                    i_ = act.activation(TA[:, d * GT:(d + 1) * GT], PS[:, 7 * 512 + d * GT:7 * 512 + (d + 1) * GT],
                                        ACT.Tanh, bias=DER[:, ds(p + 16 + d * 8, 1)], scale=0.5)
                i_.then_inc(s_th, 1)
                act.wait_ge(s_vt, it + 2)
                for h in range(2):
                    i_ = act.activation(units(VST[64 * h:64 * h + 64, :]),
                                        PS[0:64, 6 * 512:8 * 512].rearrange("p (u g v) -> p u g v", u=NU, g=2)[:, :, h, :],
                                        ACT.Copy)
                i_.then_inc(s_vc, 1)
                act.wait_ge(s_cum, it + 1)
                act.activation(XN, IN, ACT.Exp, scale=DECAY)
                act.activation(EX, EX, ACT.Exp, scale=-DECAY)
                act.drain()
                act.activation(IN, IN, ACT.Exp, scale=-DECAY).then_inc(s_xp, 1)
                act.wait_ge(s_hat, it + 2)
                for h in range(2):
                    act.activation(half(BDB, h), units(BH[64 * h:64 * h + 64, :]), ACT.Copy)
                for h in range(2):
                    i_ = act.activation(half(BDA, h),
                                        AR[64 * h:64 * h + 64, :].rearrange("p (u x t) -> p u x t", u=NU, x=2)[:, :, 0, :],
                                        ACT.Copy)
                i_.then_inc(s_bd, 1)
                for lv in range(NL):
                    act.wait_ge(s_gt, it * NL + lv + 1)
                    for h in range(2):
                        i_ = act.activation(half(TBD, h),
                                            PS[0:64, 2 * 512:4 * 512].rearrange("p (u g v) -> p u g v", u=NU, g=2)[:, :, h, :],
                                            ACT.Copy)
                    i_.then_inc(s_gtc, 1)
                    if lv < 4:
                        act.wait_ge(s_tr, it * 4 + lv + 1)
                        act.activation(BT[:, lv * 512:(lv + 1) * 512], bank(7), ACT.Copy).then_inc(s_trc, 1)
                act.wait_ge(s_g, (it + 1) * (NL + 1))
                for h in range(2):
                    i_ = act.activation(half(GBD, h), units(GS[64 * h:64 * h + 64, :]), ACT.Copy)
                i_.then_inc(s_gb, 1)
                for s in range(4):
                    act.wait_ge(s_W, it * 4 + s + 1)
                    act.activation(WSB, PS[:, 0:P], ACT.Copy).then_inc(s_Wc, 1)
                    act.wait_ge(s_U, it * 4 + s + 1)
                    act.activation(USB, PS[:, P:2 * P], ACT.Copy).then_inc(s_Uc, 1)

            groups(act, body)

        def scan_pool(pool):
            def body(p, g, ctx_):
                it = p * NGR + g
                pool.wait_ge(s_kin, it * 112 + 112)
                pool.wait_ge(s_cum, it + 1)
                apart(pool)
                pool.tensor_scalar(TK, TA, KA[:, 0:1], KA[:, 1:2], ALU.mult, ALU.add)
                pool.tensor_scalar(TB, TA, 0.5, 0.5, ALU.mult, ALU.add)
                pool.drain()
                pool.tensor_tensor(TK, TK, KIN[:, 0:2 * GT], ALU.mult)
                pool.tensor_tensor(TB, TB, KIN[:, 2 * GT:4 * GT], ALU.mult).then_inc(s_kd, 1)
                if not ctx_:
                    pool.wait_ge(s_hat, it + 2)
                    apart(pool)
                    for h in range(2):
                        i_ = pool.tensor_copy(half(BDR, h), AR[64 * h:64 * h + 64, :].rearrange(
                            "p (u x t) -> p u x t", u=NU, x=2)[:, :, 1, :])
                    i_.then_inc(s_bdr, 1)
                else:
                    pool.sem_inc(s_bdr, 1)

            groups(pool, body)

        def scan_dve(dve):
            def body(p, g, ctx_):
                it = p * NGR + g
                itl = p * (NGR - 1) + g - 1
                if ctx_:
                    dve.memset(MS[0], 0.0)
                    dve.wait_ge(s_kd, it + 1)
                    dve.tensor_copy(KA[:, 0:1], DER[:, ds(p + 32, 1)])
                    dve.tensor_copy(KA[:, 1:2], DER[:, ds(p + 40, 1)])
                dve.wait_ge(s_th, it + 1)
                dve.tensor_scalar(TZ, TZ, 0.5, 0.5, ALU.mult, ALU.add)
                dve.drain()
                sg = [TZ[:, 0:GT], TZ[:, GT:2 * GT]]
                i0, i1, e0, e1 = IN[:, 0:GT], IN[:, GT:2 * GT], EX[:, 0:GT], EX[:, GT:2 * GT]
                dve.tensor_tensor_scan(i0, CM, sg[0], 0.0, ALU.mult, ALU.add)
                dve.tensor_tensor_scan(F1, CM, sg[1], 0.0, ALU.mult, ALU.add)
                dve.drain()
                dve.tensor_tensor(e0, i0, sg[0], ALU.subtract)
                dve.tensor_tensor(units(e1), units(F1)[:, :, CH - 1:CH].broadcast_to([P, 4, CH]), units(F1), ALU.subtract)
                dve.drain()
                dve.tensor_tensor(i1, e1, sg[1], ALU.add).then_inc(s_cum, 1)
                dve.wait_ge(s_kd, it + 2)
                dve.wait_ge(s_xp, it + 1)
                dve.tensor_tensor(BH, TB, XN, ALU.mult)
                for h in range(2):
                    dve.tensor_tensor(half(BDK, h), units(TK[64 * h:64 * h + 64, :]), units(XN[64 * h:64 * h + 64, :]),
                                      ALU.mult)
                ar = AR.rearrange("p (u x t) -> p u x t", u=NU, x=2)
                if not ctx_:
                    dve.wait_ge(s_rin, itl * 32 + 32)
                    dve.wait_ge(s_bdr, it)
                    dve.tensor_tensor(ar[:, :, 1, :], units(KIN[:, 6 * GT:8 * GT]), units(IN), ALU.mult)
                dve.scalar_tensor_tensor(ar[:, :, 0, :], units(KIN[:, 2 * GT:4 * GT]), -1.0, units(EX), ALU.mult, ALU.mult
                                         ).then_inc(s_hat, 1)
                dve.wait_ge(s_s1, it * 3 + 1)
                for h in range(2):
                    dve.tensor_tensor(half4(NB, h), dct(PS[64 * h:64 * h + 64, 6 * 512:7 * 512]), mask_half(STRICT, h),
                                      ALU.mult)
                dve.wait_ge(s_s1, it * 3 + 2)
                s1 = PS[:, 2 * 512:4 * 512].rearrange("p (d c x t) -> p d c x t", d=2, c=4, x=2)
                s2 = PS[:, 4 * 512:6 * 512].rearrange("p (d c x t) -> p d c x t", d=2, c=4, x=2)
                dve.tensor_tensor(dct(GS), s1[:, :, :, 0, :], mask_all(0), ALU.mult)
                if not ctx_:
                    for h in range(2):
                        dve.tensor_tensor(half4(ARB, h), s1[64 * h:64 * h + 64, :, :, 1, :], mask_half(INCL_T, h), ALU.mult)
                dve.drain()
                dve.tensor_tensor(dct(GS), dct(GS), mask_all(EYE), ALU.add).then_inc(s_g, 1)
                dve.wait_ge(s_s1, it * 3 + 3)
                for h in range(2):
                    i_ = dve.tensor_tensor(half4(AAK, h), s2[64 * h:64 * h + 64, :, :, 0, :], mask_half(STRICT_T, h),
                                           ALU.mult)
                if not ctx_:
                    for h in range(2):
                        i_ = dve.tensor_tensor(half4(ARK, h), s2[64 * h:64 * h + 64, :, :, 1, :], mask_half(INCL_T, h),
                                               ALU.mult)
                i_.then_inc(s_m1, 1)
                for lv in range(NL):
                    dve.wait_ge(s_z, it * NL + lv + 1)
                    dve.tensor_tensor(dct(ZS), dct(bank(4)), mask_all(lv + 1), ALU.mult).then_inc(s_zc, 1)
                    dve.wait_ge(s_gz, it * NL + lv + 1)
                    dve.tensor_tensor(GS, GS, bank(5), ALU.add).then_inc(s_g, 1)
                for s in range(4):
                    m, nxt = MS[s % 2], MS[(s + 1) % 2]
                    pc = []
                    for d in range(2):
                        u = scan_unit(d, s)
                        o = u * CH + (CH - 1 if d == 0 else 0)
                        pc.append(IN[:, o:o + 1])
                    for d in range(2):
                        dve.tensor_scalar(MP[:, d * CH:(d + 1) * CH], m[:, d * CH:(d + 1) * CH], pc[d], None, ALU.mult)
                    dve.drain()
                    dve.wait_ge(s_D, it * 4 + s + 1)
                    for d in range(2):
                        i_ = dve.scalar_tensor_tensor(nxt[:, d * CH:(d + 1) * CH], PS[:, 2 * P + d * CH:2 * P + (d + 1) * CH],
                                                      pc[d], MP[:, d * CH:(d + 1) * CH], ALU.mult, ALU.add)
                    i_.then_inc(s_St, 1)
                    dve.drain()
                if not ctx_:
                    dve.wait_ge(s_y, itl * 4 + 4)
                    for d, t0 in enumerate(((g - 1) * GT, (4 - g) * GT)):
                        ys = YS[:, ds(p * TL + t0, GT)]
                        i_ = dve.tensor_tensor(ys, ys, PS[:, 512 + d * GT:512 + (d + 1) * GT], ALU.add)
                    i_.then_inc(s_yc, 1)
                    dve.drain()

            groups(dve, body)

        HALVES = [(0, 512), (512, 512)]

        def read_loads(sp):
            with sp.Fori(0, NPAIR) as p:
                sp.wait_ge(s_r3r, p + 1)
                sp.wait_ge(s_r3p, p * 6 + 1)
                for x, dram in enumerate((k_dram, r_dram, v_dram)):
                    sp.dma_start(RIN[:, x * TL:(x + 1) * TL], dram[ds(p, 1), :, TC:T].rearrange("o p t -> (o p) t")
                                 ).then_inc(s_r3, 16)
                sp.dma_start(RW2, a_lora2[ds(p, 1), :, 2 * P:4 * P].rearrange("o p q -> (o p) q")).then_inc(s_r3, 16)
                sp.dma_start(RG2, a_g2[ds(p, 1)].rearrange("o p q -> (o p) q")).then_inc(s_r3, 16)

        def read_pool(pool):
            with pool.Fori(0, NPAIR) as p:
                pool.wait_ge(s_r3p, p * 6 + 1)
                pool.tensor_copy(YC, YS[:, ds(p * TL, TL)]).then_inc(s_r3c, 1)

        def read_pe(pe):
            with pe.Fori(0, NPAIR) as p:
                pe.wait_ge(s_r3c, p + 1)
                pe.wait_ge(s_r3v, p * 5 + 1)
                apart(pe)
                for c in range(TL // CH):
                    mm = pe.transpose(PS[0:64, c * P:(c + 1) * P], YC[:, c * CH:(c + 1) * CH], cst("ident"))
                mm.then_inc(s_r3p, 1)
                pe.wait_ge(s_r3a, p * 4 + 1)
                for c, w in HALVES:
                    mm = pe.matmul(PS[:, 2048 + c:2048 + c + w], cst("mean64"), YT[:, c:c + w], start=True, stop=True)
                mm.then_inc(s_r3p, 1)
                pe.wait_ge(s_r3, p * 80 + 80)
                for d in range(2):
                    for c, w in HALVES:
                        mm = pe.matmul(PS[:, d * TL + c:d * TL + c + w], RW2[:, d * P:(d + 1) * P],
                                       HA[:, TC + c:TC + c + w], start=True, stop=True)
                mm.then_inc(s_r3p, 1)
                pe.wait_ge(s_r3a, p * 4 + 2)
                for c, w in HALVES:
                    mm = pe.matmul(PS[:, 3072 + c:3072 + c + w], cst("mean64"), SQY[:, c:c + w], start=True, stop=True)
                mm.then_inc(s_r3p, 1)
                pe.wait_ge(s_r3v, p * 5 + 3)
                for c, w in HALVES:
                    mm = pe.matmul(PS[:, 2048 + c:2048 + c + w], cst("sum64"), RBY[:, c:c + w], start=True, stop=True)
                mm.then_inc(s_r3p, 1)
                pe.wait_ge(s_r3a, p * 4 + 3)
                for c, w in HALVES:
                    for kt in range(2):
                        mm = pe.matmul(PS[:, 3072 + c:3072 + c + w], RG2[:, kt * P:(kt + 1) * P],
                                       HG[:, kt * TL + c:kt * TL + c + w], start=kt == 0, stop=kt == 1)
                mm.then_inc(s_r3p, 1)

        def read_act(act):
            with act.Fori(0, NPAIR) as p:
                act.wait_ge(s_r3p, p * 6 + 2)
                act.wait_ge(s_r3v, p * 5 + 1)
                for h in range(2):
                    i_ = act.activation(units(YT[64 * h:64 * h + 64, :]),
                                        PS[0:64, 0:2048].rearrange("p (u g v) -> p u g v", u=TL // CH, g=2)[:, :, h, :],
                                        ACT.Copy)
                i_.then_inc(s_r3a, 1)
                act.wait_ge(s_r3v, p * 5 + 2)
                act.activation(SQY, YT, ACT.Square).then_inc(s_r3a, 1)
                act.wait_ge(s_r3p, p * 6 + 5)
                act.activation(RTY, PS[:, 3072:4096], ACT.Sqrt, bias=NEG[:, 2:3]).then_inc(s_r3a, 1)
                for d in range(2):
                    i_ = act.activation(RTA[:, d * TL:(d + 1) * TL], PS[:, d * TL:(d + 1) * TL], ACT.Tanh,
                                        bias=DER[:, ds(p + 16 + d * 8, 1)], scale=0.5)
                i_.then_inc(s_r3a, 1)

        def read_dve(dve):
            k, r, v = (RIN[:, x * TL:(x + 1) * TL] for x in range(3))
            t0, t1 = RTA[:, 0:TL], RTA[:, TL:2 * TL]
            with dve.Fori(0, NPAIR) as p:
                dve.wait_ge(s_r3p, p * 6 + 3)
                dve.tensor_tensor(YT, YT, PS[:, 2048:3072], ALU.subtract).then_inc(s_r3v, 1)
                dve.wait_ge(s_r3a, p * 4 + 4)
                dve.wait_ge(s_r3, p * 80 + 80)
                dve.tensor_tensor(t0, t0, t1, ALU.add)
                dve.drain()
                dve.tensor_scalar(t0, t0, DER[:, ds(p + 32, 1)], NEG[:, ds(p + 8, 1)], ALU.mult, ALU.add)
                dve.drain()
                dve.tensor_tensor(t0, t0, k, ALU.mult)
                dve.drain()
                dve.scalar_tensor_tensor(RBY, r, vec("r_k", p), t0, ALU.mult, ALU.mult).then_inc(s_r3v, 1)
                dve.reciprocal(RTY, RTY)
                dve.drain()
                dve.tensor_tensor(YT, YT, RTY, ALU.mult)
                dve.drain()
                dve.tensor_scalar(YT, YT, vec("gn_w", p), vec("gn_b", p), ALU.mult, ALU.add)
                dve.wait_ge(s_r3p, p * 6 + 6)
                dve.tensor_tensor(BVY, v, PS[:, 2048:3072], ALU.mult).then_inc(s_r3r, 1)
                dve.drain().then_inc(s_r3v, 1)
                dve.tensor_tensor(YT, YT, BVY, ALU.add).then_inc(s_r3v, 1)
                dve.drain()
                dve.wait_ge(s_r3p, p * 6 + 7)
                dve.tensor_tensor(YS[:, ds(p * TL, TL)], YT, PS[:, 3072:4096], ALU.mult)
                dve.drain().then_inc(s_r3v, 1)

        def ada_loads(sp):
            AW = [SB[:, base + x * 4096:base + (x + 1) * 4096] for x in range(2)]
            for s in range(2):
                sp.dma_start(AW[s], a_adaw[s]).then_inc(s_adaw[s], 16)
            with sp.Fori(1, 12) as i:
                for s in range(2):
                    sp.wait_ge(s_adap, 2 * i + s - 1)
                    sp.dma_start(AW[s], a_adaw[ds(2 * i + s, 1)].rearrange("o p q -> (o p) q")).then_inc(s_adaw[s], 16)

        def ada_pe(pe):
            pe.wait_ge(s_silu, 1)
            with pe.Fori(0, 12) as i:
                for s in range(2):
                    aw = SB[:, base + s * 4096:base + (s + 1) * 4096]
                    pe.wait_ge(s_adaw[s], i * 16 + 16)
                    for n in range(4):
                        for k in range(KD):
                            mm = pe.matmul(PS[:, ds(i * 16 + s * 8 + n * 2, 2)], aw[:, k * 512 + n * P:k * 512 + (n + 1) * P],
                                           SILU[:, 2 * k:2 * k + 2], start=k == 0, stop=k == KD - 1)
                    mm.then_inc(s_adap, 1)

        def ada_dve(dve):
            dve.tensor_scalar(DER[:, 0:16], vec("w0", 0, 16), 0.5, None, ALU.mult)
            dve.tensor_scalar(DER[:, 16:32], vec("a0", 0, 16), 0.5, None, ALU.mult)
            dve.tensor_scalar(DER[:, 32:40], vec("k_a", 0, 8), 0.5, None, ALU.mult)
            dve.tensor_scalar(DER[:, 40:48], vec("k_a", 0, 8), -0.5, 1.0, ALU.mult, ALU.add)
            dve.tensor_scalar(NEG[:, 8:16], vec("k_a", 0, 8), -1.0, 2.0, ALU.mult, ALU.add)
            dve.tensor_scalar(vec("qk_gain", 0, 8), vec("qk_gain", 0, 8), DH ** -0.5, None, ALU.mult)
            dve.wait_ge(s_adap, 24)
            m = MOD.rearrange("p (n s) -> p n s", s=2)
            dve.tensor_tensor(m, PS[:, 0:192].rearrange("p (n s) -> p n s", s=2),
                              vec("ada_b", 0, 96).unsqueeze(2).broadcast_to([P, 96, 2]), ALU.add)
            dve.drain()
            for lay in range(2):
                for which in range(2):
                    o = ((lay * 6 + 3 * which + 1) * 8) * 2
                    q = (lay * 2 + which) * 16
                    dve.tensor_scalar(SCL[:, q:q + 16], MOD[:, o:o + 16], 1.0, None, ALU.add)

        def run(steps):
            for name in steps:
                if name == stop:
                    break

        @block.sync
        def _(sp):
            def steps():
                sp.dma_start(SILU, a_cT).then_inc(s_const, 16)
                sp.dma_start(VECS, a_vec).then_inc(s_const, 16)
                sp.dma_start(CSTS, a_cst).then_inc(s_const, 16)
                sp.dma_start(XC.rearrange("p (k t) -> p k t", k=KD), a_xT[:, :, 0:TC]).then_inc(s_const, 16)
                sp.dma_start(XL.rearrange("p (k t) -> p k t", k=KD), a_xT[:, :, TC:T]).then_inc(s_const, 16)
                ada_loads(sp)
                dense_loads(sp, "qk")
                sp.wait_ge(s_bar, over("norm_a0"))
                sp.dma_start(ROPE, a_rope).then_inc(s_load, 16)
                sp.dma_start(WV, a_wv).then_inc(s_load, 16)
                yield "norm_a0"
                yield "qk"
                dense_loads(sp, "wo")
                yield "wo"
                for h in range(2):
                    dense_loads(sp, f"up0{h}")
                    dense_loads(sp, f"dn0{h}")
                yield "ffn0"
                for name in ("lw", "la", "g"):
                    dense_loads(sp, name)
                dense_loads(sp, "v", spill_store(sp, "v", v_dram))
                dense_loads(sp, "r", spill_store(sp, "r", r_dram))
                dense_loads(sp, "k")
                sp.wait_ge(s_bar, over("scan_init"))
                scan_loads(sp)
                yield "scan"
                sp.wait_ge(s_bar, over("scan"))
                read_loads(sp)
                yield "read"
                dense_loads(sp, "ro")
                yield "ro"
                for h in range(2):
                    dense_loads(sp, f"up1{h}")
                    dense_loads(sp, f"dn1{h}")
                yield "ffn1"

            run(steps())
            sp.wait_ge(s_bar, over(stop))
            for f in range(2):
                o = f * 4
                sp.dma_start(out[:, o:o + 4, :], XL[:, o * TL:(o + 4) * TL].rearrange("p (k t) -> p k t", k=4)
                             ).then_inc(s_out, 16)
            sp.wait_ge(s_out, 32)

        @block.gpsimd
        def _(pool):
            def steps():
                pool.memset(NEG[:, 0:1], 0.0)
                pool.memset(NEG[:, 1:2], EPS)
                pool.memset(NEG[:, 2:3], GN_EPS)
                pool.sem_inc(s_kd, 1)
                for s in range(2):
                    pool.sem_inc(s_spd[s], 16)
                stage_over(pool, "start")
                stage_over(pool, "ada")
                stage_over(pool, "norm_a0")
                yield "norm_a0"
                stage_over(pool, "qk")
                stage_over(pool, "heads")
                for b in QS:
                    for q in b:
                        pool.memset(q, 0.0)
                pool.drain()
                att_pool(pool, lat)
                att_pool(pool, con)
                stage_over(pool, "attention")
                stage_over(pool, "wo")
                yield "wo"
                for b in UB:
                    for c in (0, TC + 1, T + 2):
                        pool.memset(b[:, c:c + 1], 0.0)
                stage_over(pool, "norm_f0")
                stage_over(pool, "ffn0")
                yield "ffn0"
                for c in (0, TC + 1, T + 2):
                    pool.memset(HP.rearrange("p (k t) -> p k t", k=KD)[:, :, c:c + 1], 0.0)
                stage_over(pool, "norm_a1")
                shift_pool(pool)
                for name in ("shift", "mix1", "lw", "mix4", "la", "mix5", "g", "mix3"):
                    stage_over(pool, name)
                stage_over(pool, "v")
                stage_over(pool, "mix0")
                for s in range(2):
                    pool.wait_ge(s_spd[s], 16 * 9)
                stage_over(pool, "r")
                stage_over(pool, "mix2")
                stage_over(pool, "k")
                for n in range(KD):
                    pool.wait_ge(s_qn, 11 + n)
                    pool.dma_start(k_dram[n], KF[:, n * T:(n + 1) * T]).then_inc(s_kst, 16)
                    pool.dma_start(n_dram[n], NF[:, n * T:(n + 1) * T]).then_inc(s_kst, 16)
                pool.wait_ge(s_kst, 32 * KD)
                stage_over(pool, "kk")
                yield "kk"
                for b in (BDB, BDK, BDA, BDR, AR):
                    pool.memset(b, 0.0)
                stage_over(pool, "scan_init")
                scan_pool(pool)
                stage_over(pool, "scan")
                yield "scan"
                read_pool(pool)
                stage_over(pool, "read")
                yield "read"
                stage_over(pool, "ro")
                yield "ro"
                for b in UB:
                    for c in (0, TC + 1, T + 2):
                        pool.memset(b[:, c:c + 1], 0.0)
                stage_over(pool, "norm_f1")
                stage_over(pool, "ffn1")
                yield "ffn1"
                stage_over(pool, "norm_end")

            run(steps())

        @block.scalar
        def _(act):
            def steps():
                act.sem_inc(s_pr, 2)
                act.sem_inc(s_otc, 2)
                act.sem_inc(s_hroot, 1)
                act.wait_ge(s_const, 80)
                act.activation(SILU, SILU, ACT.Silu).then_inc(s_silu, 1)
                stage_over(act, "start")
                stage_over(act, "ada")
                norm_act(act, "a0", 0, 0, ah_h)
                stage_over(act, "norm_a0")
                yield "norm_a0"
                dense_evac(act, "qk", lambda n, s, j, sl, ps: act.activation(QK[:, ds(n * T + sl[0], sl[1])], ps, ACT.Copy),
                           only=(0,))
                stage_over(act, "qk")
                qk_act(act)
                stage_over(act, "heads")
                att_act(act, lat)
                att_act(act, con)
                stage_over(act, "attention")
                stage_over(act, "wo")
                yield "wo"
                norm_act(act, "f0", 0, 1, fh_h)
                stage_over(act, "norm_f0")
                for h in range(2):
                    up_evac_act(act, 0, h, SLICES, h * FH)
                stage_over(act, "ffn0")
                yield "ffn0"
                norm_act(act, "a1", 1, 0, hp_h)
                stage_over(act, "norm_a1")
                stage_over(act, "shift")
                stage_over(act, "mix1")
                dense_evac(act, "lw", lambda n, s, j, sl, ps: act.activation(HW[:, sl[0]:sl[0] + sl[1]], ps, ACT.Tanh))
                stage_over(act, "lw")
                stage_over(act, "mix4")
                dense_evac(act, "la", lambda n, s, j, sl, ps: act.activation(HA[:, sl[0]:sl[0] + sl[1]], ps, ACT.Copy))
                stage_over(act, "la")
                stage_over(act, "mix5")
                dense_evac(act, "g", lambda n, s, j, sl, ps: act.activation(
                    HG[:, n * TL + sl[0] - TC:n * TL + sl[0] - TC + sl[1]], ps, ACT.Sigmoid))
                stage_over(act, "g")
                stage_over(act, "mix3")
                spill_act(act, "v", 0)
                stage_over(act, "v")
                stage_over(act, "mix0")
                spill_act(act, "r", 4)
                stage_over(act, "r")
                stage_over(act, "mix2")
                dense_evac(act, "k", lambda n, s, j, sl, ps: act.activation(KF[:, ds(n * T + sl[0], sl[1])], ps, ACT.Copy),
                           only=(0,))
                stage_over(act, "k")
                kk_act(act)
                stage_over(act, "kk")
                yield "kk"
                stage_over(act, "scan_init")
                scan_act(act)
                stage_over(act, "scan")
                yield "scan"
                read_act(act)
                stage_over(act, "read")
                yield "read"
                stage_over(act, "ro")
                yield "ro"
                norm_act(act, "f1", 1, 1, fh_h)
                stage_over(act, "norm_f1")
                for h in range(2):
                    up_evac_act(act, 1, h, LAT, (2 + h) * FH)
                stage_over(act, "ffn1")
                yield "ffn1"
                norm_act(act, "end", 0, 0, None)
                stage_over(act, "norm_end")

            run(steps())

        @block.tensor
        def _(pe):
            def steps():
                pe.sem_inc(s_sc, 4)
                pe.sem_inc(s_pv, 2)
                pe.sem_inc(s_ot, 2)
                pe.sem_inc(s_hms, 1)
                pe.sem_inc(s_vt, 1)
                pe.sem_inc(s_r3p, 1)
                stage_over(pe, "start")
                ada_pe(pe)
                stage_over(pe, "ada")
                norm_pe(pe, "a0")
                stage_over(pe, "norm_a0")
                yield "norm_a0"
                dense_products(pe, "qk", a_rhs)
                pe.wait_ge(s_load, 32)
                for t in range(T // P):
                    if t >= 2:
                        pe.wait_ge(s_vr, t - 1)
                    for k in range(KD):
                        mm = pe.matmul(PS[:, (6 + t % 2) * 512:(6 + t % 2) * 512 + HKV * DH],
                                       AH[:, k * T + t * P:k * T + (t + 1) * P], WV[:, k * 256:(k + 1) * 256],
                                       start=k == 0, stop=k == KD - 1)
                    mm.then_inc(s_v, 1)
                stage_over(pe, "qk")
                qk_pe(pe)
                stage_over(pe, "heads")
                att_pe(pe, lat)
                att_pe(pe, con)
                stage_over(pe, "attention")
                dense_products(pe, "wo", a_rhs)
                stage_over(pe, "wo")
                yield "wo"
                norm_pe(pe, "f0")
                stage_over(pe, "norm_f0")
                for h in range(2):
                    if h:
                        for s in range(2):
                            pe.wait_ge(s_read["dn00"][s], 5 * order["dn00"].j)
                    dense_products(pe, f"up0{h}", f_rhs)
                    pe.wait_ge(s_gd, h + 1)
                    dense_products(pe, f"dn0{h}", g_rhs)
                stage_over(pe, "ffn0")
                yield "ffn0"
                norm_pe(pe, "a1")
                for name in ("norm_a1", "shift", "mix1"):
                    stage_over(pe, name)
                for name, nxt in (("lw", "mix4"), ("la", "mix5"), ("g", "mix3"), ("v", "mix0"), ("r", "mix2"), ("k", None)):
                    dense_products(pe, name, m_rhs)
                    stage_over(pe, name)
                    if nxt:
                        stage_over(pe, nxt)
                kk_pe(pe)
                stage_over(pe, "kk")
                yield "kk"
                stage_over(pe, "scan_init")
                scan_pe(pe)
                stage_over(pe, "scan")
                yield "scan"
                read_pe(pe)
                stage_over(pe, "read")
                yield "read"
                dense_products(pe, "ro", lambda k, sl: YS[:, k * TL + sl[0] - TC:k * TL + sl[0] - TC + sl[1]])
                stage_over(pe, "ro")
                yield "ro"
                norm_pe(pe, "f1")
                stage_over(pe, "norm_f1")
                for h in range(2):
                    if h:
                        for s in range(2):
                            pe.wait_ge(s_read["dn10"][s], 5 * order["dn10"].j)
                    dense_products(pe, f"up1{h}", f_rhs)
                    pe.wait_ge(s_gd, 2 + h + 1)
                    dense_products(pe, f"dn1{h}", g_rhs)
                stage_over(pe, "ffn1")
                yield "ffn1"
                norm_pe(pe, "end")
                stage_over(pe, "norm_end")

            run(steps())

        @block.vector
        def _(dve):
            def steps():
                dve.sem_inc(s_os, 2)
                dve.sem_inc(s_qkd, 1)
                dve.sem_inc(s_cv[0], 1)
                dve.sem_inc(s_cv[1], 1)
                dve.sem_inc(s_hat, 1)
                dve.sem_inc(s_yc, 1)
                dve.sem_inc(s_St, 1)
                dve.sem_inc(s_r3v, 1)
                dve.sem_inc(s_r3r, 1)
                stage_over(dve, "start")
                dve.wait_ge(s_const, 80)
                ada_dve(dve)
                stage_over(dve, "ada")
                norm_dve(dve, "a0", ah_h)
                stage_over(dve, "norm_a0")
                yield "norm_a0"
                dense_evac(dve, "qk", lambda n, s, j, sl, ps: dve.tensor_copy(QK[:, ds(n * T + sl[0], sl[1])], ps),
                           only=(1,))
                for t in range(T // P):
                    dve.wait_ge(s_v, t + 1)
                    dve.tensor_copy(VT[:, t * 256:(t + 1) * 256], PS[:, (6 + t % 2) * 512:(6 + t % 2) * 512 + 256]
                                    ).then_inc(s_vr, 1)
                stage_over(dve, "qk")
                dve.wait_ge(s_load, 32)
                qk_dve(dve)
                dve.drain()
                for j in range(HKV):
                    for h in range(2):
                        src_ = QK[64 * (j % 2):64 * (j % 2) + 64, (8 + j // 2) * T:(9 + j // 2) * T]
                        dve.tensor_copy(KDUP[64 * h:64 * h + 64, j * T:(j + 1) * T], src_)
                stage_over(dve, "heads")
                att_dve(dve, lat)
                att_dve(dve, con)
                stage_over(dve, "attention")
                add_to_stream(dve, "wo", 0, 2)
                stage_over(dve, "wo")
                yield "wo"
                norm_dve(dve, "f0", fh_h)
                stage_over(dve, "norm_f0")
                for h in range(2):
                    up_evac_dve(dve, 0, h, SLICES, h * FH)
                    dve.drain().then_inc(s_gd, 1)
                    add_to_stream(dve, f"dn0{h}", 0, 5)
                    dve.drain()
                stage_over(dve, "ffn0")
                yield "ffn0"
                norm_dve(dve, "a1", hp_h)
                stage_over(dve, "norm_a1")
                shift_dve(dve)
                stage_over(dve, "shift")
                for m, name in ((1, "lw"), (4, "la"), (5, "g"), (3, "v"), (0, "r"), (2, "k")):
                    mix(dve, m)
                    stage_over(dve, f"mix{m}")
                    if name == "k":
                        dense_evac(dve, "k", lambda n, s, j, sl, ps: dve.tensor_copy(KF[:, ds(n * T + sl[0], sl[1])], ps),
                                   only=(1,))
                    stage_over(dve, name)
                kk_dve(dve)
                stage_over(dve, "kk")
                yield "kk"
                for b in (NB, AAK, ARB, ARK, TBD, GBD, YS):
                    dve.memset(b, 0.0)
                dve.memset(CM, 1.0)
                dve.drain()
                dve.memset(units(CM)[:, :, 0:1], 0.0)
                stage_over(dve, "scan_init")
                scan_dve(dve)
                stage_over(dve, "scan")
                yield "scan"
                read_dve(dve)
                stage_over(dve, "read")
                yield "read"
                add_to_stream(dve, "ro", 1, 2)
                stage_over(dve, "ro")
                yield "ro"
                norm_dve(dve, "f1", fh_h)
                stage_over(dve, "norm_f1")
                for h in range(2):
                    up_evac_dve(dve, 1, h, LAT, (2 + h) * FH)
                    dve.drain().then_inc(s_gd, 1)
                    add_to_stream(dve, f"dn1{h}", 1, 5)
                    dve.drain()
                stage_over(dve, "ffn1")
                yield "ffn1"
                norm_dve(dve, "end", None)
                stage_over(dve, "norm_end")

            run(steps())


STOP = "norm_end"


def constants():
    i = np.arange(P)
    c = np.zeros((P, NCST), np.float32)
    c[:, CST["mean1024"]:CST["mean1024"] + P] = 1.0 / D
    same = (i[:, None] // 64 == i[None, :] // 64).astype(np.float32)
    c[:, CST["mean64"]:CST["mean64"] + P] = same / DH
    c[:, CST["sum64"]:CST["sum64"] + P] = same
    swap = np.zeros((P, P), np.float32)
    swap[i[0::2] + 1, i[0::2]] = -1.0
    swap[i[0::2], i[0::2] + 1] = 1.0
    c[:, CST["swap"]:CST["swap"] + P] = swap
    c[:, CST["ident"]:CST["ident"] + P] = np.eye(P)
    a, b = np.meshgrid(np.arange(CH), np.arange(CH), indexing="ij")
    m = np.zeros((NLEV, 2, CH, CH), np.float32)
    for lev in range(6):
        w = 2 ** lev
        seam = (a // (2 * w) == b // (2 * w)) & (a // w % 2 == 0) & (b // w % 2 == 1)
        m[lev, 0], m[lev, 1] = seam, seam.T
    m[6, 0], m[6, 1] = b < a, b > a
    m[7, 0], m[7, 1] = b > a, b < a
    m[8, 0], m[8, 1] = b >= a, b <= a
    m[9, :] = a == b
    m = m.transpose(2, 0, 1, 3).reshape(CH, -1)
    c[:, CST["masks"]:] = np.concatenate([m, m], 0)
    grid_w, nf = 64, DH // 4
    inv = (np.float32(10000.0) ** (-np.arange(nf, dtype=np.float32) / np.float32(nf))).astype(np.float32)
    t = np.arange(TL)
    ang = np.concatenate([(t // grid_w).astype(np.float32)[:, None] * inv, (t % grid_w).astype(np.float32)[:, None] * inv], 1)
    rope = np.zeros((P, 2, T), np.float32)
    rope[:, 0, :TC] = 1.0
    rope[:, 0, TC:] = np.cos(ang).astype(np.float32).T[(i % DH) // 2]
    rope[:, 1, TC:] = np.sin(ang).astype(np.float32).T[(i % DH) // 2]
    return c, rope.reshape(P, 2 * T)


def tiles(w):
    k, n = w.shape
    return w.reshape(k // P, P, n // P, P).transpose(2, 1, 0, 3).reshape(n // P, P, k)


def feat(v):
    return v.reshape(-1, P).T


def layout(x, c, ctx, c_ctx, ada_w, ada_b, attn_w_qkv, attn_q_gain, attn_k_gain, attn_w_o,
           rwkv_mu, rwkv_w_r, rwkv_w_k, rwkv_w_v, rwkv_w_o, rwkv_decay_w0, rwkv_decay_w1, rwkv_decay_w2,
           rwkv_aaa_a0, rwkv_aaa_a1, rwkv_aaa_a2, rwkv_gate_g1, rwkv_gate_g2, rwkv_k_k, rwkv_k_a, rwkv_r_k,
           rwkv_gn_w, rwkv_gn_b, ffn_w_up, ffn_conv_w, ffn_conv_b, ffn_w_down, final_gain):
    cst, rope = constants()
    xx = np.concatenate([ctx[0], x[0]], 0)
    xT = xx.T.reshape(KD, P, T).transpose(1, 0, 2)
    cT = np.stack([c[0], c_ctx], 0).reshape(2, KD, P).transpose(2, 1, 0).reshape(P, 16)
    gains = np.stack([np.concatenate([g, g]) for g in [attn_q_gain[0]] * 8 + [attn_k_gain[0]] * 2], 1)
    conv = np.concatenate([ffn_conv_w, ffn_conv_b[:, None]], 1)
    conv = conv.reshape(2, 4, 2, FJ, P).transpose(4, 0, 3, 2, 1).reshape(P, -1)
    vecs = np.concatenate([feat(ada_b), gains, feat(rwkv_mu[0]), feat(rwkv_decay_w0[0]), feat(rwkv_aaa_a0[0]),
                           feat(rwkv_k_k[0]), feat(rwkv_k_a[0]), feat(rwkv_r_k[0]), feat(rwkv_gn_w[0]),
                           feat(rwkv_gn_b[0]), feat(final_gain), conv], 1)
    adaw = ada_w.reshape(2, KD, P, 12, 512).transpose(0, 3, 2, 1, 4).reshape(24, P, KD * 512)
    wqk = tiles(attn_w_qkv[0][:, :Q_COLS])
    wv = attn_w_qkv[0][:, Q_COLS:].reshape(KD, P, HKV * DH).transpose(1, 0, 2).reshape(P, -1)
    wup = np.stack([tiles(w).reshape(2, 2, FH, P, D).transpose(1, 2, 0, 3, 4).reshape(2, 2 * FH, P, D) for w in ffn_w_up])
    wdn = np.stack([np.stack([tiles(w[h * FH * P:(h + 1) * FH * P]) for h in range(2)]) for w in ffn_w_down])
    lora1 = np.stack([tiles(np.concatenate(list(w[0]), 1))[0] for w in (rwkv_decay_w1, rwkv_aaa_a1)])
    g1 = tiles(np.pad(rwkv_gate_g1[0], ((0, 0), (0, 96))))
    g2 = tiles(np.pad(rwkv_gate_g2[0], ((0, 96), (0, 0))))
    lora2 = np.zeros((KD, P, 4, P), np.float32)
    for n, w in enumerate((rwkv_decay_w2[0], rwkv_aaa_a2[0])):
        for d in range(2):
            lora2[:, 64 * d:64 * d + 64, 2 * n + d] = w[d].reshape(64, KD, P).transpose(1, 0, 2)
    return [xT, cT, vecs, cst, rope, adaw, wqk, wv, tiles(attn_w_o[0]), wup, wdn, lora1, g1,
            tiles(rwkv_w_k[0]), tiles(rwkv_w_v[0]), tiles(rwkv_w_r[0]), tiles(rwkv_w_o[0]),
            lora2.reshape(KD, P, 4 * P), g2]


Q_COLS = H * DH + HKV * DH


def kernel(**inputs):
    import numpy as _np
    import concourse.bacc as _bacc
    from concourse import mybir as _mybir
    from concourse.bass_utils import run_bass_kernel_spmd as _run

    nc = _bacc.Bacc("TRN2", target_bir_lowering=False, num_devices=1)
    arrays, args = {}, []
    for n, a in enumerate(layout(**{k: _np.asarray(v) for k, v in inputs.items()})):
        a = _np.ascontiguousarray(a)
        arrays[f"in_{n}_dram"] = a
        args.append(nc.dram_tensor(f"in_{n}_dram", a.shape, _mybir.dt.from_np(a.dtype), kind="ExternalInput").ap())
    args.append(nc.dram_tensor("out_dram", (P, KD, TL), F32, kind="ExternalOutput").ap())
    program(nc, STOP, *args)
    r = _run(nc, [arrays], core_ids=[0])
    y = r.results[0]["out_dram"]
    return _np.ascontiguousarray(y.transpose(2, 1, 0).reshape(1, TL, D))
```

```python
from contextlib import ExitStack

import concourse.bass as bass
from concourse import mybir
import numpy as np

F32 = mybir.dt.float32
ALU = mybir.AluOpType
ACT = mybir.ActivationFunctionType
AX_X = mybir.AxisListType.X
ds = bass.ds

P = 128
D = 1024
KD = D // P
TC, TL = 256, 1024
T = TC + TL
H, HKV, DH = 16, 4, 64
FF = 2816
FJ = FF // P
FH = FJ // 2
CH = 64
NU = 8
GT = 4 * CH
NGR = T // GT
NPAIR = H // 2
LEVELS = [2, 4, 8, 16, 32]
EPS, GN_EPS = 1e-6, 64e-5
DECAY = float(np.exp(-0.5))
NLEV = 11

SLICES = [(0, TC, 1), (TC, 512, 0), (TC + 512, 512, 0)]
LAT = SLICES[1:]
PADW = T + 4


def padded(t0):
    return t0 + 1 if t0 < TC else t0 + 2


VEC = {}
_at = 0
for _name, _n in (("ada_b", 96), ("qk_gain", 10), ("mu", 48), ("w0", 16), ("a0", 16), ("k_k", 8), ("k_a", 8),
                  ("r_k", 8), ("gn_w", 8), ("gn_b", 8), ("final_gain", 8), ("conv", 2 * FJ * 2 * 4)):
    VEC[_name] = _at
    _at += _n
NVEC = _at
CST = {"mean1024": 0, "mean64": 128, "sum64": 256, "swap": 384, "ident": 512, "masks": 640}
NCST = 640 + NLEV * 2 * CH


class Dense:

    def __init__(self, n, k, slices, before):
        self.n, self.k, self.slices, self.j = n, k, slices, len(slices)
        self.slots = min(n, 2)
        self.loops = n // self.slots
        self.w0 = [0, 0] if before is None else list(before.w1)
        self.p0 = [0, 0] if before is None else list(before.p1)
        self.w1 = [w + (self.loops if s < self.slots else 0) for s, w in enumerate(self.w0)]
        self.p1 = [p + (self.loops * self.j if s < self.slots else 0) for s, p in enumerate(self.p0)]


def program(nc, stop, a_xT, a_cT, a_vec, a_cst, a_rope, a_adaw, a_wqk, a_wv, a_wo, a_wup, a_wdn,
            a_lora1, a_g1, a_rk, a_rv, a_rr, a_ro, a_lora2, a_g2, out):
    order = {}
    last = None

    def dense(name, n, k, slices):
        nonlocal last
        last = order[name] = Dense(n, k, slices, last)

    dense("qk", 10, 8, SLICES)
    dense("wo", 8, 8, SLICES)
    for half in range(2):
        dense(f"up0{half}", 2 * FH, 8, SLICES)
        dense(f"dn0{half}", 8, FH, SLICES)
    dense("lw", 1, 8, SLICES)
    dense("la", 1, 8, SLICES)
    dense("g", 2, 8, LAT)
    dense("v", 8, 8, SLICES)
    dense("r", 8, 8, LAT)
    dense("k", 8, 8, SLICES)
    dense("ro", 8, 8, LAT)
    for half in range(2):
        dense(f"up1{half}", 2 * FH, 8, LAT)
        dense(f"dn1{half}", 8, FH, LAT)
    src = {"qk": a_wqk, "wo": a_wo, "lw": a_lora1[0:1], "la": a_lora1[1:2], "k": a_rk, "v": a_rv, "r": a_rr,
           "g": a_g1, "ro": a_ro}
    for lay in range(2):
        for half in range(2):
            src[f"up{lay}{half}"] = a_wup[lay, half]
            src[f"dn{lay}{half}"] = a_wdn[lay, half]

    k_dram = nc.dram_tensor("k_scratch", (KD, P, T), F32, kind="Internal").ap()
    n_dram = nc.dram_tensor("kk_scratch", (KD, P, T), F32, kind="Internal").ap()
    v_dram = nc.dram_tensor("v_scratch", (KD, P, T), F32, kind="Internal").ap()
    r_dram = nc.dram_tensor("r_scratch", (KD, P, T), F32, kind="Internal").ap()

    with ExitStack() as ctx:
        SB = ctx.enter_context(nc.sbuf_tensor("SB", [P, 52900], F32))
        PS = ctx.enter_context(nc.psum_tensor("PS", [P, 4096], F32))
        top = [0]

        def take(n):
            top[0] += n
            assert top[0] <= 52900, top[0]
            return SB[:, top[0] - n:top[0]]

        def sem(name):
            return ctx.enter_context(nc.semaphore(name))

        def bank(b, n=1):
            return PS[:, b * 512:(b + n) * 512]

        XL = take(KD * TL)
        MOD = take(192)
        SCL = take(64)
        VECS = take(NVEC)
        CSTS = take(NCST)
        SILU = take(16)
        DER = take(48)
        WS = [take(FH * P) for _ in range(2)]
        KA = take(4)
        NEG = take(16)
        XC = take(KD * TC)
        base = top[0]

        def xs(f, sl):
            t0, w, stream = sl
            if stream:
                return XC[:, ds(f * TC, w)]
            return XL[:, ds(f * TL + (t0 - TC), w)]

        def cst(name, rows=P, n=P):
            return CSTS[0:rows, CST[name]:CST[name] + n]

        def mask(lev):
            o = CST["masks"] + lev * 2 * CH
            return CSTS[:, o:o + 2 * CH]

        def vec(name, i=0, n=1):
            return VECS[:, ds(VEC[name] + i, n)]

        def mod(layer, comp, f, stream):
            return MOD[:, ds(((layer * 6 + comp) * 8 + f) * 2 + stream, 1)]

        def scl(layer, norm, f, stream):
            return SCL[:, ds(((layer * 2 + norm) * 8 + f) * 2 + stream, 1)]

        s_const = sem("const_loaded")
        s_adaw = [sem(f"ada_w_loaded{i}") for i in range(2)]
        s_adap = sem("ada_product")
        s_silu = sem("silu_c")
        s_bar = sem("stage_over")
        s_passed = sem("wait_passed")
        s_w = [sem(f"weights_loaded{i}") for i in range(2)]
        s_ps = [sem(f"tile_summed{i}") for i in range(2)]
        s_read = {name: [sem(f"tile_read_{name}_{i}") for i in range(2)] for name in order}
        s_sq = sem("squares_ready")
        s_ms = sem("mean_square_ready")
        s_root = sem("root_ready")
        s_scaled = sem("scaled_ready")
        s_hsq = sem("head_squares_ready")
        s_hms = sem("head_sums_ready")
        s_hroot = sem("head_roots_ready")
        s_rd = sem("rms_done_reading")
        s_load = sem("stage_input_loaded")
        s_v = sem("v_tile_summed")
        s_vr = sem("v_tile_read")
        s_qn = sem("qk_normed")
        s_rot = sem("qk_swapped")
        s_cosd = sem("cos_part_ready")
        s_qkd = sem("qk_roped")
        s_qs = sem("q_block_copied")
        s_qsr = sem("q_block_used")
        s_sc = sem("scores_ready")
        s_mx = sem("max_ready")
        s_pr = sem("probs_ready")
        s_pt = sem("probs_turned")
        s_pta = sem("probs_even_copied")
        s_ptd = sem("probs_odd_copied")
        s_pv = sem("values_summed")
        s_os = sem("head_out_scaled")
        s_ot = sem("head_out_turned")
        s_otc = sem("head_out_copied")
        s_cv = [sem(f"conv_done{i}") for i in range(2)]
        s_sg = sem("gate_silu_ready")
        s_gd = sem("gated_ready")
        s_mix = sem("mix_ready")
        s_sp = sem("spill_ready")
        s_kst = sem("k_stored")
        s_spd = [sem(f"spill_stored{i}") for i in range(2)]
        s_kin = sem("group_inputs_loaded")
        s_rin = sem("group_r_loaded")
        s_lz = sem("lora_summed")
        s_th = sem("tanh_ready")
        s_cum = sem("decay_sums_ready")
        s_xp = sem("decay_powers_ready")
        s_kd = sem("k_and_b_ready")
        s_hat = sem("hats_ready")
        s_vt = sem("v_turned")
        s_vc = sem("v_stacked")
        s_s1 = sem("products_ready")
        s_m1 = sem("products_masked")
        s_tr = sem("hat_turned")
        s_trc = sem("hat_turned_copied")
        s_tt = sem("turned_inverse_grown")
        s_tz = sem("turned_join_ready")
        s_z = sem("join_inner_ready")
        s_zc = sem("join_inner_masked")
        s_gz = sem("join_outer_ready")
        s_g = sem("inverse_grown")
        s_W = sem("w_summed")
        s_Wc = sem("w_copied")
        s_U = sem("u_summed")
        s_Uc = sem("u_copied")
        s_D = sem("state_delta_ready")
        s_St = sem("state_updated")
        s_y = sem("y_ready")
        s_yc = sem("y_added")
        s_out = sem("out_stored")
        s_r3 = sem("readout_loaded")
        s_r3c = sem("readout_copied")
        s_r3p = sem("readout_product")
        s_r3a = sem("readout_act")
        s_r3v = sem("readout_vector")
        s_r3r = sem("readout_inputs_used")
        block = ctx.enter_context(nc.Block())

        STAGES = ["start", "ada", "norm_a0", "qk", "heads", "attention", "wo", "norm_f0", "ffn0", "norm_a1", "shift",
                  "mix1", "lw", "mix4", "la", "mix5", "g", "mix3", "v", "mix0", "r", "mix2", "k", "kk", "scan_init",
                  "scan", "read", "ro", "norm_f1", "ffn1", "norm_end"]

        def over(name):
            return 4 * (STAGES.index(name) + 1)

        def stage_over(eng, name):
            eng.drain().then_inc(s_bar, 1)
            eng.wait_ge(s_bar, over(name))

        def apart(eng):
            eng.sem_inc(s_passed, 1)

        def dense_loads(sp, name, store=None):
            d = order[name]
            w = src[name]

            def load(i, s):
                sp.dma_start(WS[s][:, 0:d.k * P], w[d.slots * i + s] if isinstance(i, int) else
                             w[ds(d.slots * i + s, 1)].rearrange("o p q -> (o p) q")).then_inc(s_w[s], 16)

            for s in range(d.slots):
                if d.w0[s] > 0:
                    sp.wait_ge(s_ps[s], d.p0[s])
                load(0, s)
            if d.loops > 1:
                with sp.Fori(1, d.loops) as i:
                    for s in range(d.slots):
                        sp.wait_ge(s_ps[s], i * d.j + d.p0[s])
                        load(i, s)
                        if store:
                            store(i - 1, s)
                for s in range(d.slots if store else 0):
                    store(d.loops - 1, s)

        def dense_products(pe, name, rhs):
            d = order[name]

            def body(i):
                for s in range(d.slots):
                    pe.wait_ge(s_w[s], (i + d.w0[s] + 1) * 16)
                    for j, sl in enumerate(d.slices):
                        pe.wait_ge(s_read[name][s], i * d.j + (j + 1))
                        o = PS[:, (3 * s + j) * 512:(3 * s + j) * 512 + sl[1]]
                        for k in range(d.k):
                            mm = pe.matmul(o, WS[s][:, k * P:(k + 1) * P], rhs(k, sl), start=k == 0, stop=k == d.k - 1)
                        mm.then_inc(s_ps[s], 1)

            if d.loops > 1:
                with pe.Fori(0, d.loops) as i:
                    body(i)
            else:
                body(0)

        def dense_evac(eng, name, read, before=None, after=None, only=(0, 1)):
            d = order[name]
            for s in [x for x in only if x < d.slots]:
                eng.sem_inc(s_read[name][s], d.j)

            def body(i):
                for s in [x for x in only if x < d.slots]:
                    if before:
                        before(i, s)
                    for j, sl in enumerate(d.slices):
                        eng.wait_ge(s_ps[s], i * d.j + (d.p0[s] + j + 1))
                        o = PS[:, (3 * s + j) * 512:(3 * s + j) * 512 + sl[1]]
                        read(i * d.slots + s, s, j, sl, o).then_inc(s_read[name][s], 1)
                    if after:
                        after(i, s)

            if d.loops > 1:
                with eng.Fori(0, d.loops) as i:
                    body(i)
            else:
                body(0)

        norms = {}
        nn = 0
        for key, sls in (("a0", SLICES), ("f0", SLICES), ("a1", SLICES), ("f1", LAT), ("end", LAT)):
            norms[key] = (nn, sls)
            nn += len(sls)

        def norm_act(act, key, layer, which, hs):
            n0, sls = norms[key]
            sq, rr = norm_tmp[key]
            for q, sl in enumerate(sls):
                n = n0 + q
                for f in range(KD):
                    m = n * KD + f
                    if m >= 2:
                        act.wait_ge(s_rd, m - 1)
                    act.activation(sq[f % 2][:, 0:sl[1]], xs(f, sl), ACT.Square).then_inc(s_sq, 1)
                act.wait_ge(s_ms, n + 1)
                if q:
                    act.wait_ge(s_scaled, (n - 1) * KD + KD)
                act.activation(rr[:, 0:sl[1]], PS[:, 6 * 512:6 * 512 + sl[1]], ACT.Sqrt, bias=NEG[:, 1:2]
                               ).then_inc(s_root, 1)
                if hs is not None:
                    for f in range(KD):
                        act.wait_ge(s_scaled, n * KD + f + 1)
                        act.activation(hs(f, sl), hs(f, sl), ACT.Identity, bias=mod(layer, 3 * which, f, sl[2]),
                                       scale=scl(layer, which, f, sl[2]))

        def norm_pe(pe, key):
            n0, sls = norms[key]
            sq, _ = norm_tmp[key]
            for q, sl in enumerate(sls):
                n = n0 + q
                if q:
                    pe.wait_ge(s_root, n)
                for f in range(KD):
                    pe.wait_ge(s_sq, n * KD + f + 1)
                    mm = pe.matmul(PS[:, 6 * 512:6 * 512 + sl[1]], cst("mean1024"), sq[f % 2][:, 0:sl[1]],
                                   start=f == 0, stop=f == KD - 1)
                    mm.then_inc(s_rd, 1)
                pe.drain().then_inc(s_ms, 1)

        def norm_dve(dve, key, hs):
            n0, sls = norms[key]
            _, rr = norm_tmp[key]
            for q, sl in enumerate(sls):
                n = n0 + q
                dve.wait_ge(s_root, n + 1)
                r = rr[:, 0:sl[1]]
                dve.reciprocal(r, r)
                dve.drain()
                for f in range(KD):
                    if hs is None:
                        dve.scalar_tensor_tensor(xs(f, sl), xs(f, sl), vec("final_gain", f), r, ALU.mult, ALU.mult
                                                 ).then_inc(s_scaled, 1)
                    else:
                        dve.tensor_tensor(hs(f, sl), xs(f, sl), r, ALU.mult).then_inc(s_scaled, 1)

        top[0] = base
        AH = take(KD * T)
        QK = take(10 * T)
        VT = take(10 * HKV * DH)
        KDUP = take(HKV * T)
        ROPE = take(2 * T)
        at_tmp = top[0]
        WV = take(KD * HKV * DH)
        sq_at = top[0]
        top[0] = at_tmp
        SQQ = take(T)
        T1 = take(T)
        top[0] = base + KD * T + 10 * T + 10 * HKV * DH + HKV * T
        PB = [take(T) for _ in range(2)]
        PTB = take(T)
        QS = [[take(P) for _ in range(2)] for _ in range(2)]
        OS = [take(P) for _ in range(2)]
        MXN = take(4)
        RSUM = take(4)
        RINV = take(4)
        att_top = top[0]
        SQ_att = [None, None]
        SQa = [KDUP[:, 0:512], KDUP[:, 512:1024]]
        RRa = KDUP[:, 1024:1536]
        top[0] = base
        FHB = take(KD * T)
        G = take(FH * T)
        UB = [take(PADW) for _ in range(2)]
        CB = [take(PADW) for _ in range(2)]
        SQf = [take(512) for _ in range(2)]
        RRf = take(512)
        HW = SB[:, base - KD * TC:base - KD * TC + T]
        top[0] = base
        HP = take(KD * PADW)
        XX = take(KD * PADW)
        MX1 = take(KD * PADW)
        HA = take(T)
        HG = take(2 * TL)
        STG = [take(T) for _ in range(2)]
        SQr = [STG[0][:, 0:512], STG[0][:, 512:1024]]
        RRr = STG[1][:, 0:512]
        KF = HP[:, 0:KD * T]
        NF = XX[:, 0:KD * T]
        top[0] = base
        YS = take(KD * TL)
        KIN = take(4 * 2 * GT)
        W2 = take(4 * P)
        TZ = take(2 * GT)
        TA = take(2 * GT)
        F1 = take(GT)
        IN = take(2 * GT)
        EX = take(2 * GT)
        XN = take(2 * GT)
        TK = take(2 * GT)
        TB = take(2 * GT)
        BH = take(4 * GT)
        BK = take(4 * GT)
        PCS = [take(NU) for _ in range(2)]
        AR = [take(2 * 2 * GT) for _ in range(2)]
        BT = [take(2 * 2 * GT) for _ in range(2)]
        AAK, ARB, ARK, GS = ([take(2 * GT) for _ in range(2)] for _ in range(4))
        VST = [take(4 * GT) for _ in range(2)]
        NB = take(4 * GT)
        GTS = take(2 * GT)
        ZS = take(4 * GT)
        MST = take(P)
        MP = take(P)
        MS = [take(2 * P) for _ in range(2)]
        WSB = take(2 * P)
        USB = take(2 * P)
        CM = STG[0][:, 0:GT]
        assert top[0] <= base + 3 * KD * PADW, top[0] - base - 3 * KD * PADW
        top[0] = base + KD * TL
        RIN = take(3 * TL)
        RW2 = take(2 * P)
        RG2 = take(2 * P)
        YC = take(TL)
        YT = take(TL)
        SQY = take(TL)
        RTY = take(TL)
        RTA = take(2 * TL)
        RBY = take(TL)
        BVY = take(TL)

        norm_tmp = {"a0": (SQa, RRa), "f0": (SQf, RRf), "a1": (SQr, RRr), "f1": (SQf, RRf), "end": (SQf, RRf)}

        def a_rhs(k, sl):
            return AH[:, k * T + sl[0]:k * T + sl[0] + sl[1]]

        def f_rhs(k, sl):
            return FHB[:, k * T + sl[0]:k * T + sl[0] + sl[1]]

        def g_rhs(k, sl):
            return G[:, k * T + sl[0]:k * T + sl[0] + sl[1]]

        def m_rhs(k, sl):
            return MX1[:, k * PADW + padded(sl[0]):k * PADW + padded(sl[0]) + sl[1]]

        def ah_h(f, sl):
            return AH[:, f * T + sl[0]:f * T + sl[0] + sl[1]]

        def fh_h(f, sl):
            return FHB[:, f * T + sl[0]:f * T + sl[0] + sl[1]]

        def hp_h(f, sl):
            return HP[:, f * PADW + padded(sl[0]):f * PADW + padded(sl[0]) + sl[1]]

        lat = dict(nk=10, q0=TC, per=4, it0=0, its=NPAIR * 4, even=2, odd=1, g0=0, e0=0, o0=0)
        con = dict(nk=2, q0=0, per=1, it0=NPAIR * 4, its=NPAIR, even=1, odd=0, g0=NPAIR * 16 * 3, e0=NPAIR * 16 * 2,
                   o0=NPAIR * 16)

        def att_pieces(a):
            return [(c, min(512, a["nk"] * P - c)) for c in range(0, a["nk"] * P, 512)]

        def att_groups(a):
            return [list(range(g, min(g + 4, a["nk"]))) for g in range(0, a["nk"], 4)]

        def att_cols(a, i, tt):
            if a["per"] == 1:
                return i, a["q0"] + tt * P
            return i // a["per"], (i % a["per"]) * (2 * P) + (a["q0"] + tt * P)

        def att_ahead(a, i, u, n):
            return (i, u + n) if u + n < 4 else (i + 1, u + n - 4)

        def att_steps(eng, a, body):
            with eng.Fori(0, a["its"] - 1) as i:
                for u in range(4):
                    body(i, u, False)
            for u in range(4):
                body(a["its"] - 1, u, True)

        def att_pe(pe, a):
            pieces, groups = att_pieces(a), att_groups(a)
            ng = len(groups)

            def scores(i, u, piece):
                tt, hh = u // 2, u % 2
                hp, _ = att_cols(a, i, tt)
                if piece == 0:
                    pe.wait_ge(s_qs, (i + a["it0"]) * 2 + tt + 1)
                    pe.wait_ge(s_pr, (i + a["it0"]) * 4 + u + 1)
                c, w = pieces[piece]
                mm = pe.matmul(PS[:, 1536 * (u % 2) + c:1536 * (u % 2) + c + w], QS[tt][hh],
                               KDUP[:, ds((hp // 2) * T + c, w)], start=True, stop=True)
                if piece == len(pieces) - 1:
                    mm.then_inc(s_sc, 1)

            def unit(i, u, last):
                tt, hh = u // 2, u % 2
                n = (i + a["it0"]) * 4 + u
                b = (i + a["it0"]) * 2 + tt
                hp, _ = att_cols(a, i, tt)
                nxt = None if last and u >= 2 else att_ahead(a, i, u, 2)
                left = list(range(len(pieces))) if nxt else []
                pe.wait_ge(s_pr, n + 3)
                for g, tiles in enumerate(groups):
                    if g == 1:
                        pe.wait_ge(s_pta, (i * 4 + u) * a["even"] + a["e0"] + 1)
                    if g == 2:
                        pe.wait_ge(s_ptd, (i * 4 + u) * a["odd"] + a["o0"] + 1)
                    for x, kt in enumerate(tiles):
                        o = 6 * 512 + x * P
                        mm = pe.transpose(PS[:, o:o + P], PB[u % 2][:, kt * P:(kt + 1) * P], cst("ident"))
                    mm.then_inc(s_pt, 1)
                    if left:
                        scores(*nxt, left.pop(0))
                while left:
                    scores(*nxt, left.pop(0))
                pe.wait_ge(s_os, n + 2)
                pe.wait_ge(s_otc, b + 2)
                pe.wait_ge(s_pta, (i * 4 + u) * a["even"] + a["e0"] + a["even"])
                if a["odd"]:
                    pe.wait_ge(s_ptd, (i * 4 + u) * a["odd"] + a["o0"] + a["odd"])
                o = 7 * 512
                for kt in range(a["nk"]):
                    mm = pe.matmul(PS[:, o:o + DH], PTB[:, kt * P:(kt + 1) * P],
                                   VT[:, ds((hp // 2) * DH + kt * HKV * DH, DH)], start=kt == 0, stop=kt == a["nk"] - 1)
                mm.then_inc(s_pv, 1)
                if hh == 1:
                    pe.wait_ge(s_os, n + 3)
                    o = 7 * 512 + 256
                    pe.transpose(PS[:, o:o + P], OS[tt], cst("ident")).then_inc(s_ot, 1)

            for u in range(2):
                for p in range(len(pieces)):
                    scores(0, u, p)
            att_steps(pe, a, unit)

        def att_pool(pool, a):
            with pool.Fori(0, a["its"]) as i:
                for tt in range(2):
                    hp, t0 = att_cols(a, i, tt)
                    pool.wait_ge(s_sc, (i + a["it0"]) * 4 + 2 * tt + 2)
                    for hh in range(2):
                        i_ = pool.tensor_copy(QS[tt][hh][64 * hh:64 * hh + 64, :],
                                              QK[64 * hh:64 * hh + 64, ds(hp * T + t0, P)])
                    i_.then_inc(s_qs, 1)

        def att_dve(dve, a):
            groups = att_groups(a)

            def row_max(i, u):
                dve.wait_ge(s_sc, (i + a["it0"]) * 4 + u + 5)
                dve.tensor_reduce(MXN[:, u:u + 1], PS[:, 1536 * (u % 2):1536 * (u % 2) + a["nk"] * P], AX_X, ALU.max,
                                  negate=True).then_inc(s_mx, 1)

            def unit(i, u, last):
                tt, hh = u // 2, u % 2
                n = (i + a["it0"]) * 4 + u
                if not (last and u == 3):
                    row_max(*att_ahead(a, i, u, 1))
                for g in range(1, len(groups), 2):
                    w = len(groups[g]) * P
                    dve.wait_ge(s_pt, (i * 4 + u) * len(groups) + a["g0"] + g + 1)
                    dve.wait_ge(s_pv, n + 2)
                    dve.tensor_copy(PTB[:, groups[g][0] * P:groups[g][0] * P + w],
                                    PS[:, 6 * 512:6 * 512 + w]).then_inc(s_ptd, 1)
                dve.wait_ge(s_pr, n + 3)
                dve.reciprocal(RINV[:, u:u + 1], RSUM[:, u:u + 1])
                dve.drain()
                dve.wait_ge(s_pv, n + 3)
                if hh == 0:
                    dve.wait_ge(s_ot, (i + a["it0"]) * 2 + tt + 1)
                o = 7 * 512
                dve.tensor_scalar(OS[tt][:, hh * DH:(hh + 1) * DH], PS[:, o:o + DH], RINV[:, u:u + 1], None, ALU.mult
                                  ).then_inc(s_os, 1)

            row_max(0, 0)
            att_steps(dve, a, unit)

        def att_act(act, a):
            groups = att_groups(a)

            def probs(i, u):
                act.wait_ge(s_mx, (i + a["it0"]) * 4 + u + 1)
                act.wait_ge(s_pv, (i + a["it0"]) * 4 + u + 1)
                act.activation(PB[u % 2][:, 0:a["nk"] * P], PS[:, 1536 * (u % 2):1536 * (u % 2) + a["nk"] * P],
                               ACT.Exp, bias=MXN[:, u:u + 1], accum_out=RSUM[:, u:u + 1]).then_inc(s_pr, 1)

            def unit(i, u, last):
                tt, hh = u // 2, u % 2
                n = (i + a["it0"]) * 4 + u
                if not (last and u == 3):
                    probs(*att_ahead(a, i, u, 1))
                for g in range(0, len(groups), 2):
                    w = len(groups[g]) * P
                    act.wait_ge(s_pt, (i * 4 + u) * len(groups) + a["g0"] + g + 1)
                    act.wait_ge(s_pv, n + 2)
                    act.activation(PTB[:, groups[g][0] * P:groups[g][0] * P + w], PS[:, 6 * 512:6 * 512 + w],
                                   ACT.Copy).then_inc(s_pta, 1)
                if hh == 1:
                    hp, t0 = att_cols(a, i, tt)
                    act.wait_ge(s_ot, (i + a["it0"]) * 2 + tt + 3)
                    o = 7 * 512 + 256
                    act.activation(AH[:, ds(hp * T + t0, P)], PS[:, o:o + P], ACT.Copy).then_inc(s_otc, 1)

            probs(0, 0)
            att_steps(act, a, unit)

        PIECES = [(0, 512), (512, 512), (1024, 256)]

        def qk_pe(pe):
            with pe.Fori(0, 10) as n:
                pe.wait_ge(s_hsq, n + 1)
                pe.wait_ge(s_hroot, n + 1)
                for c, w in PIECES:
                    mm = pe.matmul(PS[:, c:c + w], cst("mean64"), SQQ[:, c:c + w], start=True, stop=True)
                mm.then_inc(s_hms, 1)
                pe.wait_ge(s_qn, n + 1)
                pe.wait_ge(s_qkd, n + 1)
                for c, w in PIECES:
                    mm = pe.matmul(PS[:, 1536 + c:1536 + c + w], cst("swap"), QK[:, ds(n * T + c, w)], start=True,
                                   stop=True)
                mm.then_inc(s_rot, 1)

        def qk_act(act):
            with act.Fori(0, 10) as n:
                act.wait_ge(s_hms, n + 1)
                act.activation(SQQ, QK[:, ds(n * T, T)], ACT.Square).then_inc(s_hsq, 1)
                act.wait_ge(s_hms, n + 2)
                act.wait_ge(s_qkd, n + 1)
                act.activation(T1, PS[:, 0:T], ACT.Sqrt, bias=NEG[:, 1:2]).then_inc(s_hroot, 1)

        def qk_dve(dve):
            with dve.Fori(0, 10) as n:
                q = QK[:, ds(n * T, T)]
                dve.wait_ge(s_hroot, n + 2)
                dve.reciprocal(T1, T1)
                dve.drain()
                dve.scalar_tensor_tensor(q, q, vec("qk_gain", n), T1, ALU.mult, ALU.mult).then_inc(s_qn, 1)
                dve.drain()
                dve.tensor_tensor(T1, q, ROPE[:, 0:T], ALU.mult)
                dve.drain()
                dve.wait_ge(s_rot, n + 1)
                dve.tensor_tensor(q, PS[:, 1536:1536 + T], ROPE[:, T:2 * T], ALU.mult)
                dve.drain()
                dve.tensor_tensor(q, q, T1, ALU.add).then_inc(s_qkd, 1)

        def up_evac_act(act, lay, half, slices, q0):
            name = f"up{lay}{half}"
            lo = padded(slices[0][0])
            w = padded(T) - lo

            def before(i, s):
                act.wait_ge(s_cv[s], i + q0 + 1)

            def read(n, s, j, sl, ps):
                return act.activation(UB[s][:, padded(sl[0]):padded(sl[0]) + sl[1]], ps, ACT.Copy)

            def after(i, s):
                if s == 1:
                    act.wait_ge(s_cv[0], i + q0 + 2)
                    act.activation(CB[0][:, lo:lo + w], CB[0][:, lo:lo + w], ACT.Silu).then_inc(s_sg, 1)

            dense_evac(act, name, read, before, after)

        def up_evac_dve(dve, lay, half, slices, q0):
            name = f"up{lay}{half}"
            d = order[name]
            lo = padded(slices[0][0])
            w = padded(T) - lo
            with dve.Fori(0, d.loops) as i:
                for s in range(2):
                    dve.wait_ge(s_read[name][s], i * d.j + 2 * d.j)
                    cv = VEC["conv"] + ((lay * FJ + half * FH) * 2 + s) * 4
                    cw = [VECS[:, ds(i * 8 + cv + x, 1)] for x in range(4)]
                    u, c = UB[s], CB[s][:, lo:lo + w]
                    dve.tensor_scalar(c, u[:, lo:lo + w], cw[1], cw[3], ALU.mult, ALU.add)
                    dve.drain()
                    dve.scalar_tensor_tensor(c, u[:, lo - 1:lo - 1 + w], cw[0], c, ALU.mult, ALU.add)
                    dve.drain()
                    dve.scalar_tensor_tensor(c, u[:, lo + 1:lo + 1 + w], cw[2], c, ALU.mult, ALU.add
                                             ).then_inc(s_cv[s], 1)
                dve.drain()
                dve.wait_ge(s_sg, i + q0 + 1)
                for t0, n in ([(0, TC)] if slices[0][0] == 0 else []) + [(TC, TL)]:
                    dve.tensor_tensor(G[:, ds(i * T + t0, n)], CB[0][:, padded(t0):padded(t0) + n],
                                      CB[1][:, padded(t0):padded(t0) + n], ALU.mult)
                dve.drain()

        def add_to_stream(dve, name, lay, comp):
            def read(n, s, j, sl, ps):
                x = xs(n, sl)
                return dve.scalar_tensor_tensor(x, ps, mod(lay, comp, n, sl[2]), x, ALU.mult, ALU.add)

            dense_evac(dve, name, read)

        def mix(dve, m):
            for f in range(KD):
                dve.scalar_tensor_tensor(MX1[:, f * PADW + 1:f * PADW + T + 2], XX[:, f * PADW + 1:f * PADW + T + 2],
                                         vec("mu", m * KD + f), HP[:, f * PADW + 1:f * PADW + T + 2], ALU.mult, ALU.add)

        def shift_pool(pool):
            for f in range(KD):
                o = f * PADW
                pool.tensor_tensor(XX[:, o + 1:o + T + 2], HP[:, o:o + T + 1], HP[:, o + 2:o + T + 3], ALU.add
                                   ).then_inc(s_mix, 1)

        def shift_dve(dve):
            for f in range(KD):
                o = f * PADW
                dve.wait_ge(s_mix, f + 1)
                dve.scalar_tensor_tensor(XX[:, o + 1:o + T + 2], XX[:, o + 1:o + T + 2], 0.5, HP[:, o + 1:o + T + 2],
                                         ALU.mult, ALU.subtract)

        def spill_act(act, name, sp0):
            def before(i, s):
                act.wait_ge(s_spd[s], (i + sp0 + 1) * 16)

            def read(n, s, j, sl, ps):
                return act.activation(STG[s][:, sl[0]:sl[0] + sl[1]], ps, ACT.Copy)

            dense_evac(act, name, read, before)

        def spill_store(sp, name, dram):
            d = order[name]
            t0 = d.slices[0][0]

            def store(i, s):
                sp.wait_ge(s_read[name][s], i * d.j + 2 * d.j)
                o = dram[i * 2 + s] if isinstance(i, int) else dram[ds(i * 2 + s, 1)].rearrange("o p t -> (o p) t")
                sp.dma_start(o[:, t0:T], STG[s][:, t0:T]).then_inc(s_spd[s], 16)

            return store

        KQ, KR = STG

        def kk_pe(pe):
            with pe.Fori(0, KD) as n:
                pe.wait_ge(s_hsq, n + 11)
                pe.wait_ge(s_hroot, n + 11)
                for c, w in PIECES:
                    mm = pe.matmul(PS[:, c:c + w], cst("sum64"), KQ[:, c:c + w], start=True, stop=True)
                mm.then_inc(s_hms, 1)

        def kk_act(act):
            with act.Fori(0, KD) as n:
                act.wait_ge(s_hms, n + 11)
                act.activation(KQ, KF[:, ds(n * T, T)], ACT.Square, scale=vec("k_k", n)).then_inc(s_hsq, 1)
                act.wait_ge(s_hms, n + 12)
                act.wait_ge(s_qn, n + 10)
                act.activation(KR, PS[:, 0:T], ACT.Sqrt).then_inc(s_hroot, 1)

        def kk_dve(dve):
            with dve.Fori(0, KD) as n:
                dve.wait_ge(s_hroot, n + 12)
                dve.tensor_scalar(KR, KR, 1e-12, None, ALU.max)
                dve.drain()
                dve.reciprocal(KR, KR)
                dve.drain()
                dve.scalar_tensor_tensor(NF[:, ds(n * T, T)], KF[:, ds(n * T, T)], vec("k_k", n), KR, ALU.mult, ALU.mult
                                         ).then_inc(s_qn, 1)

        def units(ap):
            return ap.rearrange("p (u t) -> p u t", t=CH)

        def own(buf, h):
            n = buf.shape[1] // 2
            return buf[HEADS[h], h * n:(h + 1) * n]

        def mask_half(lev, h):
            return mask(lev)[HEADS[h]].rearrange("p (d t) -> p d t", d=2).unsqueeze(2).broadcast_to([64, 2, 4, CH])

        def mask_all(lev):
            return mask(lev).rearrange("p (d t) -> p d t", d=2).unsqueeze(2).broadcast_to([P, 2, 4, CH])

        def dct(ap):
            return ap.rearrange("p (d c t) -> p d c t", d=2, c=4)

        STRICT, STRICT_T, INCL_T, EYE, FIRST_T = 6, 7, 8, 9, 10
        NL = len(LEVELS)
        NI = 2 * NGR
        HEADS = [slice(0, 64), slice(64, 128)]

        def is_context(i):
            return i % NGR == 0

        def starts(i):
            g = i % NGR
            return [g * GT, (5 - g) % 5 * GT]

        def latent_before(q, i):
            return q * (NI - 2) + (i - 1 - i // NGR if i % NGR else i - i // NGR)

        def state_count(q, c, s):
            return q * (4 * NI + 2) + (4 * c + s + 1 + c // NGR)

        def scan_unit(d, s):
            return s if d == 0 else 7 - s

        def scan_loads(sp):
            with sp.Fori(0, NPAIR // 2) as q:
                for i in range(NI):
                    it = q * NI + i
                    sp.wait_ge(s_hat, it + 1)
                    sp.wait_ge(s_kd, it + 1)
                    sp.wait_ge(s_vt, it + 1)
                    g0 = starts(i)
                    pair = ds(q * 2 + i // NGR, 1)
                    sp.dma_start(W2, a_lora2[pair].rearrange("o p q -> (o p) q")).then_inc(s_kin, 16)
                    for x, dram in enumerate((k_dram, n_dram, v_dram)):
                        for d in range(2):
                            o = x * 2 * GT + d * GT
                            sp.dma_start(KIN[:, o:o + GT], dram[pair, :, g0[d]:g0[d] + GT].rearrange("o p t -> (o p) t")
                                         ).then_inc(s_kin, 16)
                    if not is_context(i):
                        for d in range(2):
                            o = 3 * 2 * GT + d * GT
                            sp.dma_start(KIN[:, o:o + GT], r_dram[pair, :, g0[d]:g0[d] + GT].rearrange("o p t -> (o p) t")
                                         ).then_inc(s_rin, 16)

        def scan_pe(pe):
            def per_head(out, b, lhs, rhs, n=CH):
                for h in range(2):
                    for u in range(NU):
                        mm = pe.matmul(PS[HEADS[h], b * 512 + u * n:b * 512 + (u + 1) * n], lhs(h, u), rhs(h, u),
                                       start=True, stop=True)
                mm.then_inc(out, 1)

            def stacked(buf, o=0, step=CH, n=CH):
                return lambda h, u: buf[:, o + u * step:o + u * step + n]

            def spread(buf):
                return lambda h, u: buf[:, (h * NU + u) * CH:(h * NU + u + 1) * CH]

            def eye(h, u=0):
                return CSTS[:, CST["ident"] + h * CH:CST["ident"] + (h + 1) * CH]

            def two(buf, h, d):
                return buf[:, (h * 2 + d) * CH:(h * 2 + d + 1) * CH]

            def lora(q, i):
                g0 = starts(i)
                pe.wait_ge(s_kin, (q * NI + i) * 112 + 112)
                apart(pe)
                for x, (hid, b) in enumerate(((HW, 3), (HA, 6))):
                    for d in range(2):
                        o = b * 512 + d * GT
                        mm = pe.matmul(PS[:, o:o + GT], W2[:, (2 * x + d) * P:(2 * x + d + 1) * P],
                                       hid[:, g0[d]:g0[d] + GT], start=True, stop=True)
                mm.then_inc(s_lz, 1)

            def turn(sem_, buf, o=0):
                per_head(sem_, 7, stacked(buf, o) if buf is KIN else spread(buf), eye)

            def chain_w(q, c, s):
                m, par = MS[s % 2], c % 2
                pe.wait_ge(s_St, state_count(q, c, s))
                apart(pe)
                for h in range(2):
                    for d in range(2):
                        u = scan_unit(d, s)
                        o = PS[HEADS[h], d * CH:(d + 1) * CH]
                        pe.matmul(o, AR[par][:, u * P:u * P + CH], two(m, h, d), start=True, stop=False)
                        mm = pe.matmul(o, AAK[par][:, u * CH:(u + 1) * CH], spread(VST[par])(h, u),
                                       start=False, stop=True)
                mm.then_inc(s_W, 1)

            def chain_u(q, c, s):
                it, par = q * NI + c, c % 2
                pe.wait_ge(s_Wc, it * 4 + s + 1)
                apart(pe)
                for h in range(2):
                    for d in range(2):
                        u = scan_unit(d, s)
                        mm = pe.matmul(PS[HEADS[h], P + d * CH:P + (d + 1) * CH], GS[par][:, u * CH:(u + 1) * CH],
                                       two(WSB, h, d), start=True, stop=True)
                mm.then_inc(s_U, 1)

            def chain_d(q, c, s):
                it, par = q * NI + c, c % 2
                m = MS[s % 2]
                pe.wait_ge(s_Uc, it * 4 + s + 1)
                apart(pe)
                for h in range(2):
                    for d in range(2):
                        u = scan_unit(d, s)
                        o = PS[HEADS[h], 2 * P + d * CH:2 * P + (d + 1) * CH]
                        pe.matmul(o, BT[par][:, u * CH:(u + 1) * CH], two(USB, h, d), start=True, stop=False)
                        mm = pe.matmul(o, BT[par][:, (NU + u) * CH:(NU + u + 1) * CH], spread(VST[par])(h, u),
                                       start=False, stop=True)
                mm.then_inc(s_D, 1)
                if is_context(c):
                    return
                if s == 0:
                    pe.wait_ge(s_yc, latent_before(q, c) + 1)
                    apart(pe)
                for h in range(2):
                    for d in range(2):
                        u = scan_unit(d, s)
                        o = PS[HEADS[h], 512 + u * CH:512 + (u + 1) * CH]
                        pe.matmul(o, AR[par][:, u * P + CH:(u + 1) * P], two(m, h, d), start=True, stop=False)
                        pe.matmul(o, ARB[par][:, u * CH:(u + 1) * CH], two(USB, h, d), start=False, stop=False)
                        mm = pe.matmul(o, ARK[par][:, u * CH:(u + 1) * CH], spread(VST[par])(h, u),
                                       start=False, stop=True)
                if s == 3:
                    mm.then_inc(s_y, 1)

            def body(q, i):
                it, par = q * NI + i, i % 2
                c = i - 1
                if c >= 0:
                    pe.wait_ge(s_trc, (it - 1) * 2 + 2)
                    chain_w(q, c, 0)
                pe.wait_ge(s_hat, it + 2)
                apart(pe)
                per_head(s_s1, 6, stacked(AR[par], 0, P), spread(BH))
                if c >= 0:
                    chain_u(q, c, 0)
                n = CH if is_context(i) else P
                for x, b in ((2, BH), (4, BK)):
                    for h in range(2):
                        for u in range(NU):
                            o = x * 512 + u * P
                            mm = pe.matmul(PS[HEADS[h], o:o + n], spread(b)(h, u), AR[par][:, u * P:u * P + n],
                                           start=True, stop=True)
                    mm.then_inc(s_s1, 1)
                    if c >= 0:
                        if x == 2:
                            chain_d(q, c, 0)
                        else:
                            chain_w(q, c, 1)
                pe.wait_ge(s_vc, it + 1)
                apart(pe)
                turn(s_tr, BH)
                if c >= 0:
                    chain_u(q, c, 1)
                pe.wait_ge(s_m1, it + 1)
                for lv in range(NL):
                    pe.wait_ge(s_g, it * (NL + 1) + lv + 1)
                    apart(pe)
                    per_head(s_z, 4, spread(NB), stacked(GS[par]))
                    if c >= 0:
                        if lv == 0:
                            chain_d(q, c, 1)
                        elif lv == 1:
                            chain_u(q, c, 2)
                        elif lv == 2:
                            chain_w(q, c, 3)
                        elif lv == 3:
                            chain_d(q, c, 3)
                    if lv == 1 and i + 1 < NI:
                        lora(q, i + 1)
                    pe.wait_ge(s_tt, it * NL + lv + 1)
                    pe.wait_ge(s_zc, it * NL + lv + 1)
                    apart(pe)
                    per_head(s_gz, 5, stacked(GTS), spread(ZS))
                    if lv < NL - 1:
                        per_head(s_tz, 2, spread(ZS), stacked(GTS))
                    if c >= 0:
                        if lv == 0:
                            chain_w(q, c, 2)
                        elif lv == 1:
                            chain_d(q, c, 2)
                        elif lv == 2:
                            chain_u(q, c, 3)
                    if lv == 1:
                        pe.wait_ge(s_trc, it * 2 + 1)
                        apart(pe)
                        turn(s_tr, BK)
                    if lv == 3 and i + 1 < NI:
                        pe.wait_ge(s_trc, it * 2 + 2)
                        apart(pe)
                        turn(s_vt, KIN, 2 * 2 * GT)

            with pe.Fori(0, NPAIR // 2) as q:
                lora(q, 0)
                turn(s_vt, KIN, 2 * 2 * GT)
                for i in range(NI):
                    body(q, i)
                pe.wait_ge(s_trc, q * (2 * NI) + 2 * NI)
                pe.wait_ge(s_g, q * (NI * (NL + 1)) + NI * (NL + 1))
                for s in range(4):
                    chain_w(q, NI - 1, s)
                    chain_u(q, NI - 1, s)
                    chain_d(q, NI - 1, s)

        def scan_act(act):
            def tanhs(q, i):
                pair = q * 2 + i // NGR
                act.wait_ge(s_lz, q * NI + i + 1)
                apart(act)
                for d in range(2):
                    act.activation(TZ[:, d * GT:(d + 1) * GT], PS[:, 3 * 512 + d * GT:3 * 512 + (d + 1) * GT], ACT.Tanh,
                                   bias=DER[:, ds(pair + d * 8, 1)], scale=0.5)
                for d in range(2):
                    i_ = act.activation(TA[:, d * GT:(d + 1) * GT], PS[:, 6 * 512 + d * GT:6 * 512 + (d + 1) * GT],
                                        ACT.Tanh, bias=DER[:, ds(pair + 16 + d * 8, 1)], scale=0.5)
                i_.then_inc(s_th, 1)

            def powers(q, i):
                act.wait_ge(s_cum, q * NI + i + 1)
                act.activation(XN, IN, ACT.Exp, scale=DECAY)
                act.activation(EX, EX, ACT.Exp, scale=-DECAY)
                act.drain()
                act.activation(IN, IN, ACT.Exp, scale=-DECAY).then_inc(s_xp, 1)

            def values(q, i):
                act.wait_ge(s_vt, q * NI + i + 2)
                for h in range(2):
                    i_ = act.activation(own(VST[i % 2], h), bank(7)[HEADS[h]], ACT.Copy)
                i_.then_inc(s_vc, 1)

            def turned(q, i, x):
                act.wait_ge(s_tr, (q * NI + i) * 2 + x + 1)
                act.activation(BT[i % 2][:, x * 512:(x + 1) * 512], bank(7), ACT.Copy).then_inc(s_trc, 1)

            def copy_w(q, c, s):
                if c >= 0:
                    act.wait_ge(s_W, (q * NI + c) * 4 + s + 1)
                    for h in range(2):
                        i_ = act.activation(own(WSB, h), PS[HEADS[h], 0:P], ACT.Copy)
                    i_.then_inc(s_Wc, 1)

            def copy_u(q, c, s):
                if c >= 0:
                    act.wait_ge(s_U, (q * NI + c) * 4 + s + 1)
                    for h in range(2):
                        i_ = act.activation(own(USB, h), PS[HEADS[h], P:2 * P], ACT.Copy)
                    i_.then_inc(s_Uc, 1)

            with act.Fori(0, NPAIR // 2) as q:
                tanhs(q, 0)
                values(q, 0)
                powers(q, 0)
                for i in range(NI):
                    c = i - 1
                    copy_w(q, c, 0)
                    copy_u(q, c, 0)
                    copy_w(q, c, 1)
                    turned(q, i, 0)
                    copy_u(q, c, 1)
                    copy_w(q, c, 2)
                    copy_u(q, c, 2)
                    if i + 1 < NI:
                        tanhs(q, i + 1)
                    turned(q, i, 1)
                    copy_w(q, c, 3)
                    copy_u(q, c, 3)
                    if i + 1 < NI:
                        powers(q, i + 1)
                        values(q, i + 1)
                for s in range(4):
                    copy_w(q, NI - 1, s)
                    copy_u(q, NI - 1, s)

        def scan_pool(pool):
            with pool.Fori(0, NPAIR // 2) as q:
                for i in range(NI):
                    it = q * NI + i
                    pool.wait_ge(s_kin, it * 112 + 112)
                    pool.wait_ge(s_cum, it + 1)
                    apart(pool)
                    ka = 2 * (i // NGR)
                    pool.tensor_scalar(TK, TA, KA[:, ka:ka + 1], KA[:, ka + 1:ka + 2], ALU.mult, ALU.add)
                    pool.tensor_scalar(TB, TA, 0.5, 0.5, ALU.mult, ALU.add)
                    pool.drain()
                    pool.tensor_tensor(TK, TK, KIN[:, 0:2 * GT], ALU.mult)
                    pool.tensor_tensor(TB, TB, KIN[:, 2 * GT:4 * GT], ALU.mult).then_inc(s_kd, 1)

        def scan_dve(dve):
            def sums(q, i):
                dve.wait_ge(s_th, q * NI + i + 1)
                dve.tensor_scalar(TZ, TZ, 0.5, 0.5, ALU.mult, ALU.add)
                dve.drain()
                sg = [TZ[:, 0:GT], TZ[:, GT:2 * GT]]
                i0, i1, e0, e1 = IN[:, 0:GT], IN[:, GT:2 * GT], EX[:, 0:GT], EX[:, GT:2 * GT]
                dve.tensor_tensor_scan(i0, CM, sg[0], 0.0, ALU.mult, ALU.add)
                dve.tensor_tensor_scan(F1, CM, sg[1], 0.0, ALU.mult, ALU.add)
                dve.drain()
                dve.tensor_tensor(e0, i0, sg[0], ALU.subtract)
                dve.tensor_tensor(units(e1), units(F1)[:, :, CH - 1:CH].broadcast_to([P, 4, CH]), units(F1), ALU.subtract)
                dve.drain()
                dve.tensor_tensor(i1, e1, sg[1], ALU.add).then_inc(s_cum, 1)

            def hats(q, i):
                par = i % 2
                dve.wait_ge(s_kd, q * NI + i + 2)
                dve.wait_ge(s_xp, q * NI + i + 1)
                for h in range(2):
                    dve.tensor_tensor(own(BH, h), TB[HEADS[h]], XN[HEADS[h]], ALU.mult)
                    dve.tensor_tensor(own(BK, h), TK[HEADS[h]], XN[HEADS[h]], ALU.mult)
                ar = AR[par].rearrange("p (u x t) -> p u x t", u=NU, x=2)
                if not is_context(i):
                    dve.wait_ge(s_rin, latent_before(q, i) * 32 + 32)
                    dve.tensor_tensor(ar[:, :, 1, :], units(KIN[:, 6 * GT:8 * GT]), units(IN), ALU.mult)
                dve.tensor_copy(PCS[par][:, 0:4], units(IN)[:, 0:4, CH - 1])
                dve.tensor_copy(PCS[par][:, 4:8], units(IN)[:, 4:8, 0])
                dve.scalar_tensor_tensor(ar[:, :, 0, :], units(KIN[:, 2 * GT:4 * GT]), -1.0, units(EX), ALU.mult, ALU.mult
                                         ).then_inc(s_hat, 1)

            def zero_state(c):
                if is_context(c):
                    dve.memset(MST, 0.0)
                    dve.memset(MS[0], 0.0).then_inc(s_St, 1)
                    dve.drain()

            def chain(q, c, s):
                if c < 0:
                    return
                nxt = MS[(s + 1) % 2]
                pc = [PCS[c % 2][:, scan_unit(d, s):scan_unit(d, s) + 1] for d in range(2)]
                for d in range(2):
                    dve.tensor_scalar(MP[:, d * CH:(d + 1) * CH], MST[:, d * CH:(d + 1) * CH], pc[d], None, ALU.mult)
                dve.drain()
                dve.wait_ge(s_D, (q * NI + c) * 4 + s + 1)
                for d in range(2):
                    dve.scalar_tensor_tensor(MST[:, d * CH:(d + 1) * CH], PS[:, 2 * P + d * CH:2 * P + (d + 1) * CH],
                                             pc[d], MP[:, d * CH:(d + 1) * CH], ALU.mult, ALU.add)
                dve.drain()
                for h in range(2):
                    i_ = dve.tensor_copy(own(nxt, h), MST[HEADS[h]])
                i_.then_inc(s_St, 1)
                dve.drain()

            def add_y(q, c):
                if c < 0 or is_context(c):
                    return
                dve.wait_ge(s_y, latent_before(q, c) + 1)
                g = c % NGR
                for d, t0 in enumerate(((g - 1) * GT, (4 - g) * GT)):
                    ys = YS[:, ds((q * 2 + c // NGR) * TL + t0, GT)]
                    i_ = dve.tensor_tensor(ys, ys, PS[:, 512 + d * GT:512 + (d + 1) * GT], ALU.add)
                i_.then_inc(s_yc, 1)
                dve.drain()

            def middle(q, i):
                it, par, c = q * NI + i, i % 2, i - 1
                gs = GS[par]
                dve.wait_ge(s_s1, it * 3 + 1)
                for h in range(2):
                    dve.tensor_tensor(dct(own(NB, h)), dct(bank(6)[HEADS[h]]), mask_half(STRICT, h), ALU.mult)
                dve.tensor_tensor(dct(GTS), dct(bank(6)), mask_all(FIRST_T), ALU.mult)
                dve.wait_ge(s_s1, it * 3 + 2)
                s1 = PS[:, 2 * 512:4 * 512].rearrange("p (d c x t) -> p d c x t", d=2, c=4, x=2)
                s2 = PS[:, 4 * 512:6 * 512].rearrange("p (d c x t) -> p d c x t", d=2, c=4, x=2)
                dve.tensor_tensor(dct(gs), s1[:, :, :, 0, :], mask_all(0), ALU.mult)
                dve.drain()
                dve.tensor_tensor(dct(gs), dct(gs), mask_all(EYE), ALU.add).then_inc(s_g, 1)
                dve.tensor_tensor(dct(GTS), dct(GTS), mask_all(EYE), ALU.add).then_inc(s_tt, 1)
                if not is_context(i):
                    dve.tensor_tensor(dct(ARB[par]), s1[:, :, :, 1, :], mask_all(INCL_T), ALU.mult)
                chain(q, c, 0)
                dve.wait_ge(s_s1, it * 3 + 3)
                i_ = dve.tensor_tensor(dct(AAK[par]), s2[:, :, :, 0, :], mask_all(STRICT_T), ALU.mult)
                if not is_context(i):
                    i_ = dve.tensor_tensor(dct(ARK[par]), s2[:, :, :, 1, :], mask_all(INCL_T), ALU.mult)
                i_.then_inc(s_m1, 1)
                for lv in range(NL):
                    dve.wait_ge(s_z, it * NL + lv + 1)
                    for h in range(2):
                        i_ = dve.tensor_tensor(dct(own(ZS, h)), dct(bank(4)[HEADS[h]]), mask_half(lv + 1, h), ALU.mult)
                    i_.then_inc(s_zc, 1)
                    if lv == 0:
                        chain(q, c, 1)
                    if lv == 3:
                        chain(q, c, 3)
                        if i:
                            zero_state(i)
                    dve.wait_ge(s_gz, it * NL + lv + 1)
                    dve.tensor_tensor(gs, gs, bank(5), ALU.add).then_inc(s_g, 1)
                    if lv < NL - 1:
                        dve.wait_ge(s_tz, it * (NL - 1) + lv + 1)
                        dve.tensor_tensor(GTS, GTS, bank(2), ALU.add).then_inc(s_tt, 1)
                    if lv == 1:
                        chain(q, c, 2)
                    if lv == 2 and i + 1 < NI:
                        sums(q, i + 1)
                    if lv == 3:
                        add_y(q, c)

            with dve.Fori(0, NPAIR // 2) as q:
                zero_state(0)
                dve.wait_ge(s_kd, q * NI + 1)
                for x in range(2):
                    dve.tensor_copy(KA[:, 2 * x:2 * x + 1], DER[:, ds(q * 2 + 32 + x, 1)])
                    dve.tensor_copy(KA[:, 2 * x + 1:2 * x + 2], DER[:, ds(q * 2 + 40 + x, 1)])
                sums(q, 0)
                hats(q, 0)
                for i in range(NI):
                    middle(q, i)
                    if i + 1 < NI:
                        hats(q, i + 1)
                for s in range(4):
                    chain(q, NI - 1, s)
                add_y(q, NI - 1)

        HALVES = [(0, 512), (512, 512)]

        def read_loads(sp):
            with sp.Fori(0, NPAIR) as p:
                sp.wait_ge(s_r3r, p + 1)
                sp.wait_ge(s_r3p, p * 6 + 1)
                for x, dram in enumerate((k_dram, r_dram, v_dram)):
                    sp.dma_start(RIN[:, x * TL:(x + 1) * TL], dram[ds(p, 1), :, TC:T].rearrange("o p t -> (o p) t")
                                 ).then_inc(s_r3, 16)
                sp.dma_start(RW2, a_lora2[ds(p, 1), :, 2 * P:4 * P].rearrange("o p q -> (o p) q")).then_inc(s_r3, 16)
                sp.dma_start(RG2, a_g2[ds(p, 1)].rearrange("o p q -> (o p) q")).then_inc(s_r3, 16)

        def read_pool(pool):
            with pool.Fori(0, NPAIR) as p:
                pool.wait_ge(s_r3p, p * 6 + 1)
                pool.tensor_copy(YC, YS[:, ds(p * TL, TL)]).then_inc(s_r3c, 1)

        def read_pe(pe):
            with pe.Fori(0, NPAIR) as p:
                pe.wait_ge(s_r3c, p + 1)
                pe.wait_ge(s_r3v, p * 5 + 1)
                apart(pe)
                for c in range(TL // CH):
                    mm = pe.transpose(PS[0:64, c * P:(c + 1) * P], YC[:, c * CH:(c + 1) * CH], cst("ident"))
                mm.then_inc(s_r3p, 1)
                pe.wait_ge(s_r3a, p * 4 + 1)
                for c, w in HALVES:
                    mm = pe.matmul(PS[:, 2048 + c:2048 + c + w], cst("mean64"), YT[:, c:c + w], start=True, stop=True)
                mm.then_inc(s_r3p, 1)
                pe.wait_ge(s_r3, p * 80 + 80)
                for d in range(2):
                    for c, w in HALVES:
                        mm = pe.matmul(PS[:, d * TL + c:d * TL + c + w], RW2[:, d * P:(d + 1) * P],
                                       HA[:, TC + c:TC + c + w], start=True, stop=True)
                mm.then_inc(s_r3p, 1)
                pe.wait_ge(s_r3a, p * 4 + 2)
                for c, w in HALVES:
                    mm = pe.matmul(PS[:, 3072 + c:3072 + c + w], cst("mean64"), SQY[:, c:c + w], start=True, stop=True)
                mm.then_inc(s_r3p, 1)
                pe.wait_ge(s_r3v, p * 5 + 3)
                for c, w in HALVES:
                    mm = pe.matmul(PS[:, 2048 + c:2048 + c + w], cst("sum64"), RBY[:, c:c + w], start=True, stop=True)
                mm.then_inc(s_r3p, 1)
                pe.wait_ge(s_r3a, p * 4 + 3)
                for c, w in HALVES:
                    for kt in range(2):
                        mm = pe.matmul(PS[:, 3072 + c:3072 + c + w], RG2[:, kt * P:(kt + 1) * P],
                                       HG[:, kt * TL + c:kt * TL + c + w], start=kt == 0, stop=kt == 1)
                mm.then_inc(s_r3p, 1)

        def read_act(act):
            with act.Fori(0, NPAIR) as p:
                act.wait_ge(s_r3p, p * 6 + 2)
                act.wait_ge(s_r3v, p * 5 + 1)
                for h in range(2):
                    i_ = act.activation(units(YT[64 * h:64 * h + 64, :]),
                                        PS[0:64, 0:2048].rearrange("p (u g v) -> p u g v", u=TL // CH, g=2)[:, :, h, :],
                                        ACT.Copy)
                i_.then_inc(s_r3a, 1)
                act.wait_ge(s_r3v, p * 5 + 2)
                act.activation(SQY, YT, ACT.Square).then_inc(s_r3a, 1)
                act.wait_ge(s_r3p, p * 6 + 5)
                act.activation(RTY, PS[:, 3072:4096], ACT.Sqrt, bias=NEG[:, 2:3]).then_inc(s_r3a, 1)
                for d in range(2):
                    i_ = act.activation(RTA[:, d * TL:(d + 1) * TL], PS[:, d * TL:(d + 1) * TL], ACT.Tanh,
                                        bias=DER[:, ds(p + 16 + d * 8, 1)], scale=0.5)
                i_.then_inc(s_r3a, 1)

        def read_dve(dve):
            k, r, v = (RIN[:, x * TL:(x + 1) * TL] for x in range(3))
            t0, t1 = RTA[:, 0:TL], RTA[:, TL:2 * TL]
            with dve.Fori(0, NPAIR) as p:
                dve.wait_ge(s_r3p, p * 6 + 3)
                dve.tensor_tensor(YT, YT, PS[:, 2048:3072], ALU.subtract).then_inc(s_r3v, 1)
                dve.wait_ge(s_r3a, p * 4 + 4)
                dve.wait_ge(s_r3, p * 80 + 80)
                dve.tensor_tensor(t0, t0, t1, ALU.add)
                dve.drain()
                dve.tensor_scalar(t0, t0, DER[:, ds(p + 32, 1)], NEG[:, ds(p + 8, 1)], ALU.mult, ALU.add)
                dve.drain()
                dve.tensor_tensor(t0, t0, k, ALU.mult)
                dve.drain()
                dve.scalar_tensor_tensor(RBY, r, vec("r_k", p), t0, ALU.mult, ALU.mult).then_inc(s_r3v, 1)
                dve.reciprocal(RTY, RTY)
                dve.drain()
                dve.tensor_tensor(YT, YT, RTY, ALU.mult)
                dve.drain()
                dve.tensor_scalar(YT, YT, vec("gn_w", p), vec("gn_b", p), ALU.mult, ALU.add)
                dve.wait_ge(s_r3p, p * 6 + 6)
                dve.tensor_tensor(BVY, v, PS[:, 2048:3072], ALU.mult).then_inc(s_r3r, 1)
                dve.drain().then_inc(s_r3v, 1)
                dve.tensor_tensor(YT, YT, BVY, ALU.add).then_inc(s_r3v, 1)
                dve.drain()
                dve.wait_ge(s_r3p, p * 6 + 7)
                dve.tensor_tensor(YS[:, ds(p * TL, TL)], YT, PS[:, 3072:4096], ALU.mult)
                dve.drain().then_inc(s_r3v, 1)

        def ada_loads(sp):
            AW = [SB[:, base + x * 4096:base + (x + 1) * 4096] for x in range(2)]
            for s in range(2):
                sp.dma_start(AW[s], a_adaw[s]).then_inc(s_adaw[s], 16)
            with sp.Fori(1, 12) as i:
                for s in range(2):
                    sp.wait_ge(s_adap, 2 * i + s - 1)
                    sp.dma_start(AW[s], a_adaw[ds(2 * i + s, 1)].rearrange("o p q -> (o p) q")).then_inc(s_adaw[s], 16)

        def ada_pe(pe):
            pe.wait_ge(s_silu, 1)
            with pe.Fori(0, 12) as i:
                for s in range(2):
                    aw = SB[:, base + s * 4096:base + (s + 1) * 4096]
                    pe.wait_ge(s_adaw[s], i * 16 + 16)
                    for n in range(4):
                        for k in range(KD):
                            mm = pe.matmul(PS[:, ds(i * 16 + s * 8 + n * 2, 2)], aw[:, k * 512 + n * P:k * 512 + (n + 1) * P],
                                           SILU[:, 2 * k:2 * k + 2], start=k == 0, stop=k == KD - 1)
                    mm.then_inc(s_adap, 1)

        def ada_dve(dve):
            dve.tensor_scalar(DER[:, 0:16], vec("w0", 0, 16), 0.5, None, ALU.mult)
            dve.tensor_scalar(DER[:, 16:32], vec("a0", 0, 16), 0.5, None, ALU.mult)
            dve.tensor_scalar(DER[:, 32:40], vec("k_a", 0, 8), 0.5, None, ALU.mult)
            dve.tensor_scalar(DER[:, 40:48], vec("k_a", 0, 8), -0.5, 1.0, ALU.mult, ALU.add)
            dve.tensor_scalar(NEG[:, 8:16], vec("k_a", 0, 8), -1.0, 2.0, ALU.mult, ALU.add)
            dve.tensor_scalar(vec("qk_gain", 0, 8), vec("qk_gain", 0, 8), DH ** -0.5, None, ALU.mult)
            dve.wait_ge(s_adap, 24)
            m = MOD.rearrange("p (n s) -> p n s", s=2)
            dve.tensor_tensor(m, PS[:, 0:192].rearrange("p (n s) -> p n s", s=2),
                              vec("ada_b", 0, 96).unsqueeze(2).broadcast_to([P, 96, 2]), ALU.add)
            dve.drain()
            for lay in range(2):
                for which in range(2):
                    o = ((lay * 6 + 3 * which + 1) * 8) * 2
                    q = (lay * 2 + which) * 16
                    dve.tensor_scalar(SCL[:, q:q + 16], MOD[:, o:o + 16], 1.0, None, ALU.add)

        def run(steps):
            for name in steps:
                if name == stop:
                    break

        @block.sync
        def _(sp):
            def steps():
                sp.dma_start(SILU, a_cT).then_inc(s_const, 16)
                sp.dma_start(VECS, a_vec).then_inc(s_const, 16)
                sp.dma_start(CSTS, a_cst).then_inc(s_const, 16)
                sp.dma_start(XC.rearrange("p (k t) -> p k t", k=KD), a_xT[:, :, 0:TC]).then_inc(s_const, 16)
                sp.dma_start(XL.rearrange("p (k t) -> p k t", k=KD), a_xT[:, :, TC:T]).then_inc(s_const, 16)
                ada_loads(sp)
                dense_loads(sp, "qk")
                sp.wait_ge(s_bar, over("norm_a0"))
                sp.dma_start(ROPE, a_rope).then_inc(s_load, 16)
                sp.dma_start(WV, a_wv).then_inc(s_load, 16)
                yield "norm_a0"
                yield "qk"
                dense_loads(sp, "wo")
                yield "wo"
                for h in range(2):
                    dense_loads(sp, f"up0{h}")
                    dense_loads(sp, f"dn0{h}")
                yield "ffn0"
                for name in ("lw", "la", "g"):
                    dense_loads(sp, name)
                dense_loads(sp, "v", spill_store(sp, "v", v_dram))
                dense_loads(sp, "r", spill_store(sp, "r", r_dram))
                dense_loads(sp, "k")
                sp.wait_ge(s_bar, over("scan_init"))
                scan_loads(sp)
                yield "scan"
                sp.wait_ge(s_bar, over("scan"))
                read_loads(sp)
                yield "read"
                dense_loads(sp, "ro")
                yield "ro"
                for h in range(2):
                    dense_loads(sp, f"up1{h}")
                    dense_loads(sp, f"dn1{h}")
                yield "ffn1"

            run(steps())
            sp.wait_ge(s_bar, over(stop))
            for f in range(2):
                o = f * 4
                sp.dma_start(out[:, o:o + 4, :], XL[:, o * TL:(o + 4) * TL].rearrange("p (k t) -> p k t", k=4)
                             ).then_inc(s_out, 16)
            sp.wait_ge(s_out, 32)

        @block.gpsimd
        def _(pool):
            def steps():
                pool.memset(NEG[:, 0:1], 0.0)
                pool.memset(NEG[:, 1:2], EPS)
                pool.memset(NEG[:, 2:3], GN_EPS)
                pool.sem_inc(s_kd, 1)
                for s in range(2):
                    pool.sem_inc(s_spd[s], 16)
                stage_over(pool, "start")
                stage_over(pool, "ada")
                stage_over(pool, "norm_a0")
                yield "norm_a0"
                stage_over(pool, "qk")
                stage_over(pool, "heads")
                for b in QS:
                    for q in b:
                        pool.memset(q, 0.0)
                pool.drain()
                att_pool(pool, lat)
                att_pool(pool, con)
                stage_over(pool, "attention")
                stage_over(pool, "wo")
                yield "wo"
                for b in UB:
                    for c in (0, TC + 1, T + 2):
                        pool.memset(b[:, c:c + 1], 0.0)
                stage_over(pool, "norm_f0")
                stage_over(pool, "ffn0")
                yield "ffn0"
                for c in (0, TC + 1, T + 2):
                    pool.memset(HP.rearrange("p (k t) -> p k t", k=KD)[:, :, c:c + 1], 0.0)
                stage_over(pool, "norm_a1")
                shift_pool(pool)
                for name in ("shift", "mix1", "lw", "mix4", "la", "mix5", "g", "mix3"):
                    stage_over(pool, name)
                stage_over(pool, "v")
                stage_over(pool, "mix0")
                for s in range(2):
                    pool.wait_ge(s_spd[s], 16 * 9)
                stage_over(pool, "r")
                stage_over(pool, "mix2")
                stage_over(pool, "k")
                for n in range(KD):
                    pool.wait_ge(s_qn, 11 + n)
                    pool.dma_start(k_dram[n], KF[:, n * T:(n + 1) * T]).then_inc(s_kst, 16)
                    pool.dma_start(n_dram[n], NF[:, n * T:(n + 1) * T]).then_inc(s_kst, 16)
                pool.wait_ge(s_kst, 32 * KD)
                stage_over(pool, "kk")
                yield "kk"
                for b in (*VST, *MS, WSB, USB):
                    pool.memset(b, 0.0)
                stage_over(pool, "scan_init")
                scan_pool(pool)
                stage_over(pool, "scan")
                yield "scan"
                read_pool(pool)
                stage_over(pool, "read")
                yield "read"
                stage_over(pool, "ro")
                yield "ro"
                for b in UB:
                    for c in (0, TC + 1, T + 2):
                        pool.memset(b[:, c:c + 1], 0.0)
                stage_over(pool, "norm_f1")
                stage_over(pool, "ffn1")
                yield "ffn1"
                stage_over(pool, "norm_end")

            run(steps())

        @block.scalar
        def _(act):
            def steps():
                act.sem_inc(s_pr, 2)
                act.sem_inc(s_otc, 2)
                act.sem_inc(s_hroot, 1)
                act.wait_ge(s_const, 80)
                act.activation(SILU, SILU, ACT.Silu).then_inc(s_silu, 1)
                stage_over(act, "start")
                stage_over(act, "ada")
                norm_act(act, "a0", 0, 0, ah_h)
                stage_over(act, "norm_a0")
                yield "norm_a0"
                dense_evac(act, "qk", lambda n, s, j, sl, ps: act.activation(QK[:, ds(n * T + sl[0], sl[1])], ps, ACT.Copy),
                           only=(0,))
                stage_over(act, "qk")
                qk_act(act)
                stage_over(act, "heads")
                att_act(act, lat)
                att_act(act, con)
                stage_over(act, "attention")
                stage_over(act, "wo")
                yield "wo"
                norm_act(act, "f0", 0, 1, fh_h)
                stage_over(act, "norm_f0")
                for h in range(2):
                    up_evac_act(act, 0, h, SLICES, h * FH)
                stage_over(act, "ffn0")
                yield "ffn0"
                norm_act(act, "a1", 1, 0, hp_h)
                stage_over(act, "norm_a1")
                stage_over(act, "shift")
                stage_over(act, "mix1")
                dense_evac(act, "lw", lambda n, s, j, sl, ps: act.activation(HW[:, sl[0]:sl[0] + sl[1]], ps, ACT.Tanh))
                stage_over(act, "lw")
                stage_over(act, "mix4")
                dense_evac(act, "la", lambda n, s, j, sl, ps: act.activation(HA[:, sl[0]:sl[0] + sl[1]], ps, ACT.Copy))
                stage_over(act, "la")
                stage_over(act, "mix5")
                dense_evac(act, "g", lambda n, s, j, sl, ps: act.activation(
                    HG[:, n * TL + sl[0] - TC:n * TL + sl[0] - TC + sl[1]], ps, ACT.Sigmoid))
                stage_over(act, "g")
                stage_over(act, "mix3")
                spill_act(act, "v", 0)
                stage_over(act, "v")
                stage_over(act, "mix0")
                spill_act(act, "r", 4)
                stage_over(act, "r")
                stage_over(act, "mix2")
                dense_evac(act, "k", lambda n, s, j, sl, ps: act.activation(KF[:, ds(n * T + sl[0], sl[1])], ps, ACT.Copy),
                           only=(0,))
                stage_over(act, "k")
                kk_act(act)
                stage_over(act, "kk")
                yield "kk"
                stage_over(act, "scan_init")
                scan_act(act)
                stage_over(act, "scan")
                yield "scan"
                read_act(act)
                stage_over(act, "read")
                yield "read"
                stage_over(act, "ro")
                yield "ro"
                norm_act(act, "f1", 1, 1, fh_h)
                stage_over(act, "norm_f1")
                for h in range(2):
                    up_evac_act(act, 1, h, LAT, (2 + h) * FH)
                stage_over(act, "ffn1")
                yield "ffn1"
                norm_act(act, "end", 0, 0, None)
                stage_over(act, "norm_end")

            run(steps())

        @block.tensor
        def _(pe):
            def steps():
                pe.sem_inc(s_sc, 4)
                pe.sem_inc(s_pv, 2)
                pe.sem_inc(s_ot, 2)
                pe.sem_inc(s_hms, 1)
                pe.sem_inc(s_vt, 1)
                pe.sem_inc(s_r3p, 1)
                stage_over(pe, "start")
                ada_pe(pe)
                stage_over(pe, "ada")
                norm_pe(pe, "a0")
                stage_over(pe, "norm_a0")
                yield "norm_a0"
                dense_products(pe, "qk", a_rhs)
                pe.wait_ge(s_load, 32)
                for t in range(T // P):
                    if t >= 2:
                        pe.wait_ge(s_vr, t - 1)
                    for k in range(KD):
                        mm = pe.matmul(PS[:, (6 + t % 2) * 512:(6 + t % 2) * 512 + HKV * DH],
                                       AH[:, k * T + t * P:k * T + (t + 1) * P], WV[:, k * 256:(k + 1) * 256],
                                       start=k == 0, stop=k == KD - 1)
                    mm.then_inc(s_v, 1)
                stage_over(pe, "qk")
                qk_pe(pe)
                stage_over(pe, "heads")
                att_pe(pe, lat)
                att_pe(pe, con)
                stage_over(pe, "attention")
                dense_products(pe, "wo", a_rhs)
                stage_over(pe, "wo")
                yield "wo"
                norm_pe(pe, "f0")
                stage_over(pe, "norm_f0")
                for h in range(2):
                    if h:
                        for s in range(2):
                            pe.wait_ge(s_read["dn00"][s], 5 * order["dn00"].j)
                    dense_products(pe, f"up0{h}", f_rhs)
                    pe.wait_ge(s_gd, h + 1)
                    dense_products(pe, f"dn0{h}", g_rhs)
                stage_over(pe, "ffn0")
                yield "ffn0"
                norm_pe(pe, "a1")
                for name in ("norm_a1", "shift", "mix1"):
                    stage_over(pe, name)
                for name, nxt in (("lw", "mix4"), ("la", "mix5"), ("g", "mix3"), ("v", "mix0"), ("r", "mix2"), ("k", None)):
                    dense_products(pe, name, m_rhs)
                    stage_over(pe, name)
                    if nxt:
                        stage_over(pe, nxt)
                kk_pe(pe)
                stage_over(pe, "kk")
                yield "kk"
                stage_over(pe, "scan_init")
                scan_pe(pe)
                stage_over(pe, "scan")
                yield "scan"
                read_pe(pe)
                stage_over(pe, "read")
                yield "read"
                dense_products(pe, "ro", lambda k, sl: YS[:, k * TL + sl[0] - TC:k * TL + sl[0] - TC + sl[1]])
                stage_over(pe, "ro")
                yield "ro"
                norm_pe(pe, "f1")
                stage_over(pe, "norm_f1")
                for h in range(2):
                    if h:
                        for s in range(2):
                            pe.wait_ge(s_read["dn10"][s], 5 * order["dn10"].j)
                    dense_products(pe, f"up1{h}", f_rhs)
                    pe.wait_ge(s_gd, 2 + h + 1)
                    dense_products(pe, f"dn1{h}", g_rhs)
                stage_over(pe, "ffn1")
                yield "ffn1"
                norm_pe(pe, "end")
                stage_over(pe, "norm_end")

            run(steps())

        @block.vector
        def _(dve):
            def steps():
                dve.sem_inc(s_os, 2)
                dve.sem_inc(s_qkd, 1)
                dve.sem_inc(s_cv[0], 1)
                dve.sem_inc(s_cv[1], 1)
                dve.sem_inc(s_hat, 1)
                dve.sem_inc(s_yc, 1)
                dve.sem_inc(s_r3v, 1)
                dve.sem_inc(s_r3r, 1)
                stage_over(dve, "start")
                dve.wait_ge(s_const, 80)
                ada_dve(dve)
                stage_over(dve, "ada")
                norm_dve(dve, "a0", ah_h)
                stage_over(dve, "norm_a0")
                yield "norm_a0"
                dense_evac(dve, "qk", lambda n, s, j, sl, ps: dve.tensor_copy(QK[:, ds(n * T + sl[0], sl[1])], ps),
                           only=(1,))
                for t in range(T // P):
                    dve.wait_ge(s_v, t + 1)
                    dve.tensor_copy(VT[:, t * 256:(t + 1) * 256], PS[:, (6 + t % 2) * 512:(6 + t % 2) * 512 + 256]
                                    ).then_inc(s_vr, 1)
                stage_over(dve, "qk")
                dve.wait_ge(s_load, 32)
                qk_dve(dve)
                dve.drain()
                for j in range(HKV):
                    for h in range(2):
                        src_ = QK[64 * (j % 2):64 * (j % 2) + 64, (8 + j // 2) * T:(9 + j // 2) * T]
                        dve.tensor_copy(KDUP[64 * h:64 * h + 64, j * T:(j + 1) * T], src_)
                stage_over(dve, "heads")
                att_dve(dve, lat)
                att_dve(dve, con)
                stage_over(dve, "attention")
                add_to_stream(dve, "wo", 0, 2)
                stage_over(dve, "wo")
                yield "wo"
                norm_dve(dve, "f0", fh_h)
                stage_over(dve, "norm_f0")
                for h in range(2):
                    up_evac_dve(dve, 0, h, SLICES, h * FH)
                    dve.drain().then_inc(s_gd, 1)
                    add_to_stream(dve, f"dn0{h}", 0, 5)
                    dve.drain()
                stage_over(dve, "ffn0")
                yield "ffn0"
                norm_dve(dve, "a1", hp_h)
                stage_over(dve, "norm_a1")
                shift_dve(dve)
                stage_over(dve, "shift")
                for m, name in ((1, "lw"), (4, "la"), (5, "g"), (3, "v"), (0, "r"), (2, "k")):
                    mix(dve, m)
                    stage_over(dve, f"mix{m}")
                    if name == "k":
                        dense_evac(dve, "k", lambda n, s, j, sl, ps: dve.tensor_copy(KF[:, ds(n * T + sl[0], sl[1])], ps),
                                   only=(1,))
                    stage_over(dve, name)
                kk_dve(dve)
                stage_over(dve, "kk")
                yield "kk"
                for b in (YS, BH, BK, NB, ZS):
                    dve.memset(b, 0.0)
                dve.memset(CM, 1.0)
                dve.drain()
                dve.memset(units(CM)[:, :, 0:1], 0.0)
                stage_over(dve, "scan_init")
                scan_dve(dve)
                stage_over(dve, "scan")
                yield "scan"
                read_dve(dve)
                stage_over(dve, "read")
                yield "read"
                add_to_stream(dve, "ro", 1, 2)
                stage_over(dve, "ro")
                yield "ro"
                norm_dve(dve, "f1", fh_h)
                stage_over(dve, "norm_f1")
                for h in range(2):
                    up_evac_dve(dve, 1, h, LAT, (2 + h) * FH)
                    dve.drain().then_inc(s_gd, 1)
                    add_to_stream(dve, f"dn1{h}", 1, 5)
                    dve.drain()
                stage_over(dve, "ffn1")
                yield "ffn1"
                norm_dve(dve, "end", None)
                stage_over(dve, "norm_end")

            run(steps())


STOP = "norm_end"


def constants():
    i = np.arange(P)
    c = np.zeros((P, NCST), np.float32)
    c[:, CST["mean1024"]:CST["mean1024"] + P] = 1.0 / D
    same = (i[:, None] // 64 == i[None, :] // 64).astype(np.float32)
    c[:, CST["mean64"]:CST["mean64"] + P] = same / DH
    c[:, CST["sum64"]:CST["sum64"] + P] = same
    swap = np.zeros((P, P), np.float32)
    swap[i[0::2] + 1, i[0::2]] = -1.0
    swap[i[0::2], i[0::2] + 1] = 1.0
    c[:, CST["swap"]:CST["swap"] + P] = swap
    c[:, CST["ident"]:CST["ident"] + P] = np.eye(P)
    a, b = np.meshgrid(np.arange(CH), np.arange(CH), indexing="ij")
    m = np.zeros((NLEV, 2, CH, CH), np.float32)
    for lev in range(6):
        w = 2 ** lev
        seam = (a // (2 * w) == b // (2 * w)) & (a // w % 2 == 0) & (b // w % 2 == 1)
        m[lev, 0], m[lev, 1] = seam, seam.T
    m[6, 0], m[6, 1] = b < a, b > a
    m[7, 0], m[7, 1] = b > a, b < a
    m[8, 0], m[8, 1] = b >= a, b <= a
    m[9, :] = a == b
    m[10, 0], m[10, 1] = m[0, 1], m[0, 0]
    m = m.transpose(2, 0, 1, 3).reshape(CH, -1)
    c[:, CST["masks"]:] = np.concatenate([m, m], 0)
    grid_w, nf = 64, DH // 4
    inv = (np.float32(10000.0) ** (-np.arange(nf, dtype=np.float32) / np.float32(nf))).astype(np.float32)
    t = np.arange(TL)
    ang = np.concatenate([(t // grid_w).astype(np.float32)[:, None] * inv, (t % grid_w).astype(np.float32)[:, None] * inv], 1)
    rope = np.zeros((P, 2, T), np.float32)
    rope[:, 0, :TC] = 1.0
    rope[:, 0, TC:] = np.cos(ang).astype(np.float32).T[(i % DH) // 2]
    rope[:, 1, TC:] = np.sin(ang).astype(np.float32).T[(i % DH) // 2]
    return c, rope.reshape(P, 2 * T)


def tiles(w):
    k, n = w.shape
    return w.reshape(k // P, P, n // P, P).transpose(2, 1, 0, 3).reshape(n // P, P, k)


def feat(v):
    return v.reshape(-1, P).T


def layout(x, c, ctx, c_ctx, ada_w, ada_b, attn_w_qkv, attn_q_gain, attn_k_gain, attn_w_o,
           rwkv_mu, rwkv_w_r, rwkv_w_k, rwkv_w_v, rwkv_w_o, rwkv_decay_w0, rwkv_decay_w1, rwkv_decay_w2,
           rwkv_aaa_a0, rwkv_aaa_a1, rwkv_aaa_a2, rwkv_gate_g1, rwkv_gate_g2, rwkv_k_k, rwkv_k_a, rwkv_r_k,
           rwkv_gn_w, rwkv_gn_b, ffn_w_up, ffn_conv_w, ffn_conv_b, ffn_w_down, final_gain):
    cst, rope = constants()
    xx = np.concatenate([ctx[0], x[0]], 0)
    xT = xx.T.reshape(KD, P, T).transpose(1, 0, 2)
    cT = np.stack([c[0], c_ctx], 0).reshape(2, KD, P).transpose(2, 1, 0).reshape(P, 16)
    gains = np.stack([np.concatenate([g, g]) for g in [attn_q_gain[0]] * 8 + [attn_k_gain[0]] * 2], 1)
    conv = np.concatenate([ffn_conv_w, ffn_conv_b[:, None]], 1)
    conv = conv.reshape(2, 4, 2, FJ, P).transpose(4, 0, 3, 2, 1).reshape(P, -1)
    vecs = np.concatenate([feat(ada_b), gains, feat(rwkv_mu[0]), feat(rwkv_decay_w0[0]), feat(rwkv_aaa_a0[0]),
                           feat(rwkv_k_k[0]), feat(rwkv_k_a[0]), feat(rwkv_r_k[0]), feat(rwkv_gn_w[0]),
                           feat(rwkv_gn_b[0]), feat(final_gain), conv], 1)
    adaw = ada_w.reshape(2, KD, P, 12, 512).transpose(0, 3, 2, 1, 4).reshape(24, P, KD * 512)
    wqk = tiles(attn_w_qkv[0][:, :Q_COLS])
    wv = attn_w_qkv[0][:, Q_COLS:].reshape(KD, P, HKV * DH).transpose(1, 0, 2).reshape(P, -1)
    wup = np.stack([tiles(w).reshape(2, 2, FH, P, D).transpose(1, 2, 0, 3, 4).reshape(2, 2 * FH, P, D) for w in ffn_w_up])
    wdn = np.stack([np.stack([tiles(w[h * FH * P:(h + 1) * FH * P]) for h in range(2)]) for w in ffn_w_down])
    lora1 = np.stack([tiles(np.concatenate(list(w[0]), 1))[0] for w in (rwkv_decay_w1, rwkv_aaa_a1)])
    g1 = tiles(np.pad(rwkv_gate_g1[0], ((0, 0), (0, 96))))
    g2 = tiles(np.pad(rwkv_gate_g2[0], ((0, 96), (0, 0))))
    lora2 = np.zeros((KD, P, 4, P), np.float32)
    for n, w in enumerate((rwkv_decay_w2[0], rwkv_aaa_a2[0])):
        for d in range(2):
            lora2[:, 64 * d:64 * d + 64, 2 * n + d] = w[d].reshape(64, KD, P).transpose(1, 0, 2)
    return [xT, cT, vecs, cst, rope, adaw, wqk, wv, tiles(attn_w_o[0]), wup, wdn, lora1, g1,
            tiles(rwkv_w_k[0]), tiles(rwkv_w_v[0]), tiles(rwkv_w_r[0]), tiles(rwkv_w_o[0]),
            lora2.reshape(KD, P, 4 * P), g2]


Q_COLS = H * DH + HKV * DH


def kernel(**inputs):
    import numpy as _np
    import concourse.bacc as _bacc
    from concourse import mybir as _mybir
    from concourse.bass_utils import run_bass_kernel_spmd as _run

    nc = _bacc.Bacc("TRN2", target_bir_lowering=False, num_devices=1)
    arrays, args = {}, []
    for n, a in enumerate(layout(**{k: _np.asarray(v) for k, v in inputs.items()})):
        a = _np.ascontiguousarray(a)
        arrays[f"in_{n}_dram"] = a
        args.append(nc.dram_tensor(f"in_{n}_dram", a.shape, _mybir.dt.from_np(a.dtype), kind="ExternalInput").ap())
    args.append(nc.dram_tensor("out_dram", (P, KD, TL), F32, kind="ExternalOutput").ap())
    program(nc, STOP, *args)
    r = _run(nc, [arrays], core_ids=[0])
    y = r.results[0]["out_dram"]
    return _np.ascontiguousarray(y.transpose(2, 1, 0).reshape(1, TL, D))
```

```python
from contextlib import ExitStack

import concourse.bass as bass
from concourse import mybir
import numpy as np

F32 = mybir.dt.float32
ALU = mybir.AluOpType
ACT = mybir.ActivationFunctionType
AX_X = mybir.AxisListType.X
ds = bass.ds

P = 128
D = 1024
KD = D // P
TC, TL = 256, 1024
T = TC + TL
H, HKV, DH = 16, 4, 64
FF = 2816
FJ = FF // P
FH = FJ // 2
CH = 64
NU = 8
GT = 4 * CH
NGR = T // GT
NPAIR = H // 2
LEVELS = [2, 4, 8, 16, 32]
EPS, GN_EPS = 1e-6, 64e-5
DECAY = float(np.exp(-0.5))
NLEV = 11

SLICES = [(0, TC, 1), (TC, 512, 0), (TC + 512, 512, 0)]
LAT = SLICES[1:]
PADW = T + 4


def padded(t0):
    return t0 + 1 if t0 < TC else t0 + 2


VEC = {}
_at = 0
for _name, _n in (("ada_b", 96), ("qk_gain", 10), ("mu", 48), ("w0", 16), ("a0", 16), ("k_k", 8), ("k_a", 8),
                  ("r_k", 8), ("gn_w", 8), ("gn_b", 8), ("final_gain", 8), ("conv", 2 * FJ * 2 * 4)):
    VEC[_name] = _at
    _at += _n
NVEC = _at
CST = {"mean1024": 0, "mean64": 128, "sum64": 256, "swap": 384, "ident": 512, "masks": 640}
NCST = 640 + NLEV * 2 * CH


class Dense:

    def __init__(self, n, k, slices, before):
        self.n, self.k, self.slices, self.j = n, k, slices, len(slices)
        self.slots = min(n, 2)
        self.loops = n // self.slots
        self.w0 = [0, 0] if before is None else list(before.w1)
        self.p0 = [0, 0] if before is None else list(before.p1)
        self.w1 = [w + (self.loops if s < self.slots else 0) for s, w in enumerate(self.w0)]
        self.p1 = [p + (self.loops * self.j if s < self.slots else 0) for s, p in enumerate(self.p0)]


def program(nc, a_xT, a_cT, a_vec, a_cst, a_rope, a_adaw, a_wqk, a_wv, a_wo, a_wup, a_wdn,
            a_lora1, a_g1, a_rk, a_rv, a_rr, a_ro, a_lora2, a_g2, out):
    order = {}
    last = None

    def dense(name, n, k, slices):
        nonlocal last
        last = order[name] = Dense(n, k, slices, last)

    dense("qk", 10, 8, SLICES)
    dense("wo", 8, 8, SLICES)
    for half in range(2):
        dense(f"up0{half}", 2 * FH, 8, SLICES)
        dense(f"dn0{half}", 8, FH, SLICES)
    dense("lw", 1, 8, SLICES)
    dense("la", 1, 8, SLICES)
    dense("g", 2, 8, LAT)
    dense("v", 8, 8, SLICES)
    dense("r", 8, 8, LAT)
    dense("k", 8, 8, SLICES)
    dense("ro", 8, 8, LAT)
    for half in range(2):
        dense(f"up1{half}", 2 * FH, 8, LAT)
        dense(f"dn1{half}", 8, FH, LAT)
    src = {"qk": a_wqk, "wo": a_wo, "lw": a_lora1[0:1], "la": a_lora1[1:2], "k": a_rk, "v": a_rv, "r": a_rr,
           "g": a_g1, "ro": a_ro}
    for lay in range(2):
        for half in range(2):
            src[f"up{lay}{half}"] = a_wup[lay, half]
            src[f"dn{lay}{half}"] = a_wdn[lay, half]

    k_dram = nc.dram_tensor("k_scratch", (KD, P, T), F32, kind="Internal").ap()
    n_dram = nc.dram_tensor("kk_scratch", (KD, P, T), F32, kind="Internal").ap()
    v_dram = nc.dram_tensor("v_scratch", (KD, P, T), F32, kind="Internal").ap()
    r_dram = nc.dram_tensor("r_scratch", (KD, P, T), F32, kind="Internal").ap()

    with ExitStack() as ctx:
        SB = ctx.enter_context(nc.sbuf_tensor("SB", [P, 52900], F32))
        PS = ctx.enter_context(nc.psum_tensor("PS", [P, 4096], F32))
        top = [0]

        def take(n):
            top[0] += n
            assert top[0] <= 52900, top[0]
            return SB[:, top[0] - n:top[0]]

        def sem(name):
            return ctx.enter_context(nc.semaphore(name))

        def bank(b, n=1):
            return PS[:, b * 512:(b + n) * 512]

        XL = take(KD * TL)
        MOD = take(192)
        SCL = take(64)
        VECS = take(NVEC)
        CSTS = take(NCST)
        SILU = take(16)
        DER = take(48)
        WS = [take(FH * P) for _ in range(2)]
        KA = take(4)
        NEG = take(16)
        XC = take(KD * TC)
        base = top[0]

        def xs(f, sl):
            t0, w, stream = sl
            if stream:
                return XC[:, ds(f * TC, w)]
            return XL[:, ds(f * TL + (t0 - TC), w)]

        def cst(name, rows=P, n=P):
            return CSTS[0:rows, CST[name]:CST[name] + n]

        def mask(lev):
            o = CST["masks"] + lev * 2 * CH
            return CSTS[:, o:o + 2 * CH]

        def vec(name, i=0, n=1):
            return VECS[:, ds(VEC[name] + i, n)]

        def mod(layer, comp, f, stream):
            return MOD[:, ds(((layer * 6 + comp) * 8 + f) * 2 + stream, 1)]

        def scl(layer, norm, f, stream):
            return SCL[:, ds(((layer * 2 + norm) * 8 + f) * 2 + stream, 1)]

        s_const = sem("const_loaded")
        s_adaw = [sem(f"ada_w_loaded{i}") for i in range(2)]
        s_adap = sem("ada_product")
        s_adac = sem("ada_rows_copied")
        s_adat = sem("ada_rows_turned")
        s_adam = sem("ada_columns_added")
        s_silu = sem("silu_c")
        s_bar = sem("stage_over")
        s_passed = sem("wait_passed")
        s_w = [sem(f"weights_loaded{i}") for i in range(2)]
        s_ps = [sem(f"tile_summed{i}") for i in range(2)]
        s_read = {name: [sem(f"tile_read_{name}_{i}") for i in range(2)] for name in order}
        s_sq = sem("squares_ready")
        s_ms = sem("mean_square_ready")
        s_root = sem("root_ready")
        s_scaled = sem("scaled_ready")
        s_hsq = sem("head_squares_ready")
        s_hms = sem("head_sums_ready")
        s_hroot = sem("head_roots_ready")
        s_hp = sem("head_selectors_ready")
        s_hrec = sem("head_factors_ready")
        s_hb = sem("head_factors_spread")
        s_rd = sem("rms_done_reading")
        s_load = sem("stage_input_loaded")
        s_v = sem("v_tile_summed")
        s_vr = sem("v_tile_read")
        s_qn = sem("qk_normed")
        s_rot = sem("qk_swapped")
        s_qkd = sem("qk_roped")
        s_qs = sem("q_block_copied")
        s_sc = sem("scores_ready")
        s_mx = sem("max_ready")
        s_pr = sem("probs_ready")
        s_pt = sem("probs_turned")
        s_pta = sem("probs_even_copied")
        s_ptd = sem("probs_odd_copied")
        s_pv = sem("values_summed")
        s_os = sem("head_out_scaled")
        s_ot = sem("head_out_turned")
        s_otc = sem("head_out_copied")
        s_cv = [sem(f"conv_done{i}") for i in range(2)]
        s_sg = sem("gate_silu_ready")
        s_gd = sem("gated_ready")
        s_mix = sem("mix_ready")
        s_kst = sem("k_stored")
        s_spd = [sem(f"spill_stored{i}") for i in range(2)]
        s_kin = sem("group_inputs_loaded")
        s_rin = sem("group_r_loaded")
        s_lz = sem("lora_summed")
        s_th = sem("tanh_ready")
        s_cum = sem("decay_sums_ready")
        s_xp = sem("decay_powers_ready")
        s_kd = sem("k_and_b_ready")
        s_hat = sem("hats_ready")
        s_vt = sem("v_turned")
        s_vc = sem("v_stacked")
        s_s1 = sem("products_ready")
        s_m1 = sem("products_masked")
        s_tr = sem("hat_turned")
        s_trc = sem("hat_turned_copied")
        s_tt = sem("turned_inverse_grown")
        s_tz = sem("turned_join_ready")
        s_z = sem("join_inner_ready")
        s_zc = sem("join_inner_masked")
        s_gz = sem("join_outer_ready")
        s_g = sem("inverse_grown")
        s_W = sem("w_summed")
        s_Wc = sem("w_copied")
        s_U = sem("u_summed")
        s_Uc = sem("u_copied")
        s_D = sem("state_delta_ready")
        s_St = sem("state_updated")
        s_y = sem("y_ready")
        s_yc = sem("y_added")
        s_out = sem("out_stored")
        s_yt = sem("y_turned")
        s_yf = sem("y_feature_major")
        s_ym = sem("y_mean_ready")
        s_yd = sem("y_centred")
        s_ysq = sem("y_squares_ready")
        s_yv = sem("y_variance_summed")
        s_yr = sem("y_root_ready")
        s_r3 = sem("readout_loaded")
        s_lo = sem("readout_a_summed")
        s_ta = sem("readout_a_ready")
        s_kr = sem("k_r_ready")
        s_rb = sem("bonus_inner_ready")
        s_fs = sem("factors_spread")
        s_fu = sem("factors_used")
        s_bs = sem("bonus_summed")
        s_bu = sem("bonus_used")
        s_gs = sem("gate_summed")
        s_gg = sem("gate_used")
        block = ctx.enter_context(nc.Block())

        STAGES = ["start", "ada", "norm_a0", "qk", "heads", "attention", "wo", "norm_f0", "ffn0", "norm_a1", "shift",
                  "mix1", "lw", "mix4", "la", "mix5", "g", "mix3", "v", "mix0", "r", "mix2", "k", "kk", "scan_init",
                  "scan", "centre", "read", "ro", "norm_f1", "ffn1", "norm_end"]

        def over(name):
            return 4 * (STAGES.index(name) + 1)

        def stage_over(eng, name):
            eng.drain().then_inc(s_bar, 1)
            eng.wait_ge(s_bar, over(name))

        def apart(eng):
            eng.sem_inc(s_passed, 1)

        def dense_loads(sp, name, store=None):
            d = order[name]
            w = src[name]

            def load(i, s):
                sp.dma_start(WS[s][:, 0:d.k * P], w[d.slots * i + s] if isinstance(i, int) else
                             w[ds(d.slots * i + s, 1)].rearrange("o p q -> (o p) q")).then_inc(s_w[s], 16)

            for s in range(d.slots):
                if d.w0[s] > 0:
                    sp.wait_ge(s_ps[s], d.p0[s])
                load(0, s)
            if d.loops > 1:
                with sp.Fori(1, d.loops) as i:
                    for s in range(d.slots):
                        sp.wait_ge(s_ps[s], i * d.j + d.p0[s])
                        load(i, s)
                        if store:
                            store(i - 1, s)
                for s in range(d.slots if store else 0):
                    store(d.loops - 1, s)

        def dense_products(pe, name, rhs):
            d = order[name]

            def body(i):
                for s in range(d.slots):
                    pe.wait_ge(s_w[s], (i + d.w0[s] + 1) * 16)
                    for j, sl in enumerate(d.slices):
                        pe.wait_ge(s_read[name][s], i * d.j + (j + 1))
                        o = PS[:, (3 * s + j) * 512:(3 * s + j) * 512 + sl[1]]
                        for k in range(d.k):
                            mm = pe.matmul(o, WS[s][:, k * P:(k + 1) * P], rhs(k, sl), start=k == 0, stop=k == d.k - 1)
                        mm.then_inc(s_ps[s], 1)

            if d.loops > 1:
                with pe.Fori(0, d.loops) as i:
                    body(i)
            else:
                body(0)

        def dense_evac(eng, name, read, before=None, after=None, only=(0, 1)):
            d = order[name]
            for s in [x for x in only if x < d.slots]:
                eng.sem_inc(s_read[name][s], d.j)

            def body(i):
                for s in [x for x in only if x < d.slots]:
                    if before:
                        before(i, s)
                    for j, sl in enumerate(d.slices):
                        eng.wait_ge(s_ps[s], i * d.j + (d.p0[s] + j + 1))
                        o = PS[:, (3 * s + j) * 512:(3 * s + j) * 512 + sl[1]]
                        read(i * d.slots + s, s, j, sl, o).then_inc(s_read[name][s], 1)
                    if after:
                        after(i, s)

            if d.loops > 1:
                with eng.Fori(0, d.loops) as i:
                    body(i)
            else:
                body(0)

        norms = {}
        nn = 0
        for key, sls in (("a0", SLICES), ("f0", SLICES), ("a1", SLICES), ("f1", LAT), ("end", LAT)):
            norms[key] = (nn, sls)
            nn += len(sls)

        def norm_act(act, key, layer, which, hs):
            n0, sls = norms[key]
            sq, rr = norm_tmp[key]

            def scale_and_shift(q):
                sl = sls[q]
                for f in range(KD):
                    act.wait_ge(s_scaled, (n0 + q) * KD + f + 1)
                    act.activation(hs(f, sl), hs(f, sl), ACT.Identity, bias=mod(layer, 3 * which, f, sl[2]),
                                   scale=scl(layer, which, f, sl[2]))

            for q, sl in enumerate(sls):
                n = n0 + q
                for f in range(KD):
                    m = n * KD + f
                    if m >= 2:
                        act.wait_ge(s_rd, m - 1)
                    act.activation(sq[f % 2][:, 0:sl[1]], xs(f, sl), ACT.Square).then_inc(s_sq, 1)
                act.wait_ge(s_ms, n + 1)
                if q:
                    act.wait_ge(s_scaled, (n - 1) * KD + KD)
                act.activation(rr[:, 0:sl[1]], PS[:, 6 * 512:6 * 512 + sl[1]], ACT.Sqrt, bias=NEG[:, 1:2]
                               ).then_inc(s_root, 1)
                if hs is not None and q:
                    scale_and_shift(q - 1)
            if hs is not None:
                scale_and_shift(len(sls) - 1)

        def norm_pe(pe, key):
            n0, sls = norms[key]
            sq, _ = norm_tmp[key]
            for q, sl in enumerate(sls):
                n = n0 + q
                if q:
                    pe.wait_ge(s_root, n)
                for f in range(KD):
                    pe.wait_ge(s_sq, n * KD + f + 1)
                    mm = pe.matmul(PS[:, 6 * 512:6 * 512 + sl[1]], cst("mean1024"), sq[f % 2][:, 0:sl[1]],
                                   start=f == 0, stop=f == KD - 1)
                    mm.then_inc(s_rd, 1)
                pe.drain().then_inc(s_ms, 1)

        def norm_dve(dve, key, hs):
            n0, sls = norms[key]
            _, rr = norm_tmp[key]
            for q, sl in enumerate(sls):
                n = n0 + q
                dve.wait_ge(s_root, n + 1)
                r = rr[:, 0:sl[1]]
                dve.reciprocal(r, r)
                dve.drain()
                for f in range(KD):
                    if hs is None:
                        dve.scalar_tensor_tensor(xs(f, sl), xs(f, sl), vec("final_gain", f), r, ALU.mult, ALU.mult
                                                 ).then_inc(s_scaled, 1)
                    else:
                        dve.tensor_tensor(hs(f, sl), xs(f, sl), r, ALU.mult).then_inc(s_scaled, 1)

        top[0] = base
        AH = take(KD * T)
        QK = take(10 * T)
        VT = take(10 * HKV * DH)
        KDUP = take(HKV * T)
        ROPE = take(2 * T)
        at_tmp = top[0]
        WV = take(KD * HKV * DH)
        sq_at = top[0]
        top[0] = at_tmp
        SQQ = take(T)
        T1 = take(T)
        top[0] = base + KD * T + 10 * T + 10 * HKV * DH + HKV * T
        PB = [take(T) for _ in range(2)]
        PTB = take(T)
        QS = [[take(P) for _ in range(2)] for _ in range(2)]
        OS = [take(P) for _ in range(2)]
        MXN = take(4)
        RSUM = take(4)
        RINV = take(4)
        att_top = top[0]
        SQ_att = [None, None]
        SQa = [KDUP[:, 0:512], KDUP[:, 512:1024]]
        RRa = KDUP[:, 1024:1536]
        top[0] = base
        FHB = take(KD * T)
        G = take(FH * T)
        UB = [take(PADW) for _ in range(2)]
        CB = [take(PADW) for _ in range(2)]
        SQf = [take(512) for _ in range(2)]
        RRf = take(512)
        HW = SB[:, base - KD * TC:base - KD * TC + T]
        top[0] = base
        HP = take(KD * PADW)
        XX = take(KD * PADW)
        MX1 = take(KD * PADW)
        HA = take(T)
        HG = take(2 * TL)
        STG = [take(T) for _ in range(2)]
        SQr = [STG[0][:, 0:512], STG[0][:, 512:1024]]
        RRr = STG[1][:, 0:512]
        KF = HP[:, 0:KD * T]
        NF = XX[:, 0:KD * T]
        top[0] = base
        YS = take(KD * TL)
        KIN = take(4 * 2 * GT)
        W2 = take(4 * P)
        TZ = take(2 * GT)
        TA = take(2 * GT)
        F1 = take(GT)
        IN = take(2 * GT)
        EX = take(2 * GT)
        XN = take(2 * GT)
        TK = take(2 * GT)
        TB = take(2 * GT)
        BH = take(4 * GT)
        BK = take(4 * GT)
        PCS = [take(NU) for _ in range(2)]
        AR = [take(2 * 2 * GT) for _ in range(2)]
        BT = [take(2 * 2 * GT) for _ in range(2)]
        AAK, ARB, ARK, GS = ([take(2 * GT) for _ in range(2)] for _ in range(4))
        VST = [take(4 * GT) for _ in range(2)]
        NB = take(4 * GT)
        GTS = take(2 * GT)
        ZS = take(4 * GT)
        MST = take(P)
        MP = take(P)
        MS = [take(2 * P) for _ in range(2)]
        WSB = take(2 * P)
        USB = take(2 * P)
        CM = STG[0][:, 0:GT]
        assert top[0] <= base + 3 * KD * PADW, top[0] - base - 3 * KD * PADW
        top[0] = base + KD * TL
        RIN = [take(3 * TL) for _ in range(2)]
        RW2 = [take(2 * P) for _ in range(2)]
        RG2 = [take(2 * P) for _ in range(2)]
        RSEL = take(64 + 20 * DH + T)
        SQY = [take(TL) for _ in range(2)]
        RTA = take(2 * TL)
        KRY = take(TL)
        RBY = take(TL)
        BVY = take(TL)
        assert top[0] <= base + 3 * KD * PADW

        norm_tmp = {"a0": (SQa, RRa), "f0": (SQf, RRf), "a1": (SQr, RRr), "f1": (SQf, RRf), "end": (SQf, RRf)}

        def a_rhs(k, sl):
            return AH[:, k * T + sl[0]:k * T + sl[0] + sl[1]]

        def f_rhs(k, sl):
            return FHB[:, k * T + sl[0]:k * T + sl[0] + sl[1]]

        def g_rhs(k, sl):
            return G[:, k * T + sl[0]:k * T + sl[0] + sl[1]]

        def m_rhs(k, sl):
            return MX1[:, k * PADW + padded(sl[0]):k * PADW + padded(sl[0]) + sl[1]]

        def ah_h(f, sl):
            return AH[:, f * T + sl[0]:f * T + sl[0] + sl[1]]

        def fh_h(f, sl):
            return FHB[:, f * T + sl[0]:f * T + sl[0] + sl[1]]

        def hp_h(f, sl):
            return HP[:, f * PADW + padded(sl[0]):f * PADW + padded(sl[0]) + sl[1]]

        lat = dict(nk=10, q0=TC, per=4, it0=0, its=NPAIR * 4, even=2, odd=1, g0=0, e0=0, o0=0)
        con = dict(nk=2, q0=0, per=1, it0=NPAIR * 4, its=NPAIR, even=1, odd=0, g0=NPAIR * 16 * 3, e0=NPAIR * 16 * 2,
                   o0=NPAIR * 16)

        def att_pieces(a):
            return [(c, min(512, a["nk"] * P - c)) for c in range(0, a["nk"] * P, 512)]

        def att_groups(a):
            return [list(range(g, min(g + 4, a["nk"]))) for g in range(0, a["nk"], 4)]

        def att_cols(a, i, tt):
            if a["per"] == 1:
                return i, a["q0"] + tt * P
            return i // a["per"], (i % a["per"]) * (2 * P) + (a["q0"] + tt * P)

        def att_ahead(a, i, u, n):
            return (i, u + n) if u + n < 4 else (i + 1, u + n - 4)

        def att_steps(eng, a, body):
            with eng.Fori(0, a["its"] - 1) as i:
                for u in range(4):
                    body(i, u, False)
            for u in range(4):
                body(a["its"] - 1, u, True)

        def att_pe(pe, a):
            pieces, groups = att_pieces(a), att_groups(a)
            ng = len(groups)

            def scores(i, u, piece):
                tt, hh = u // 2, u % 2
                hp, _ = att_cols(a, i, tt)
                if piece == 0:
                    pe.wait_ge(s_qs, (i + a["it0"]) * 2 + tt + 1)
                    pe.wait_ge(s_pr, (i + a["it0"]) * 4 + u + 1)
                c, w = pieces[piece]
                mm = pe.matmul(PS[:, 1536 * (u % 2) + c:1536 * (u % 2) + c + w], QS[tt][hh],
                               KDUP[:, ds((hp // 2) * T + c, w)], start=True, stop=True)
                if piece == len(pieces) - 1:
                    mm.then_inc(s_sc, 1)

            def turn_out(tt, scaled):
                pe.wait_ge(s_os, scaled)
                o = 7 * 512 + 256
                pe.transpose(PS[:, o:o + P], OS[tt], cst("ident")).then_inc(s_ot, 1)

            def unit(i, u, last):
                tt, hh = u // 2, u % 2
                n = (i + a["it0"]) * 4 + u
                b = (i + a["it0"]) * 2 + tt
                hp, _ = att_cols(a, i, tt)
                nxt = None if last and u >= 2 else att_ahead(a, i, u, 2)
                left = list(range(len(pieces))) if nxt else []
                pe.wait_ge(s_pr, n + 3)
                for g, tiles in enumerate(groups):
                    if g == 1:
                        pe.wait_ge(s_pta, (i * 4 + u) * a["even"] + a["e0"] + 1)
                    if g == 2:
                        pe.wait_ge(s_ptd, (i * 4 + u) * a["odd"] + a["o0"] + 1)
                    for x, kt in enumerate(tiles):
                        o = 6 * 512 + x * P
                        mm = pe.transpose(PS[:, o:o + P], PB[u % 2][:, kt * P:(kt + 1) * P], cst("ident"))
                    mm.then_inc(s_pt, 1)
                    if left:
                        scores(*nxt, left.pop(0))
                    if g == 0 and u == 2:
                        turn_out(0, n + 2)
                while left:
                    scores(*nxt, left.pop(0))
                pe.wait_ge(s_os, n + 2)
                pe.wait_ge(s_otc, b + 2)
                pe.wait_ge(s_pta, (i * 4 + u) * a["even"] + a["e0"] + a["even"])
                if a["odd"]:
                    pe.wait_ge(s_ptd, (i * 4 + u) * a["odd"] + a["o0"] + a["odd"])
                o = 7 * 512
                for kt in range(a["nk"]):
                    mm = pe.matmul(PS[:, o:o + DH], PTB[:, kt * P:(kt + 1) * P],
                                   VT[:, ds((hp // 2) * DH + kt * HKV * DH, DH)], start=kt == 0, stop=kt == a["nk"] - 1)
                mm.then_inc(s_pv, 1)
                if u == 3:
                    turn_out(1, n + 3)

            for u in range(2):
                for p in range(len(pieces)):
                    scores(0, u, p)
            att_steps(pe, a, unit)

        def att_pool(pool, a):
            with pool.Fori(0, a["its"]) as i:
                for tt in range(2):
                    hp, t0 = att_cols(a, i, tt)
                    pool.wait_ge(s_sc, (i + a["it0"]) * 4 + 2 * tt + 2)
                    for hh in range(2):
                        i_ = pool.tensor_copy(QS[tt][hh][64 * hh:64 * hh + 64, :],
                                              QK[64 * hh:64 * hh + 64, ds(hp * T + t0, P)])
                    i_.then_inc(s_qs, 1)

        def att_dve(dve, a):
            groups = att_groups(a)

            def row_max(i, u):
                dve.wait_ge(s_sc, (i + a["it0"]) * 4 + u + 5)
                dve.tensor_reduce(MXN[:, u:u + 1], PS[:, 1536 * (u % 2):1536 * (u % 2) + a["nk"] * P], AX_X, ALU.max,
                                  negate=True).then_inc(s_mx, 1)

            def unit(i, u, last):
                tt, hh = u // 2, u % 2
                n = (i + a["it0"]) * 4 + u
                for g in range(1, len(groups), 2):
                    w = len(groups[g]) * P
                    dve.wait_ge(s_pt, (i * 4 + u) * len(groups) + a["g0"] + g + 1)
                    dve.wait_ge(s_pv, n + 2)
                    dve.tensor_copy(PTB[:, groups[g][0] * P:groups[g][0] * P + w],
                                    PS[:, 6 * 512:6 * 512 + w]).then_inc(s_ptd, 1)
                if not (last and u >= 2):
                    row_max(*att_ahead(a, i, u, 2))
                dve.wait_ge(s_pr, n + 3)
                dve.reciprocal(RINV[:, u:u + 1], RSUM[:, u:u + 1])
                dve.drain()
                dve.wait_ge(s_pv, n + 3)
                if hh == 0:
                    dve.wait_ge(s_ot, (i + a["it0"]) * 2 + tt + 1)
                o = 7 * 512
                dve.tensor_scalar(OS[tt][:, hh * DH:(hh + 1) * DH], PS[:, o:o + DH], RINV[:, u:u + 1], None, ALU.mult
                                  ).then_inc(s_os, 1)

            row_max(0, 0)
            row_max(0, 1)
            att_steps(dve, a, unit)

        def att_act(act, a):
            groups = att_groups(a)

            def probs(i, u):
                act.wait_ge(s_mx, (i + a["it0"]) * 4 + u + 1)
                act.wait_ge(s_pv, (i + a["it0"]) * 4 + u + 1)
                act.activation(PB[u % 2][:, 0:a["nk"] * P], PS[:, 1536 * (u % 2):1536 * (u % 2) + a["nk"] * P],
                               ACT.Exp, bias=MXN[:, u:u + 1], accum_out=RSUM[:, u:u + 1]).then_inc(s_pr, 1)

            def turned_out(i, tt):
                hp, t0 = att_cols(a, i, tt)
                act.wait_ge(s_ot, (i + a["it0"]) * 2 + tt + 3)
                o = 7 * 512 + 256
                act.activation(AH[:, ds(hp * T + t0, P)], PS[:, o:o + P], ACT.Copy).then_inc(s_otc, 1)

            def unit(i, u, last):
                n = (i + a["it0"]) * 4 + u
                for g in range(0, len(groups), 2):
                    w = len(groups[g]) * P
                    act.wait_ge(s_pt, (i * 4 + u) * len(groups) + a["g0"] + g + 1)
                    act.wait_ge(s_pv, n + 2)
                    act.activation(PTB[:, groups[g][0] * P:groups[g][0] * P + w], PS[:, 6 * 512:6 * 512 + w],
                                   ACT.Copy).then_inc(s_pta, 1)
                    if g == 0:
                        if u == 2:
                            turned_out(i, 0)
                        if not (last and u == 3):
                            probs(*att_ahead(a, i, u, 1))
                if u == 3:
                    turned_out(i, 1)

            probs(0, 0)
            att_steps(act, a, unit)

        PIECES = [(0, 512), (512, 512), (1024, 256)]

        def head_selectors(dve, mem, matrix):
            sel, hexp = mem[:, 0:38], mem[0:20, 64:64 + 20 * DH]
            dve.memset(sel, 0.0)
            dve.drain()
            for h in range(2):
                dve.tensor_copy(sel[:, 18 + h:19 + h], CSTS[:, CST[matrix] + h * DH:CST[matrix] + h * DH + 1])
            dve.tensor_copy(hexp.rearrange("p (r c) -> p r c", c=DH),
                            CSTS[0:20, CST["ident"]:CST["ident"] + 20].unsqueeze(2).broadcast_to([20, 20, DH])
                            ).then_inc(s_hp, 1)

        def head_rows(mem, nt):
            return mem[0:2 * nt, 64 + 20 * DH:64 + 20 * DH + T]

        def squares_act(act, mem, nt, n0, sq, tile, bias, scale):
            for n in range(nt):
                if n >= 2:
                    act.wait_ge(s_hms, n0 + n - 1)
                act.activation(sq[n % 2], tile(n), ACT.Square, scale=scale(n)).then_inc(s_hsq, 1)
            act.wait_ge(s_hms, n0 + nt)
            act.activation(head_rows(mem, nt), PS[0:2 * nt, 0:T], ACT.Sqrt, **bias).then_inc(s_hroot, 1)

        def squares_pe(pe, mem, nt, n0, sq, stage):
            pe.wait_ge(s_hp, stage)
            for n in range(nt):
                pe.wait_ge(s_hsq, n0 + n + 1)
                for c, w in PIECES:
                    mm = pe.matmul(PS[0:2 * nt, c:c + w], mem[:, 18 - 2 * n:18 - 2 * n + 2 * nt], sq[n % 2][:, c:c + w],
                                   start=n == 0, stop=n == nt - 1)
                mm.then_inc(s_hms, 1)

        def spread_pe(pe, mem, nt, n, o):
            for c, w in PIECES:
                mm = pe.matmul(PS[:, o + c:o + c + w], mem[0:2 * nt, 64 + n * P:64 + (n + 1) * P],
                               head_rows(mem, nt)[:, c:c + w], start=True, stop=True)
            mm.then_inc(s_hb, 1)

        QT = 10

        def qk_pe(pe):
            squares_pe(pe, AH, QT, 0, (SQQ, T1), 1)
            pe.wait_ge(s_hrec, 1)
            spread_pe(pe, AH, QT, 0, 0)
            for n in range(QT):
                pe.wait_ge(s_qn, n + 1)
                if n + 1 < QT:
                    spread_pe(pe, AH, QT, n + 1, 0)
                pe.wait_ge(s_qkd, n + 1)
                for c, w in PIECES:
                    mm = pe.matmul(PS[:, 1536 + c:1536 + c + w], cst("swap"), QK[:, n * T + c:n * T + c + w], start=True,
                                   stop=True)
                mm.then_inc(s_rot, 1)

        def qk_act(act):
            squares_act(act, AH, QT, 0, (SQQ, T1), lambda n: QK[:, n * T:(n + 1) * T], dict(bias=NEG[0:2 * QT, 1:2]),
                        lambda n: 1.0)

        def qk_dve(dve):
            def normed(n):
                dve.wait_ge(s_hb, n + 1)
                q = QK[:, n * T:(n + 1) * T]
                dve.scalar_tensor_tensor(q, q, vec("qk_gain", n), PS[:, 0:T], ALU.mult, ALU.mult).then_inc(s_qn, 1)

            head_selectors(dve, AH, "mean64")
            rows = head_rows(AH, QT)
            dve.wait_ge(s_hroot, 1)
            dve.reciprocal(rows, rows).then_inc(s_hrec, 1)
            normed(0)
            for n in range(QT):
                q = QK[:, n * T:(n + 1) * T]
                if n + 1 < QT:
                    normed(n + 1)
                dve.drain()
                dve.tensor_tensor(T1, q, ROPE[:, 0:T], ALU.mult)
                dve.drain()
                dve.wait_ge(s_rot, n + 1)
                dve.tensor_tensor(q, PS[:, 1536:1536 + T], ROPE[:, T:2 * T], ALU.mult)
                dve.drain()
                dve.tensor_tensor(q, q, T1, ALU.add).then_inc(s_qkd, 1)

        def up_evac_act(act, lay, half, slices, q0):
            name = f"up{lay}{half}"
            lo = padded(slices[0][0])
            w = padded(T) - lo

            def before(i, s):
                act.wait_ge(s_cv[s], i + q0 + 1)

            def read(n, s, j, sl, ps):
                return act.activation(UB[s][:, padded(sl[0]):padded(sl[0]) + sl[1]], ps, ACT.Copy)

            def after(i, s):
                if s == 1:
                    act.wait_ge(s_cv[0], i + q0 + 2)
                    act.activation(CB[0][:, lo:lo + w], CB[0][:, lo:lo + w], ACT.Silu).then_inc(s_sg, 1)

            dense_evac(act, name, read, before, after)

        def up_evac_dve(dve, lay, half, slices, q0):
            name = f"up{lay}{half}"
            d = order[name]
            lo = padded(slices[0][0])
            w = padded(T) - lo
            with dve.Fori(0, d.loops) as i:
                for s in range(2):
                    dve.wait_ge(s_read[name][s], i * d.j + 2 * d.j)
                    cv = VEC["conv"] + ((lay * FJ + half * FH) * 2 + s) * 4
                    cw = [VECS[:, ds(i * 8 + cv + x, 1)] for x in range(4)]
                    u, c = UB[s], CB[s][:, lo:lo + w]
                    dve.tensor_scalar(c, u[:, lo:lo + w], cw[1], cw[3], ALU.mult, ALU.add)
                    dve.drain()
                    dve.scalar_tensor_tensor(c, u[:, lo - 1:lo - 1 + w], cw[0], c, ALU.mult, ALU.add)
                    dve.drain()
                    dve.scalar_tensor_tensor(c, u[:, lo + 1:lo + 1 + w], cw[2], c, ALU.mult, ALU.add
                                             ).then_inc(s_cv[s], 1)
                dve.drain()
                dve.wait_ge(s_sg, i + q0 + 1)
                for t0, n in ([(0, TC)] if slices[0][0] == 0 else []) + [(TC, TL)]:
                    dve.tensor_tensor(G[:, ds(i * T + t0, n)], CB[0][:, padded(t0):padded(t0) + n],
                                      CB[1][:, padded(t0):padded(t0) + n], ALU.mult)
                dve.drain()

        def add_to_stream(dve, name, lay, comp):
            def read(n, s, j, sl, ps):
                x = xs(n, sl)
                return dve.scalar_tensor_tensor(x, ps, mod(lay, comp, n, sl[2]), x, ALU.mult, ALU.add)

            dense_evac(dve, name, read)

        def mix(dve, m):
            for f in range(KD):
                dve.scalar_tensor_tensor(MX1[:, f * PADW + 1:f * PADW + T + 2], XX[:, f * PADW + 1:f * PADW + T + 2],
                                         vec("mu", m * KD + f), HP[:, f * PADW + 1:f * PADW + T + 2], ALU.mult, ALU.add)

        DVE_TILES, POOL_TILES = list(range(5)), list(range(5, KD))

        def shift_pool(pool):
            for f in POOL_TILES:
                o = f * PADW
                pool.tensor_tensor(XX[:, o + 1:o + T + 2], HP[:, o:o + T + 1], HP[:, o + 2:o + T + 3], ALU.add
                                   ).then_inc(s_mix, 1)

        def shift_dve(dve):
            for f in DVE_TILES:
                o = f * PADW
                dve.tensor_tensor(XX[:, o + 1:o + T + 2], HP[:, o:o + T + 1], HP[:, o + 2:o + T + 3], ALU.add)
            dve.drain()
            for f in DVE_TILES + POOL_TILES:
                o = f * PADW
                if f in POOL_TILES:
                    dve.wait_ge(s_mix, POOL_TILES.index(f) + 1)
                dve.scalar_tensor_tensor(XX[:, o + 1:o + T + 2], XX[:, o + 1:o + T + 2], 0.5, HP[:, o + 1:o + T + 2],
                                         ALU.mult, ALU.subtract)

        def spill_act(act, name, sp0):
            def before(i, s):
                act.wait_ge(s_spd[s], (i + sp0 + 1) * 16)

            def read(n, s, j, sl, ps):
                return act.activation(STG[s][:, sl[0]:sl[0] + sl[1]], ps, ACT.Copy)

            dense_evac(act, name, read, before)

        def spill_store(sp, name, dram):
            d = order[name]
            t0 = d.slices[0][0]

            def store(i, s):
                sp.wait_ge(s_read[name][s], i * d.j + 2 * d.j)
                o = dram[i * 2 + s] if isinstance(i, int) else dram[ds(i * 2 + s, 1)].rearrange("o p t -> (o p) t")
                sp.dma_start(o[:, t0:T], STG[s][:, t0:T]).then_inc(s_spd[s], 16)

            return store

        KQ, KR = STG

        def kk_pe(pe):
            squares_pe(pe, MX1, KD, QT, (KQ, KR), 2)
            pe.wait_ge(s_hrec, 2)
            for n in range(KD):
                if n >= 2:
                    pe.wait_ge(s_qn, QT + n - 1)
                spread_pe(pe, MX1, KD, n, n % 2 * 1536)

        def kk_act(act):
            squares_act(act, MX1, KD, QT, (KQ, KR), lambda n: KF[:, n * T:(n + 1) * T], {}, lambda n: vec("k_k", n))

        def kk_dve(dve):
            head_selectors(dve, MX1, "sum64")
            rows = head_rows(MX1, KD)
            dve.wait_ge(s_hroot, 2)
            dve.tensor_scalar(rows, rows, 1e-12, None, ALU.max)
            dve.drain()
            dve.reciprocal(rows, rows).then_inc(s_hrec, 1)
            for n in range(KD):
                o = n % 2 * 1536
                dve.wait_ge(s_hb, QT + n + 1)
                dve.scalar_tensor_tensor(NF[:, n * T:(n + 1) * T], KF[:, n * T:(n + 1) * T], vec("k_k", n), PS[:, o:o + T],
                                         ALU.mult, ALU.mult).then_inc(s_qn, 1)

        def units(ap):
            return ap.rearrange("p (u t) -> p u t", t=CH)

        def own(buf, h):
            n = buf.shape[1] // 2
            return buf[HEADS[h], h * n:(h + 1) * n]

        def mask_half(lev, h):
            return mask(lev)[HEADS[h]].rearrange("p (d t) -> p d t", d=2).unsqueeze(2).broadcast_to([64, 2, 4, CH])

        def mask_all(lev):
            return mask(lev).rearrange("p (d t) -> p d t", d=2).unsqueeze(2).broadcast_to([P, 2, 4, CH])

        def dct(ap):
            return ap.rearrange("p (d c t) -> p d c t", d=2, c=4)

        STRICT, STRICT_T, INCL_T, EYE, FIRST_T = 6, 7, 8, 9, 10
        NL = len(LEVELS)
        NI = 2 * NGR
        HEADS = [slice(0, 64), slice(64, 128)]

        def is_context(i):
            return i % NGR == 0

        def starts(i):
            g = i % NGR
            return [g * GT, (5 - g) % 5 * GT]

        def latent_before(q, i):
            return q * (NI - 2) + (i - 1 - i // NGR if i % NGR else i - i // NGR)

        def state_count(q, c, s):
            return q * (4 * NI + 2) + (4 * c + s + 1 + c // NGR)

        def scan_unit(d, s):
            return s if d == 0 else 7 - s

        def scan_loads(sp):
            with sp.Fori(0, NPAIR // 2) as q:
                for i in range(NI):
                    it = q * NI + i
                    sp.wait_ge(s_hat, it + 1)
                    sp.wait_ge(s_kd, it + 1)
                    sp.wait_ge(s_vt, it + 1)
                    g0 = starts(i)
                    pair = ds(q * 2 + i // NGR, 1)
                    sp.dma_start(W2, a_lora2[pair].rearrange("o p q -> (o p) q")).then_inc(s_kin, 16)
                    for x, dram in enumerate((k_dram, n_dram, v_dram)):
                        for d in range(2):
                            o = x * 2 * GT + d * GT
                            sp.dma_start(KIN[:, o:o + GT], dram[pair, :, g0[d]:g0[d] + GT].rearrange("o p t -> (o p) t")
                                         ).then_inc(s_kin, 16)
                    if not is_context(i):
                        for d in range(2):
                            o = 3 * 2 * GT + d * GT
                            sp.dma_start(KIN[:, o:o + GT], r_dram[pair, :, g0[d]:g0[d] + GT].rearrange("o p t -> (o p) t")
                                         ).then_inc(s_rin, 16)

        def scan_pe(pe):
            def per_head(out, b, lhs, rhs, n=CH):
                for h in range(2):
                    for u in range(NU):
                        mm = pe.matmul(PS[HEADS[h], b * 512 + u * n:b * 512 + (u + 1) * n], lhs(h, u), rhs(h, u),
                                       start=True, stop=True)
                mm.then_inc(out, 1)

            def stacked(buf, o=0, step=CH, n=CH):
                return lambda h, u: buf[:, o + u * step:o + u * step + n]

            def spread(buf):
                return lambda h, u: buf[:, (h * NU + u) * CH:(h * NU + u + 1) * CH]

            def eye(h, u=0):
                return CSTS[:, CST["ident"] + h * CH:CST["ident"] + (h + 1) * CH]

            def two(buf, h, d):
                return buf[:, (h * 2 + d) * CH:(h * 2 + d + 1) * CH]

            def lora(q, i):
                g0 = starts(i)
                pe.wait_ge(s_kin, (q * NI + i) * 112 + 112)
                apart(pe)
                for x, (hid, b) in enumerate(((HW, 3), (HA, 6))):
                    for d in range(2):
                        o = b * 512 + d * GT
                        mm = pe.matmul(PS[:, o:o + GT], W2[:, (2 * x + d) * P:(2 * x + d + 1) * P],
                                       hid[:, g0[d]:g0[d] + GT], start=True, stop=True)
                mm.then_inc(s_lz, 1)

            def turn(sem_, buf, o=0):
                per_head(sem_, 7, stacked(buf, o) if buf is KIN else spread(buf), eye)

            def chain_w(q, c, s):
                m, par = MS[s % 2], c % 2
                pe.wait_ge(s_St, state_count(q, c, s))
                apart(pe)
                for h in range(2):
                    for d in range(2):
                        u = scan_unit(d, s)
                        o = PS[HEADS[h], d * CH:(d + 1) * CH]
                        pe.matmul(o, AR[par][:, u * P:u * P + CH], two(m, h, d), start=True, stop=False)
                        mm = pe.matmul(o, AAK[par][:, u * CH:(u + 1) * CH], spread(VST[par])(h, u),
                                       start=False, stop=True)
                mm.then_inc(s_W, 1)

            def chain_u(q, c, s):
                it, par = q * NI + c, c % 2
                pe.wait_ge(s_Wc, it * 4 + s + 1)
                apart(pe)
                for h in range(2):
                    for d in range(2):
                        u = scan_unit(d, s)
                        mm = pe.matmul(PS[HEADS[h], P + d * CH:P + (d + 1) * CH], GS[par][:, u * CH:(u + 1) * CH],
                                       two(WSB, h, d), start=True, stop=True)
                mm.then_inc(s_U, 1)

            def chain_d(q, c, s):
                it, par = q * NI + c, c % 2
                m = MS[s % 2]
                pe.wait_ge(s_Uc, it * 4 + s + 1)
                apart(pe)
                for h in range(2):
                    for d in range(2):
                        u = scan_unit(d, s)
                        o = PS[HEADS[h], 2 * P + d * CH:2 * P + (d + 1) * CH]
                        pe.matmul(o, BT[par][:, u * CH:(u + 1) * CH], two(USB, h, d), start=True, stop=False)
                        mm = pe.matmul(o, BT[par][:, (NU + u) * CH:(NU + u + 1) * CH], spread(VST[par])(h, u),
                                       start=False, stop=True)
                mm.then_inc(s_D, 1)
                if is_context(c):
                    return
                if s == 0:
                    pe.wait_ge(s_yc, latent_before(q, c) + 1)
                    apart(pe)
                for h in range(2):
                    for d in range(2):
                        u = scan_unit(d, s)
                        o = PS[HEADS[h], 512 + u * CH:512 + (u + 1) * CH]
                        pe.matmul(o, AR[par][:, u * P + CH:(u + 1) * P], two(m, h, d), start=True, stop=False)
                        pe.matmul(o, ARB[par][:, u * CH:(u + 1) * CH], two(USB, h, d), start=False, stop=False)
                        mm = pe.matmul(o, ARK[par][:, u * CH:(u + 1) * CH], spread(VST[par])(h, u),
                                       start=False, stop=True)
                if s == 3:
                    mm.then_inc(s_y, 1)

            def body(q, i):
                it, par = q * NI + i, i % 2
                c = i - 1
                if c >= 0:
                    pe.wait_ge(s_trc, (it - 1) * 2 + 2)
                    chain_w(q, c, 0)
                pe.wait_ge(s_hat, it + 2)
                apart(pe)
                per_head(s_s1, 6, stacked(AR[par], 0, P), spread(BH))
                if c >= 0:
                    pe.wait_ge(s_g, it * (NL + 1))
                    chain_u(q, c, 0)
                n = CH if is_context(i) else P
                for x, b in ((2, BH), (4, BK)):
                    for h in range(2):
                        for u in range(NU):
                            o = x * 512 + u * P
                            mm = pe.matmul(PS[HEADS[h], o:o + n], spread(b)(h, u), AR[par][:, u * P:u * P + n],
                                           start=True, stop=True)
                    mm.then_inc(s_s1, 1)
                    if c >= 0:
                        if x == 2:
                            chain_d(q, c, 0)
                        else:
                            chain_w(q, c, 1)
                pe.wait_ge(s_vc, it + 1)
                apart(pe)
                turn(s_tr, BH)
                if c >= 0:
                    chain_u(q, c, 1)
                pe.wait_ge(s_m1, it + 1)
                for lv in range(NL):
                    pe.wait_ge(s_g, it * (NL + 1) + lv + 1)
                    apart(pe)
                    per_head(s_z, 4, spread(NB), stacked(GS[par]))
                    if c >= 0:
                        if lv == 0:
                            chain_d(q, c, 1)
                        elif lv == 1:
                            chain_u(q, c, 2)
                        elif lv == 2:
                            chain_w(q, c, 3)
                        elif lv == 3:
                            chain_d(q, c, 3)
                    if lv == 1 and i + 1 < NI:
                        lora(q, i + 1)
                    pe.wait_ge(s_tt, it * NL + lv + 1)
                    pe.wait_ge(s_zc, it * NL + lv + 1)
                    apart(pe)
                    per_head(s_gz, 5, stacked(GTS), spread(ZS))
                    if lv < NL - 1:
                        per_head(s_tz, 2, spread(ZS), stacked(GTS))
                    if c >= 0:
                        if lv == 0:
                            chain_w(q, c, 2)
                        elif lv == 1:
                            chain_d(q, c, 2)
                        elif lv == 2:
                            chain_u(q, c, 3)
                    if lv == 1:
                        pe.wait_ge(s_trc, it * 2 + 1)
                        apart(pe)
                        turn(s_tr, BK)
                    if lv == 3 and i + 1 < NI:
                        pe.wait_ge(s_trc, it * 2 + 2)
                        apart(pe)
                        turn(s_vt, KIN, 2 * 2 * GT)

            with pe.Fori(0, NPAIR // 2) as q:
                lora(q, 0)
                turn(s_vt, KIN, 2 * 2 * GT)
                for i in range(NI):
                    body(q, i)
                pe.wait_ge(s_trc, q * (2 * NI) + 2 * NI)
                pe.wait_ge(s_g, q * (NI * (NL + 1)) + NI * (NL + 1))
                for s in range(4):
                    chain_w(q, NI - 1, s)
                    chain_u(q, NI - 1, s)
                    chain_d(q, NI - 1, s)

        def scan_act(act):
            def tanhs(q, i):
                pair = q * 2 + i // NGR
                act.wait_ge(s_lz, q * NI + i + 1)
                apart(act)
                for d in range(2):
                    act.activation(TZ[:, d * GT:(d + 1) * GT], PS[:, 3 * 512 + d * GT:3 * 512 + (d + 1) * GT], ACT.Tanh,
                                   bias=DER[:, ds(pair + d * 8, 1)], scale=0.5)
                for d in range(2):
                    i_ = act.activation(TA[:, d * GT:(d + 1) * GT], PS[:, 6 * 512 + d * GT:6 * 512 + (d + 1) * GT],
                                        ACT.Tanh, bias=DER[:, ds(pair + 16 + d * 8, 1)], scale=0.5)
                i_.then_inc(s_th, 1)

            def powers(q, i):
                act.wait_ge(s_cum, q * NI + i + 1)
                act.activation(XN, IN, ACT.Exp, scale=DECAY)
                act.activation(EX, EX, ACT.Exp, scale=-DECAY)
                act.drain()
                act.activation(IN, IN, ACT.Exp, scale=-DECAY).then_inc(s_xp, 1)

            def values(q, i):
                act.wait_ge(s_vt, q * NI + i + 2)
                for h in range(2):
                    i_ = act.activation(own(VST[i % 2], h), bank(7)[HEADS[h]], ACT.Copy)
                i_.then_inc(s_vc, 1)

            def turned(q, i, x):
                act.wait_ge(s_tr, (q * NI + i) * 2 + x + 1)
                act.activation(BT[i % 2][:, x * 512:(x + 1) * 512], bank(7), ACT.Copy).then_inc(s_trc, 1)

            def copy_w(q, c, s):
                if c >= 0:
                    act.wait_ge(s_W, (q * NI + c) * 4 + s + 1)
                    for h in range(2):
                        i_ = act.activation(own(WSB, h), PS[HEADS[h], 0:P], ACT.Copy)
                    i_.then_inc(s_Wc, 1)

            def copy_u(q, c, s):
                if c >= 0:
                    act.wait_ge(s_U, (q * NI + c) * 4 + s + 1)
                    for h in range(2):
                        i_ = act.activation(own(USB, h), PS[HEADS[h], P:2 * P], ACT.Copy)
                    i_.then_inc(s_Uc, 1)

            with act.Fori(0, NPAIR // 2) as q:
                tanhs(q, 0)
                values(q, 0)
                powers(q, 0)
                for i in range(NI):
                    c = i - 1
                    copy_w(q, c, 0)
                    copy_u(q, c, 0)
                    copy_w(q, c, 1)
                    turned(q, i, 0)
                    copy_u(q, c, 1)
                    copy_w(q, c, 2)
                    copy_u(q, c, 2)
                    if i + 1 < NI:
                        tanhs(q, i + 1)
                    turned(q, i, 1)
                    copy_w(q, c, 3)
                    copy_u(q, c, 3)
                    if i + 1 < NI:
                        powers(q, i + 1)
                        values(q, i + 1)
                for s in range(4):
                    copy_w(q, NI - 1, s)
                    copy_u(q, NI - 1, s)

        def scan_pool(pool):
            with pool.Fori(0, NPAIR // 2) as q:
                for i in range(NI):
                    it = q * NI + i
                    pool.wait_ge(s_kin, it * 112 + 112)
                    pool.wait_ge(s_cum, it + 1)
                    apart(pool)
                    ka = 2 * (i // NGR)
                    pool.tensor_scalar(TK, TA, KA[:, ka:ka + 1], KA[:, ka + 1:ka + 2], ALU.mult, ALU.add)
                    pool.tensor_scalar(TB, TA, 0.5, 0.5, ALU.mult, ALU.add)
                    pool.drain()
                    pool.tensor_tensor(TK, TK, KIN[:, 0:2 * GT], ALU.mult)
                    pool.tensor_tensor(TB, TB, KIN[:, 2 * GT:4 * GT], ALU.mult).then_inc(s_kd, 1)

        def scan_dve(dve):
            def sums(q, i):
                dve.wait_ge(s_th, q * NI + i + 1)
                dve.tensor_scalar(TZ, TZ, 0.5, 0.5, ALU.mult, ALU.add)
                dve.drain()
                sg = [TZ[:, 0:GT], TZ[:, GT:2 * GT]]
                i0, i1, e0, e1 = IN[:, 0:GT], IN[:, GT:2 * GT], EX[:, 0:GT], EX[:, GT:2 * GT]
                dve.tensor_tensor_scan(i0, CM, sg[0], 0.0, ALU.mult, ALU.add)
                dve.tensor_tensor_scan(F1, CM, sg[1], 0.0, ALU.mult, ALU.add)
                dve.drain()
                dve.tensor_tensor(e0, i0, sg[0], ALU.subtract)
                dve.tensor_tensor(units(e1), units(F1)[:, :, CH - 1:CH].broadcast_to([P, 4, CH]), units(F1), ALU.subtract)
                dve.drain()
                dve.tensor_tensor(i1, e1, sg[1], ALU.add).then_inc(s_cum, 1)

            def hats_bk(q, i):
                dve.wait_ge(s_kd, q * NI + i + 2)
                dve.wait_ge(s_xp, q * NI + i + 1)
                for h in range(2):
                    dve.tensor_tensor(own(BH, h), TB[HEADS[h]], XN[HEADS[h]], ALU.mult)
                    dve.tensor_tensor(own(BK, h), TK[HEADS[h]], XN[HEADS[h]], ALU.mult)

            def hats_ar(q, i):
                par = i % 2
                ar = AR[par].rearrange("p (u x t) -> p u x t", u=NU, x=2)
                if not is_context(i):
                    dve.wait_ge(s_rin, latent_before(q, i) * 32 + 32)
                    dve.tensor_tensor(ar[:, :, 1, :], units(KIN[:, 6 * GT:8 * GT]), units(IN), ALU.mult)
                dve.tensor_copy(PCS[par][:, 0:4], units(IN)[:, 0:4, CH - 1])
                dve.tensor_copy(PCS[par][:, 4:8], units(IN)[:, 4:8, 0])
                dve.scalar_tensor_tensor(ar[:, :, 0, :], units(KIN[:, 2 * GT:4 * GT]), -1.0, units(EX), ALU.mult, ALU.mult
                                         ).then_inc(s_hat, 1)

            def zero_state(c):
                if is_context(c):
                    dve.memset(MST, 0.0)
                    dve.memset(MS[0], 0.0).then_inc(s_St, 1)
                    dve.drain()

            def chain(q, c, s):
                if c < 0:
                    return
                nxt = MS[(s + 1) % 2]
                pc = [PCS[c % 2][:, scan_unit(d, s):scan_unit(d, s) + 1] for d in range(2)]
                for d in range(2):
                    dve.tensor_scalar(MP[:, d * CH:(d + 1) * CH], MST[:, d * CH:(d + 1) * CH], pc[d], None, ALU.mult)
                dve.drain()
                dve.wait_ge(s_D, (q * NI + c) * 4 + s + 1)
                for d in range(2):
                    dve.scalar_tensor_tensor(MST[:, d * CH:(d + 1) * CH], PS[:, 2 * P + d * CH:2 * P + (d + 1) * CH],
                                             pc[d], MP[:, d * CH:(d + 1) * CH], ALU.mult, ALU.add)
                dve.drain()
                for h in range(2):
                    i_ = dve.tensor_copy(own(nxt, h), MST[HEADS[h]])
                i_.then_inc(s_St, 1)
                dve.drain()

            def add_y(q, c):
                if c < 0 or is_context(c):
                    return
                dve.wait_ge(s_y, latent_before(q, c) + 1)
                g = c % NGR
                for d, t0 in enumerate(((g - 1) * GT, (4 - g) * GT)):
                    ys = YS[:, ds((q * 2 + c // NGR) * TL + t0, GT)]
                    i_ = dve.tensor_tensor(ys, ys, PS[:, 512 + d * GT:512 + (d + 1) * GT], ALU.add)
                i_.then_inc(s_yc, 1)
                dve.drain()

            def middle(q, i):
                it, par, c = q * NI + i, i % 2, i - 1
                gs = GS[par]
                dve.wait_ge(s_s1, it * 3 + 1)
                for h in range(2):
                    dve.tensor_tensor(dct(own(NB, h)), dct(bank(6)[HEADS[h]]), mask_half(STRICT, h), ALU.mult)
                dve.tensor_tensor(dct(GTS), dct(bank(6)), mask_all(FIRST_T), ALU.mult)
                dve.wait_ge(s_s1, it * 3 + 2)
                s1 = PS[:, 2 * 512:4 * 512].rearrange("p (d c x t) -> p d c x t", d=2, c=4, x=2)
                s2 = PS[:, 4 * 512:6 * 512].rearrange("p (d c x t) -> p d c x t", d=2, c=4, x=2)
                dve.tensor_tensor(dct(gs), s1[:, :, :, 0, :], mask_all(0), ALU.mult)
                dve.drain()
                dve.tensor_tensor(dct(gs), dct(gs), mask_all(EYE), ALU.add).then_inc(s_g, 1)
                dve.tensor_tensor(dct(GTS), dct(GTS), mask_all(EYE), ALU.add).then_inc(s_tt, 1)
                if not is_context(i):
                    dve.tensor_tensor(dct(ARB[par]), s1[:, :, :, 1, :], mask_all(INCL_T), ALU.mult)
                chain(q, c, 0)
                dve.wait_ge(s_s1, it * 3 + 3)
                i_ = dve.tensor_tensor(dct(AAK[par]), s2[:, :, :, 0, :], mask_all(STRICT_T), ALU.mult)
                if not is_context(i):
                    i_ = dve.tensor_tensor(dct(ARK[par]), s2[:, :, :, 1, :], mask_all(INCL_T), ALU.mult)
                i_.then_inc(s_m1, 1)
                for lv in range(NL):
                    dve.wait_ge(s_z, it * NL + lv + 1)
                    for h in range(2):
                        i_ = dve.tensor_tensor(dct(own(ZS, h)), dct(bank(4)[HEADS[h]]), mask_half(lv + 1, h), ALU.mult)
                    i_.then_inc(s_zc, 1)
                    if lv == NL - 1 and i + 1 < NI:
                        hats_ar(q, i + 1)
                    if lv == 0:
                        chain(q, c, 1)
                    if lv == 3:
                        chain(q, c, 3)
                        if i:
                            zero_state(i)
                    dve.wait_ge(s_gz, it * NL + lv + 1)
                    dve.tensor_tensor(gs, gs, bank(5), ALU.add).then_inc(s_g, 1)
                    if lv < NL - 1:
                        dve.wait_ge(s_tz, it * (NL - 1) + lv + 1)
                        dve.tensor_tensor(GTS, GTS, bank(2), ALU.add).then_inc(s_tt, 1)
                    if lv == 1:
                        chain(q, c, 2)
                    if lv == 2 and i + 1 < NI:
                        sums(q, i + 1)
                    if lv == 3:
                        add_y(q, c)
                        if i + 1 < NI:
                            hats_bk(q, i + 1)

            with dve.Fori(0, NPAIR // 2) as q:
                zero_state(0)
                dve.wait_ge(s_kd, q * NI + 1)
                for x in range(2):
                    dve.tensor_copy(KA[:, 2 * x:2 * x + 1], DER[:, ds(q * 2 + 32 + x, 1)])
                    dve.tensor_copy(KA[:, 2 * x + 1:2 * x + 2], DER[:, ds(q * 2 + 40 + x, 1)])
                sums(q, 0)
                hats_bk(q, 0)
                hats_ar(q, 0)
                for i in range(NI):
                    middle(q, i)
                for s in range(4):
                    chain(q, NI - 1, s)
                add_y(q, NI - 1)

        HALVES = [(0, 512), (512, 512)]

        def ys(p):
            return YS[:, p * TL:(p + 1) * TL]

        def centre_pe(pe):
            def turn(p):
                for h in range(2):
                    for c in range(TL // CH):
                        o = p % 2 * 1024 + c * CH
                        mm = pe.matmul(PS[HEADS[h], o:o + CH], YS[:, p * TL + c * CH:p * TL + (c + 1) * CH],
                                       CSTS[:, CST["ident"] + h * CH:CST["ident"] + (h + 1) * CH], start=True, stop=True)
                mm.then_inc(s_yt, 1)

            def variance(p):
                pe.wait_ge(s_ysq, p + 1)
                for c, w in HALVES:
                    mm = pe.matmul(PS[0:H, 3072 + c:3072 + c + w], RSEL[:, 18 - 2 * p:18 - 2 * p + H], SQY[p % 2][:, c:c + w],
                                   start=p == 0, stop=p == NPAIR - 1)
                mm.then_inc(s_yv, 1)

            pe.wait_ge(s_hp, 3)
            turn(0)
            for p in range(NPAIR):
                if p + 1 < NPAIR:
                    if p:
                        pe.wait_ge(s_yf, p)
                    turn(p + 1)
                pe.wait_ge(s_yf, p + 1)
                if p:
                    pe.wait_ge(s_yd, p)
                for c, w in HALVES:
                    mm = pe.matmul(PS[:, 2048 + c:2048 + c + w], cst("mean64"), ys(p)[:, c:c + w], start=True, stop=True)
                mm.then_inc(s_ym, 1)
                if p:
                    variance(p - 1)
            variance(NPAIR - 1)

        def centre_act(act):
            def copy(p):
                act.wait_ge(s_yt, p + 1)
                act.activation(ys(p), PS[:, p % 2 * 1024:p % 2 * 1024 + TL], ACT.Copy).then_inc(s_yf, 1)

            copy(0)
            for p in range(NPAIR):
                if p + 1 < NPAIR:
                    copy(p + 1)
                act.wait_ge(s_yd, p + 1)
                if p >= 2:
                    act.wait_ge(s_yv, p - 1)
                act.activation(SQY[p % 2], ys(p), ACT.Square).then_inc(s_ysq, 1)
            act.wait_ge(s_yv, NPAIR)
            act.activation(head_rows(RSEL, KD)[:, 0:TL], PS[0:H, 3072:4096], ACT.Sqrt, bias=NEG[0:H, 2:3]).then_inc(s_yr, 1)

        def centre_dve(dve):
            head_selectors(dve, RSEL, "mean64")
            for p in range(NPAIR):
                dve.wait_ge(s_ym, p + 1)
                dve.tensor_tensor(ys(p), ys(p), PS[:, 2048:3072], ALU.subtract).then_inc(s_yd, 1)
            dve.wait_ge(s_yr, 1)
            rows = head_rows(RSEL, KD)[:, 0:TL]
            dve.reciprocal(rows, rows)

        def read_loads(sp):
            for p in range(NPAIR):
                if p >= 2:
                    sp.wait_ge(s_gg, p - 1)
                for x, dram in enumerate((k_dram, r_dram, v_dram)):
                    sp.dma_start(RIN[p % 2][:, x * TL:(x + 1) * TL], dram[p, :, TC:T]).then_inc(s_r3, 16)
                sp.dma_start(RW2[p % 2], a_lora2[p, :, 2 * P:4 * P]).then_inc(s_r3, 16)
                sp.dma_start(RG2[p % 2], a_g2[p]).then_inc(s_r3, 16)
                sp.wait_ge(s_r3, 80 * (p + 1))

        def read_pool(pool):
            for p in range(NPAIR):
                pool.wait_ge(s_r3, 80 * (p + 1))
                if p:
                    pool.wait_ge(s_rb, p)
                pool.tensor_tensor(KRY, RIN[p % 2][:, 0:TL], RIN[p % 2][:, TL:2 * TL], ALU.mult).then_inc(s_kr, 1)

        def read_pe(pe):
            def outer(p):
                pe.wait_ge(s_r3, 80 * (p + 1))
                if p:
                    pe.wait_ge(s_ta, p)
                for d in range(2):
                    for c, w in HALVES:
                        mm = pe.matmul(PS[:, d * TL + c:d * TL + c + w], RW2[p % 2][:, d * P:(d + 1) * P],
                                       HA[:, TC + c:TC + c + w], start=True, stop=True)
                mm.then_inc(s_lo, 1)

            outer(0)
            for p in range(NPAIR):
                if p:
                    pe.wait_ge(s_bu, p)
                for c, w in HALVES:
                    mm = pe.matmul(PS[:, 2048 + c:2048 + c + w], RSEL[0:H, 64 + p * P:64 + (p + 1) * P],
                                   head_rows(RSEL, KD)[:, c:c + w], start=True, stop=True)
                mm.then_inc(s_fs, 1)
                if p:
                    pe.wait_ge(s_gg, p)
                for c, w in HALVES:
                    for kt in range(2):
                        mm = pe.matmul(PS[:, 3072 + c:3072 + c + w], RG2[p % 2][:, kt * P:(kt + 1) * P],
                                       HG[:, kt * TL + c:kt * TL + c + w], start=kt == 0, stop=kt == 1)
                mm.then_inc(s_gs, 1)
                if p + 1 < NPAIR:
                    outer(p + 1)
                pe.wait_ge(s_rb, p + 1)
                pe.wait_ge(s_fu, p + 1)
                for c, w in HALVES:
                    mm = pe.matmul(PS[:, 2048 + c:2048 + c + w], cst("sum64"), RBY[:, c:c + w], start=True, stop=True)
                mm.then_inc(s_bs, 1)

        def read_act(act):
            for p in range(NPAIR):
                act.wait_ge(s_lo, p + 1)
                if p:
                    act.wait_ge(s_rb, p)
                for d in range(2):
                    i_ = act.activation(RTA[:, d * TL:(d + 1) * TL], PS[:, d * TL:(d + 1) * TL], ACT.Tanh,
                                        bias=DER[:, 16 + d * 8 + p:17 + d * 8 + p], scale=0.5)
                i_.then_inc(s_ta, 1)

        def read_dve(dve):
            t0, t1 = RTA[:, 0:TL], RTA[:, TL:2 * TL]
            for p in range(NPAIR):
                y = ys(p)
                dve.wait_ge(s_fs, p + 1)
                dve.tensor_tensor(y, y, PS[:, 2048:3072], ALU.mult).then_inc(s_fu, 1)
                dve.wait_ge(s_ta, p + 1)
                dve.tensor_tensor(t0, t0, t1, ALU.add)
                dve.drain()
                dve.tensor_scalar(t0, t0, DER[:, 32 + p:33 + p], NEG[:, 8 + p:9 + p], ALU.mult, ALU.add)
                dve.drain()
                dve.wait_ge(s_kr, p + 1)
                dve.scalar_tensor_tensor(RBY, t0, vec("r_k", p), KRY, ALU.mult, ALU.mult).then_inc(s_rb, 1)
                dve.tensor_scalar(y, y, vec("gn_w", p), vec("gn_b", p), ALU.mult, ALU.add)
                dve.wait_ge(s_bs, p + 1)
                dve.tensor_tensor(BVY, RIN[p % 2][:, 2 * TL:3 * TL], PS[:, 2048:3072], ALU.mult).then_inc(s_bu, 1)
                dve.drain()
                dve.tensor_tensor(y, y, BVY, ALU.add)
                dve.drain()
                dve.wait_ge(s_gs, p + 1)
                dve.tensor_tensor(y, y, PS[:, 3072:4096], ALU.mult).then_inc(s_gg, 1)

        def ada_loads(sp):
            AW = [SB[:, base + x * 4096:base + (x + 1) * 4096] for x in range(2)]
            for s in range(2):
                sp.dma_start(AW[s], a_adaw[s]).then_inc(s_adaw[s], 16)
            with sp.Fori(1, 12) as i:
                for s in range(2):
                    sp.wait_ge(s_adap, 2 * i + s - 1)
                    sp.dma_start(AW[s], a_adaw[ds(2 * i + s, 1)].rearrange("o p q -> (o p) q")).then_inc(s_adaw[s], 16)

        ADR = [SB[:, base + 8192 + x * 512:base + 8192 + (x + 1) * 512] for x in range(2)]

        def ada_pe(pe):
            pe.sem_inc(s_adat, 2)
            pe.wait_ge(s_silu, 1)
            with pe.Fori(0, 12) as i:
                for s in range(2):
                    aw = SB[:, base + s * 4096:base + (s + 1) * 4096]
                    pe.wait_ge(s_adaw[s], i * 16 + 16)
                    pe.wait_ge(s_adac, 2 * i + s + 1)
                    for k in range(KD):
                        mm = pe.matmul(PS[0:2, s * 512:(s + 1) * 512], SILU[:, 2 * k:2 * k + 2],
                                       aw[:, k * 512:(k + 1) * 512], start=k == 0, stop=k == KD - 1)
                    mm.then_inc(s_adap, 1)
                for s in range(2):
                    pe.wait_ge(s_adac, 2 * i + s + 3)
                    pe.wait_ge(s_adam, 2 * i + s + 1)
                    apart(pe)
                    for n in range(4):
                        mm = pe.transpose(PS[:, (2 + s) * 512 + 2 * n:(2 + s) * 512 + 2 * n + 2],
                                          ADR[s][0:2, n * P:(n + 1) * P], CSTS[0:2, CST["ident"]:CST["ident"] + 2])
                    mm.then_inc(s_adat, 1)

        def ada_act(act):
            act.sem_inc(s_adac, 2)
            with act.Fori(0, 12) as i:
                for s in range(2):
                    act.wait_ge(s_adap, 2 * i + s + 1)
                    act.wait_ge(s_adat, 2 * i + s + 1)
                    act.activation(ADR[s][0:2, :], PS[0:2, s * 512:(s + 1) * 512], ACT.Copy).then_inc(s_adac, 1)

        def ada_dve(dve):
            dve.tensor_scalar(DER[:, 0:16], vec("w0", 0, 16), 0.5, None, ALU.mult)
            dve.tensor_scalar(DER[:, 16:32], vec("a0", 0, 16), 0.5, None, ALU.mult)
            dve.tensor_scalar(DER[:, 32:40], vec("k_a", 0, 8), 0.5, None, ALU.mult)
            dve.tensor_scalar(DER[:, 40:48], vec("k_a", 0, 8), -0.5, 1.0, ALU.mult, ALU.add)
            dve.tensor_scalar(NEG[:, 8:16], vec("k_a", 0, 8), -1.0, 2.0, ALU.mult, ALU.add)
            dve.tensor_scalar(vec("qk_gain", 0, 8), vec("qk_gain", 0, 8), DH ** -0.5, None, ALU.mult)
            dve.sem_inc(s_adam, 2)
            with dve.Fori(0, 12) as i:
                for s in range(2):
                    dve.wait_ge(s_adat, 2 * i + s + 3)
                    o = (2 + s) * 512
                    dve.tensor_tensor(MOD[:, ds(i * 16 + s * 8, 8)].rearrange("p (n s) -> p n s", s=2),
                                      PS[:, o:o + 8].rearrange("p (n s) -> p n s", s=2),
                                      VECS[:, ds(i * 8 + VEC["ada_b"] + s * 4, 4)].unsqueeze(2).broadcast_to([P, 4, 2]), ALU.add
                                      ).then_inc(s_adam, 1)
            dve.drain()
            for lay in range(2):
                for which in range(2):
                    o = ((lay * 6 + 3 * which + 1) * 8) * 2
                    q = (lay * 2 + which) * 16
                    dve.tensor_scalar(SCL[:, q:q + 16], MOD[:, o:o + 16], 1.0, None, ALU.add)

        @block.sync
        def _(sp):
            sp.dma_start(SILU, a_cT).then_inc(s_const, 16)
            sp.dma_start(VECS, a_vec).then_inc(s_const, 16)
            sp.dma_start(CSTS, a_cst).then_inc(s_const, 16)
            sp.dma_start(XC.rearrange("p (k t) -> p k t", k=KD), a_xT[:, :, 0:TC]).then_inc(s_const, 16)
            sp.dma_start(XL.rearrange("p (k t) -> p k t", k=KD), a_xT[:, :, TC:T]).then_inc(s_const, 16)
            ada_loads(sp)
            dense_loads(sp, "qk")
            sp.wait_ge(s_bar, over("norm_a0"))
            sp.dma_start(ROPE, a_rope).then_inc(s_load, 16)
            sp.dma_start(WV, a_wv).then_inc(s_load, 16)
            dense_loads(sp, "wo")
            for h in range(2):
                dense_loads(sp, f"up0{h}")
                dense_loads(sp, f"dn0{h}")
            for name in ("lw", "la", "g"):
                dense_loads(sp, name)
            dense_loads(sp, "v", spill_store(sp, "v", v_dram))
            dense_loads(sp, "r", spill_store(sp, "r", r_dram))
            dense_loads(sp, "k")
            sp.wait_ge(s_bar, over("scan_init"))
            scan_loads(sp)
            sp.wait_ge(s_bar, over("scan"))
            read_loads(sp)
            dense_loads(sp, "ro")
            for h in range(2):
                dense_loads(sp, f"up1{h}")
                dense_loads(sp, f"dn1{h}")

            sp.wait_ge(s_bar, over("norm_end"))
            for f in range(2):
                o = f * 4
                sp.dma_start(out[:, o:o + 4, :], XL[:, o * TL:(o + 4) * TL].rearrange("p (k t) -> p k t", k=4)
                             ).then_inc(s_out, 16)
            sp.wait_ge(s_out, 32)

        @block.gpsimd
        def _(pool):
            pool.memset(NEG[:, 0:1], 0.0)
            pool.memset(NEG[:, 1:2], EPS)
            pool.memset(NEG[:, 2:3], GN_EPS)
            pool.sem_inc(s_kd, 1)
            for s in range(2):
                pool.sem_inc(s_spd[s], 16)
            stage_over(pool, "start")
            stage_over(pool, "ada")
            stage_over(pool, "norm_a0")
            stage_over(pool, "qk")
            stage_over(pool, "heads")
            for b in QS:
                for q in b:
                    pool.memset(q, 0.0)
            pool.drain()
            att_pool(pool, lat)
            att_pool(pool, con)
            stage_over(pool, "attention")
            stage_over(pool, "wo")
            for b in UB:
                for c in (0, TC + 1, T + 2):
                    pool.memset(b[:, c:c + 1], 0.0)
            stage_over(pool, "norm_f0")
            stage_over(pool, "ffn0")
            for c in (0, TC + 1, T + 2):
                pool.memset(HP.rearrange("p (k t) -> p k t", k=KD)[:, :, c:c + 1], 0.0)
            stage_over(pool, "norm_a1")
            shift_pool(pool)
            for name in ("shift", "mix1", "lw", "mix4", "la", "mix5", "g", "mix3"):
                stage_over(pool, name)
            stage_over(pool, "v")
            stage_over(pool, "mix0")
            for s in range(2):
                pool.wait_ge(s_spd[s], 16 * 9)
            stage_over(pool, "r")
            stage_over(pool, "mix2")
            stage_over(pool, "k")
            for n in range(KD):
                pool.wait_ge(s_qn, 11 + n)
                pool.dma_start(k_dram[n], KF[:, n * T:(n + 1) * T]).then_inc(s_kst, 16)
                pool.dma_start(n_dram[n], NF[:, n * T:(n + 1) * T]).then_inc(s_kst, 16)
            pool.wait_ge(s_kst, 32 * KD)
            stage_over(pool, "kk")
            for b in (*VST, *MS, WSB, USB):
                pool.memset(b, 0.0)
            stage_over(pool, "scan_init")
            scan_pool(pool)
            stage_over(pool, "scan")
            stage_over(pool, "centre")
            read_pool(pool)
            stage_over(pool, "read")
            stage_over(pool, "ro")
            for b in UB:
                for c in (0, TC + 1, T + 2):
                    pool.memset(b[:, c:c + 1], 0.0)
            stage_over(pool, "norm_f1")
            stage_over(pool, "ffn1")
            stage_over(pool, "norm_end")


        @block.scalar
        def _(act):
            act.sem_inc(s_pr, 2)
            act.sem_inc(s_otc, 2)
            act.wait_ge(s_const, 80)
            act.activation(SILU, SILU, ACT.Silu).then_inc(s_silu, 1)
            stage_over(act, "start")
            ada_act(act)
            stage_over(act, "ada")
            norm_act(act, "a0", 0, 0, ah_h)
            stage_over(act, "norm_a0")
            dense_evac(act, "qk", lambda n, s, j, sl, ps: act.activation(QK[:, ds(n * T + sl[0], sl[1])], ps, ACT.Copy),
                       only=(0,))
            stage_over(act, "qk")
            qk_act(act)
            stage_over(act, "heads")
            att_act(act, lat)
            att_act(act, con)
            stage_over(act, "attention")
            stage_over(act, "wo")
            norm_act(act, "f0", 0, 1, fh_h)
            stage_over(act, "norm_f0")
            for h in range(2):
                up_evac_act(act, 0, h, SLICES, h * FH)
            stage_over(act, "ffn0")
            norm_act(act, "a1", 1, 0, hp_h)
            stage_over(act, "norm_a1")
            stage_over(act, "shift")
            stage_over(act, "mix1")
            dense_evac(act, "lw", lambda n, s, j, sl, ps: act.activation(HW[:, sl[0]:sl[0] + sl[1]], ps, ACT.Tanh))
            stage_over(act, "lw")
            stage_over(act, "mix4")
            dense_evac(act, "la", lambda n, s, j, sl, ps: act.activation(HA[:, sl[0]:sl[0] + sl[1]], ps, ACT.Copy))
            stage_over(act, "la")
            stage_over(act, "mix5")
            dense_evac(act, "g", lambda n, s, j, sl, ps: act.activation(
                HG[:, n * TL + sl[0] - TC:n * TL + sl[0] - TC + sl[1]], ps, ACT.Sigmoid))
            stage_over(act, "g")
            stage_over(act, "mix3")
            spill_act(act, "v", 0)
            stage_over(act, "v")
            stage_over(act, "mix0")
            spill_act(act, "r", 4)
            stage_over(act, "r")
            stage_over(act, "mix2")
            dense_evac(act, "k", lambda n, s, j, sl, ps: act.activation(KF[:, ds(n * T + sl[0], sl[1])], ps, ACT.Copy),
                       only=(0,))
            stage_over(act, "k")
            kk_act(act)
            stage_over(act, "kk")
            stage_over(act, "scan_init")
            scan_act(act)
            stage_over(act, "scan")
            centre_act(act)
            stage_over(act, "centre")
            read_act(act)
            stage_over(act, "read")
            stage_over(act, "ro")
            norm_act(act, "f1", 1, 1, fh_h)
            stage_over(act, "norm_f1")
            for h in range(2):
                up_evac_act(act, 1, h, LAT, (2 + h) * FH)
            stage_over(act, "ffn1")
            norm_act(act, "end", 0, 0, None)
            stage_over(act, "norm_end")


        @block.tensor
        def _(pe):
            pe.sem_inc(s_sc, 4)
            pe.sem_inc(s_pv, 2)
            pe.sem_inc(s_ot, 2)
            pe.sem_inc(s_vt, 1)
            stage_over(pe, "start")
            ada_pe(pe)
            stage_over(pe, "ada")
            norm_pe(pe, "a0")
            stage_over(pe, "norm_a0")
            dense_products(pe, "qk", a_rhs)
            pe.wait_ge(s_load, 32)
            for t in range(T // P):
                if t >= 2:
                    pe.wait_ge(s_vr, t - 1)
                for k in range(KD):
                    mm = pe.matmul(PS[:, (6 + t % 2) * 512:(6 + t % 2) * 512 + HKV * DH],
                                   AH[:, k * T + t * P:k * T + (t + 1) * P], WV[:, k * 256:(k + 1) * 256],
                                   start=k == 0, stop=k == KD - 1)
                mm.then_inc(s_v, 1)
            stage_over(pe, "qk")
            qk_pe(pe)
            stage_over(pe, "heads")
            att_pe(pe, lat)
            att_pe(pe, con)
            stage_over(pe, "attention")
            dense_products(pe, "wo", a_rhs)
            stage_over(pe, "wo")
            norm_pe(pe, "f0")
            stage_over(pe, "norm_f0")
            for h in range(2):
                if h:
                    for s in range(2):
                        pe.wait_ge(s_read["dn00"][s], 5 * order["dn00"].j)
                dense_products(pe, f"up0{h}", f_rhs)
                pe.wait_ge(s_gd, h + 1)
                dense_products(pe, f"dn0{h}", g_rhs)
            stage_over(pe, "ffn0")
            norm_pe(pe, "a1")
            for name in ("norm_a1", "shift", "mix1"):
                stage_over(pe, name)
            for name, nxt in (("lw", "mix4"), ("la", "mix5"), ("g", "mix3"), ("v", "mix0"), ("r", "mix2"), ("k", None)):
                dense_products(pe, name, m_rhs)
                stage_over(pe, name)
                if nxt:
                    stage_over(pe, nxt)
            kk_pe(pe)
            stage_over(pe, "kk")
            stage_over(pe, "scan_init")
            scan_pe(pe)
            stage_over(pe, "scan")
            centre_pe(pe)
            stage_over(pe, "centre")
            read_pe(pe)
            stage_over(pe, "read")
            dense_products(pe, "ro", lambda k, sl: YS[:, k * TL + sl[0] - TC:k * TL + sl[0] - TC + sl[1]])
            stage_over(pe, "ro")
            norm_pe(pe, "f1")
            stage_over(pe, "norm_f1")
            for h in range(2):
                if h:
                    for s in range(2):
                        pe.wait_ge(s_read["dn10"][s], 5 * order["dn10"].j)
                dense_products(pe, f"up1{h}", f_rhs)
                pe.wait_ge(s_gd, 2 + h + 1)
                dense_products(pe, f"dn1{h}", g_rhs)
            stage_over(pe, "ffn1")
            norm_pe(pe, "end")
            stage_over(pe, "norm_end")


        @block.vector
        def _(dve):
            dve.sem_inc(s_os, 2)
            dve.sem_inc(s_qkd, 1)
            dve.sem_inc(s_cv[0], 1)
            dve.sem_inc(s_cv[1], 1)
            dve.sem_inc(s_hat, 1)
            dve.sem_inc(s_yc, 1)
            stage_over(dve, "start")
            dve.wait_ge(s_const, 80)
            ada_dve(dve)
            stage_over(dve, "ada")
            norm_dve(dve, "a0", ah_h)
            stage_over(dve, "norm_a0")
            dense_evac(dve, "qk", lambda n, s, j, sl, ps: dve.tensor_copy(QK[:, ds(n * T + sl[0], sl[1])], ps),
                       only=(1,))
            for t in range(T // P):
                dve.wait_ge(s_v, t + 1)
                dve.tensor_copy(VT[:, t * 256:(t + 1) * 256], PS[:, (6 + t % 2) * 512:(6 + t % 2) * 512 + 256]
                                ).then_inc(s_vr, 1)
            stage_over(dve, "qk")
            dve.wait_ge(s_load, 32)
            qk_dve(dve)
            dve.drain()
            for j in range(HKV):
                for h in range(2):
                    src_ = QK[64 * (j % 2):64 * (j % 2) + 64, (8 + j // 2) * T:(9 + j // 2) * T]
                    dve.tensor_copy(KDUP[64 * h:64 * h + 64, j * T:(j + 1) * T], src_)
            stage_over(dve, "heads")
            att_dve(dve, lat)
            att_dve(dve, con)
            stage_over(dve, "attention")
            add_to_stream(dve, "wo", 0, 2)
            stage_over(dve, "wo")
            norm_dve(dve, "f0", fh_h)
            stage_over(dve, "norm_f0")
            for h in range(2):
                up_evac_dve(dve, 0, h, SLICES, h * FH)
                dve.drain().then_inc(s_gd, 1)
                add_to_stream(dve, f"dn0{h}", 0, 5)
                dve.drain()
            stage_over(dve, "ffn0")
            norm_dve(dve, "a1", hp_h)
            stage_over(dve, "norm_a1")
            shift_dve(dve)
            stage_over(dve, "shift")
            for m, name in ((1, "lw"), (4, "la"), (5, "g"), (3, "v"), (0, "r"), (2, "k")):
                mix(dve, m)
                stage_over(dve, f"mix{m}")
                if name == "k":
                    dense_evac(dve, "k", lambda n, s, j, sl, ps: dve.tensor_copy(KF[:, ds(n * T + sl[0], sl[1])], ps),
                               only=(1,))
                stage_over(dve, name)
            kk_dve(dve)
            stage_over(dve, "kk")
            for b in (YS, BH, BK, NB, ZS):
                dve.memset(b, 0.0)
            dve.memset(CM, 1.0)
            dve.drain()
            dve.memset(units(CM)[:, :, 0:1], 0.0)
            stage_over(dve, "scan_init")
            scan_dve(dve)
            stage_over(dve, "scan")
            centre_dve(dve)
            stage_over(dve, "centre")
            read_dve(dve)
            stage_over(dve, "read")
            add_to_stream(dve, "ro", 1, 2)
            stage_over(dve, "ro")
            norm_dve(dve, "f1", fh_h)
            stage_over(dve, "norm_f1")
            for h in range(2):
                up_evac_dve(dve, 1, h, LAT, (2 + h) * FH)
                dve.drain().then_inc(s_gd, 1)
                add_to_stream(dve, f"dn1{h}", 1, 5)
                dve.drain()
            stage_over(dve, "ffn1")
            norm_dve(dve, "end", None)
            stage_over(dve, "norm_end")



def constants():
    i = np.arange(P)
    c = np.zeros((P, NCST), np.float32)
    c[:, CST["mean1024"]:CST["mean1024"] + P] = 1.0 / D
    same = (i[:, None] // 64 == i[None, :] // 64).astype(np.float32)
    c[:, CST["mean64"]:CST["mean64"] + P] = same / DH
    c[:, CST["sum64"]:CST["sum64"] + P] = same
    swap = np.zeros((P, P), np.float32)
    swap[i[0::2] + 1, i[0::2]] = -1.0
    swap[i[0::2], i[0::2] + 1] = 1.0
    c[:, CST["swap"]:CST["swap"] + P] = swap
    c[:, CST["ident"]:CST["ident"] + P] = np.eye(P)
    a, b = np.meshgrid(np.arange(CH), np.arange(CH), indexing="ij")
    m = np.zeros((NLEV, 2, CH, CH), np.float32)
    for lev in range(6):
        w = 2 ** lev
        seam = (a // (2 * w) == b // (2 * w)) & (a // w % 2 == 0) & (b // w % 2 == 1)
        m[lev, 0], m[lev, 1] = seam, seam.T
    m[6, 0], m[6, 1] = b < a, b > a
    m[7, 0], m[7, 1] = b > a, b < a
    m[8, 0], m[8, 1] = b >= a, b <= a
    m[9, :] = a == b
    m[10, 0], m[10, 1] = m[0, 1], m[0, 0]
    m = m.transpose(2, 0, 1, 3).reshape(CH, -1)
    c[:, CST["masks"]:] = np.concatenate([m, m], 0)
    grid_w, nf = 64, DH // 4
    inv = (np.float32(10000.0) ** (-np.arange(nf, dtype=np.float32) / np.float32(nf))).astype(np.float32)
    t = np.arange(TL)
    ang = np.concatenate([(t // grid_w).astype(np.float32)[:, None] * inv, (t % grid_w).astype(np.float32)[:, None] * inv], 1)
    rope = np.zeros((P, 2, T), np.float32)
    rope[:, 0, :TC] = 1.0
    rope[:, 0, TC:] = np.cos(ang).astype(np.float32).T[(i % DH) // 2]
    rope[:, 1, TC:] = np.sin(ang).astype(np.float32).T[(i % DH) // 2]
    return c, rope.reshape(P, 2 * T)


def tiles(w):
    k, n = w.shape
    return w.reshape(k // P, P, n // P, P).transpose(2, 1, 0, 3).reshape(n // P, P, k)


def feat(v):
    return v.reshape(-1, P).T


def layout(x, c, ctx, c_ctx, ada_w, ada_b, attn_w_qkv, attn_q_gain, attn_k_gain, attn_w_o,
           rwkv_mu, rwkv_w_r, rwkv_w_k, rwkv_w_v, rwkv_w_o, rwkv_decay_w0, rwkv_decay_w1, rwkv_decay_w2,
           rwkv_aaa_a0, rwkv_aaa_a1, rwkv_aaa_a2, rwkv_gate_g1, rwkv_gate_g2, rwkv_k_k, rwkv_k_a, rwkv_r_k,
           rwkv_gn_w, rwkv_gn_b, ffn_w_up, ffn_conv_w, ffn_conv_b, ffn_w_down, final_gain):
    cst, rope = constants()
    xx = np.concatenate([ctx[0], x[0]], 0)
    xT = xx.T.reshape(KD, P, T).transpose(1, 0, 2)
    cT = np.stack([c[0], c_ctx], 0).reshape(2, KD, P).transpose(2, 1, 0).reshape(P, 16)
    gains = np.stack([np.concatenate([g, g]) for g in [attn_q_gain[0]] * 8 + [attn_k_gain[0]] * 2], 1)
    conv = np.concatenate([ffn_conv_w, ffn_conv_b[:, None]], 1)
    conv = conv.reshape(2, 4, 2, FJ, P).transpose(4, 0, 3, 2, 1).reshape(P, -1)
    vecs = np.concatenate([feat(ada_b), gains, feat(rwkv_mu[0]), feat(rwkv_decay_w0[0]), feat(rwkv_aaa_a0[0]),
                           feat(rwkv_k_k[0]), feat(rwkv_k_a[0]), feat(rwkv_r_k[0]), feat(rwkv_gn_w[0]),
                           feat(rwkv_gn_b[0]), feat(final_gain), conv], 1)
    adaw = ada_w.reshape(2, KD, P, 12, 512).transpose(0, 3, 2, 1, 4).reshape(24, P, KD * 512)
    wqk = tiles(attn_w_qkv[0][:, :Q_COLS])
    wv = attn_w_qkv[0][:, Q_COLS:].reshape(KD, P, HKV * DH).transpose(1, 0, 2).reshape(P, -1)
    wup = np.stack([tiles(w).reshape(2, 2, FH, P, D).transpose(1, 2, 0, 3, 4).reshape(2, 2 * FH, P, D) for w in ffn_w_up])
    wdn = np.stack([np.stack([tiles(w[h * FH * P:(h + 1) * FH * P]) for h in range(2)]) for w in ffn_w_down])
    lora1 = np.stack([tiles(np.concatenate(list(w[0]), 1))[0] for w in (rwkv_decay_w1, rwkv_aaa_a1)])
    g1 = tiles(np.pad(rwkv_gate_g1[0], ((0, 0), (0, 96))))
    g2 = tiles(np.pad(rwkv_gate_g2[0], ((0, 96), (0, 0))))
    lora2 = np.zeros((KD, P, 4, P), np.float32)
    for n, w in enumerate((rwkv_decay_w2[0], rwkv_aaa_a2[0])):
        for d in range(2):
            lora2[:, 64 * d:64 * d + 64, 2 * n + d] = w[d].reshape(64, KD, P).transpose(1, 0, 2)
    return [xT, cT, vecs, cst, rope, adaw, wqk, wv, tiles(attn_w_o[0]), wup, wdn, lora1, g1,
            tiles(rwkv_w_k[0]), tiles(rwkv_w_v[0]), tiles(rwkv_w_r[0]), tiles(rwkv_w_o[0]),
            lora2.reshape(KD, P, 4 * P), g2]


Q_COLS = H * DH + HKV * DH


def kernel(**inputs):
    import numpy as _np
    import concourse.bacc as _bacc
    from concourse import mybir as _mybir
    from concourse.bass_utils import run_bass_kernel_spmd as _run

    nc = _bacc.Bacc("TRN2", target_bir_lowering=False, num_devices=1)
    arrays, args = {}, []
    for n, a in enumerate(layout(**{k: _np.asarray(v) for k, v in inputs.items()})):
        a = _np.ascontiguousarray(a)
        arrays[f"in_{n}_dram"] = a
        args.append(nc.dram_tensor(f"in_{n}_dram", a.shape, _mybir.dt.from_np(a.dtype), kind="ExternalInput").ap())
    args.append(nc.dram_tensor("out_dram", (P, KD, TL), F32, kind="ExternalOutput").ap())
    program(nc, *args)
    r = _run(nc, [arrays], core_ids=[0])
    y = r.results[0]["out_dram"]
    return _np.ascontiguousarray(y.transpose(2, 1, 0).reshape(1, TL, D))
```
